# Optimizing a Trainium2 kernel written in Bass

```python
import jax
import jax.numpy as jnp
from jax import lax
import numpy as np

D_MODEL = 1024
BATCH = 1
SEQ = 128
DEPTH = 2
DEC_BATCH = 1
DEC_SEQ = 512
PAST_LEN = 128

GRID_W = 64
HEAD_DIM = 64
N_GROUPS = 4
GROUP_WIDTH = D_MODEL // N_GROUPS
N_HEADS = GROUP_WIDTH // HEAD_DIM
D_FF = ((8 * D_MODEL // 3 + 255) // 256) * 256
N_MOD = 9
GLA_RANK = 16
GLA_TAU = 16.0
CHUNK = 64
Q_BLOCK = 128
NA_KH = 8
NA_KW = 16
NA_QC = 16
NA_KCB = NA_QC + NA_KW
ROPE_BASE = 10000.0
EPS = 1e-6
SPLIT_SIZES = (GROUP_WIDTH,) * 4 + (2 * GLA_RANK,) + (GROUP_WIDTH,) * 3 + (GROUP_WIDTH,) * 4 + (2 * N_HEADS, 2 * N_HEADS) + (GROUP_WIDTH,) * 4
N_IN = sum(SPLIT_SIZES)
SPLIT_POINTS = tuple(int(s) for s in np.cumsum(SPLIT_SIZES)[:-1])

kernel_name = 'hybrid_diffusion_step'

def rmsnorm(x, w):
    xf = x.astype(jnp.float32)
    y = xf * lax.rsqrt(jnp.mean(xf * xf, axis=-1, keepdims=True) + EPS)
    return (y * w.astype(jnp.float32)).astype(x.dtype)

def modulate(h, shift, scale):
    return h * (1 + scale[:, None]) + shift[:, None]

def swiglu(h, w1, w3, w2):
    return (jax.nn.silu(h @ w1) * (h @ w3)) @ w2

def heads(t):
    B, T, _ = t.shape
    return t.reshape(B, T, -1, HEAD_DIM).transpose(0, 2, 1, 3)

def merge_heads(t):
    B, H, T, d = t.shape
    return t.transpose(0, 2, 1, 3).reshape(B, T, H * d)

def to_chunks(t):
    B, H, T = t.shape[:3]
    return jnp.moveaxis(t.reshape(B, H, T // CHUNK, CHUNK, *t.shape[3:]), 2, 0)

def from_chunks(t):
    t = jnp.moveaxis(t, 0, 2)
    return t.reshape(t.shape[0], t.shape[1], -1, *t.shape[4:])

def axial_rope(x, pos_r, pos_c):
    half = HEAD_DIM // 2
    quarter = half // 2
    inv = ROPE_BASE ** (-jnp.arange(quarter, dtype=jnp.float32) / quarter)

    def rot(xp, pos):
        ang = pos[:, None] * inv
        cos, sin = jnp.cos(ang), jnp.sin(ang)
        x1, x2 = xp[..., :quarter], xp[..., quarter:]
        return jnp.concatenate([x1 * cos - x2 * sin, x1 * sin + x2 * cos], axis=-1)

    return jnp.concatenate([rot(x[..., :half], pos_r), rot(x[..., half:], pos_c)], axis=-1)

def gla_scan(seqs, state):
    causal = jnp.tril(jnp.ones((CHUNK, CHUNK), bool))

    def step(S, xs):
        qc, kc, vc, ac = xs
        b = jnp.cumsum(ac, axis=2)
        diff = jnp.where(causal[:, :, None], b[:, :, :, None, :] - b[:, :, None, :, :], -jnp.inf)
        att = jnp.einsum('bhid,bhjd,bhijd->bhij', qc, kc, jnp.exp(diff))
        o = att @ vc + jnp.einsum('bhid,bhde->bhie', qc * jnp.exp(b), S)
        b_last = b[:, :, -1:, :]
        S = jnp.exp(b_last[:, :, 0, :, None]) * S + jnp.einsum('bhjd,bhje->bhde', kc * jnp.exp(b_last - b), vc)
        return S, o

    S, o = lax.scan(step, state[0], tuple(to_chunks(t) for t in seqs))
    return from_chunks(o), (S,)

def retention_scan(seqs, state, log_g):
    q, k, v = seqs
    idx = jnp.arange(CHUNK, dtype=jnp.float32)
    diff = idx[:, None] - idx[None, :]
    decay = jnp.where(diff >= 0, jnp.exp(jnp.maximum(diff, 0.0) * log_g[:, None, None]), 0.0)
    q_decay = jnp.exp((idx + 1.0) * log_g[:, None])
    k_decay = jnp.exp((CHUNK - 1.0 - idx) * log_g[:, None])
    chunk_decay = jnp.exp(CHUNK * log_g)

    def step(S, xs):
        qc, kc, vc = xs
        att = jnp.einsum('bhid,bhjd->bhij', qc, kc) * decay
        o = att @ vc + jnp.einsum('bhid,bhde->bhie', qc * q_decay[..., None], S)
        S = chunk_decay[:, None, None] * S + jnp.einsum('bhjd,bhje->bhde', kc * k_decay[..., None], vc)
        return S, o

    S, o = lax.scan(step, state[0], (to_chunks(q), to_chunks(k), to_chunks(v)))
    return from_chunks(o), (S,)

def mlstm_scan(seqs, state):
    causal = jnp.tril(jnp.ones((CHUNK, CHUNK), bool))

    def step(carry, xs):
        C, n, m = carry
        qc, kc, vc, ic, fc = xs
        F = jnp.cumsum(fc, axis=-1)
        logw = jnp.where(causal, F[..., :, None] - F[..., None, :] + ic[..., None, :], -jnp.inf)
        log_inter = F + m[..., None]
        m_i = jnp.maximum(log_inter, jnp.max(logw, axis=-1))
        w = jnp.exp(logw - m_i[..., None])
        w_inter = jnp.exp(log_inter - m_i)
        s = jnp.einsum('bhid,bhjd->bhij', qc, kc) * w
        num = s @ vc + w_inter[..., None] * jnp.einsum('bhid,bhde->bhie', qc, C)
        den = jnp.sum(s, axis=-1) + w_inter * jnp.einsum('bhid,bhd->bhi', qc, n)
        hc = num / jnp.maximum(jnp.abs(den), jnp.exp(-m_i))[..., None]
        m_new = m_i[..., -1]
        w_prev = jnp.exp(F[..., -1] + m - m_new)
        kw = kc * jnp.exp(F[..., -1:] - F + ic - m_new[..., None])[..., None]
        C = w_prev[..., None, None] * C + jnp.einsum('bhjd,bhje->bhde', kw, vc)
        n = w_prev[..., None] * n + jnp.sum(kw, axis=2)
        return (C, n, m_new), hc

    carry, o = lax.scan(step, state, tuple(to_chunks(t) for t in seqs))
    return from_chunks(o), carry

def bidir(run, seqs_f, seqs_b, st_f, st_b):
    o_f, s_f = run(0, seqs_f, st_f)
    o_b, s_b = run(1, tuple(jnp.flip(t, axis=2) for t in seqs_b), st_b)
    return o_f + jnp.flip(o_b, axis=2), s_f, s_b

def dense_attend(q, k, v):
    B, H, T, hd = q.shape
    qb = jnp.moveaxis(q.reshape(B, H, T // Q_BLOCK, Q_BLOCK, hd), 2, 0)

    def blk(qi):
        s = jnp.einsum('bhqd,bhkd->bhqk', qi, k).astype(jnp.float32)
        return jnp.einsum('bhqk,bhkd->bhqd', jax.nn.softmax(s, axis=-1).astype(v.dtype), v)

    o = lax.map(blk, qb)
    return jnp.moveaxis(o, 0, 2).reshape(B, H, T, hd)

def na_latent(q, k, v, k_ctx, v_ctx, rpb):
    B, H, T, hd = q.shape
    rows = T // GRID_W
    kh = min(NA_KH, rows)
    ncb = GRID_W // NA_QC
    r = np.arange(rows)
    krow = np.clip(r - kh // 2, 0, rows - kh)[:, None] + np.arange(kh)
    c0 = np.arange(ncb) * NA_QC
    kcol = np.clip(c0 - NA_KW // 2, 0, GRID_W - NA_KCB)[:, None] + np.arange(NA_KCB)
    qcol = c0[:, None] + np.arange(NA_QC)
    cs = np.clip(qcol - NA_KW // 2, 0, GRID_W - NA_KW)
    inwin = (kcol[:, None, :] >= cs[:, :, None]) & (kcol[:, None, :] < cs[:, :, None] + NA_KW)
    drow = krow - r[:, None] + NA_KH - 1
    dcol = np.clip(kcol[:, None, :] - qcol[:, :, None], -(NA_KW - 1), NA_KW - 1) + NA_KW - 1
    bias = rpb[:, drow[:, None, None, :, None], dcol[None, :, :, None, :]]

    qg = q.reshape(B, H, rows, ncb, NA_QC, hd)
    kb = jnp.take(k.reshape(B, H, rows, GRID_W, hd)[:, :, krow], kcol, axis=4)
    vb = jnp.take(v.reshape(B, H, rows, GRID_W, hd)[:, :, krow], kcol, axis=4)
    s_loc = jnp.einsum('bhrnqd,bhrkncd->bhrnqkc', qg, kb).astype(jnp.float32) + bias[None].astype(jnp.float32)
    s_loc = jnp.where(inwin[:, :, None, :], s_loc, -jnp.inf)
    s_ctx = jnp.einsum('bhrnqd,bhsd->bhrnqs', qg, k_ctx).astype(jnp.float32)
    n_loc = kh * NA_KCB
    s = jnp.concatenate([s_loc.reshape(*s_loc.shape[:5], n_loc), s_ctx], axis=-1)
    pr = jax.nn.softmax(s, axis=-1).astype(v.dtype)
    p_loc = pr[..., :n_loc].reshape(s_loc.shape)
    p_ctx = pr[..., n_loc:]
    o = jnp.einsum('bhrnqkc,bhrkncd->bhrnqd', p_loc, vb) + jnp.einsum('bhrnqs,bhsd->bhrnqd', p_ctx, v_ctx)
    return o.reshape(B, H, T, hd)

def token_mixing(h, p, l, ctx):
    f32 = jnp.float32
    B, T, _ = h.shape
    scale = HEAD_DIM ** -0.5
    u = h @ p['w_in'][l]
    (gq, gk, gv, gg, ga, nq, nk, nv, mq, mk, mv, mo, mi, mf, rq, rk, rv, rg) = jnp.split(u, SPLIT_POINTS, axis=-1)
    latent = ctx is not None
    if latent:
        def cached(name, d):
            return ctx[name][:, d].astype(f32)
        gla_st = [(cached('gla', d),) for d in (0, 1)]
        ml_st = [(cached('mC', d), cached('mn', d), cached('mm', d)) for d in (0, 1)]
        ret_st = [(cached('ret', d),) for d in (0, 1)]
    else:
        zS = jnp.zeros((B, N_HEADS, HEAD_DIM, HEAD_DIM), f32)
        zn = jnp.zeros((B, N_HEADS, HEAD_DIM), f32)
        zm = jnp.zeros((B, N_HEADS), f32)
        gla_st = [(zS,), (zS,)]
        ml_st = [(zS, zn, zm), (zS, zn, zm)]
        ret_st = [(zS,), (zS,)]

    qa = heads(gq).astype(f32) * scale
    ka = heads(gk).astype(f32)
    va = heads(gv).astype(f32)
    a_pre = jnp.einsum('btzr,zrk->zbtk', ga.reshape(B, T, 2, GLA_RANK).astype(f32), p['gla_w_a2'][l].astype(f32)) + p['gla_b_a'][l].astype(f32)[:, None, None, :]
    log_a = jax.nn.log_sigmoid(a_pre) / GLA_TAU
    oa, ga_f, ga_b = bidir(lambda d, s, st: gla_scan(s, st), (qa, ka, va, heads(log_a[0])), (qa, ka, va, heads(log_a[1])), gla_st[0], gla_st[1])
    out_a = merge_heads(rmsnorm(oa, p['gla_norm_w'][l])) * jax.nn.silu(gg.astype(f32))

    qn = heads(nq) * scale
    kn = heads(nk)
    vn = heads(nv)
    if latent:
        on = na_latent(qn, kn, vn, ctx['na_k'].astype(h.dtype), ctx['na_v'].astype(h.dtype), p['na_rpb'][l])
    else:
        on = dense_attend(qn, kn, vn)
    out_b = merge_heads(on).astype(f32)

    qm = heads(mq).astype(f32) * scale
    km = heads(mk).astype(f32)
    vm = heads(mv).astype(f32)
    ig = (mi.reshape(B, T, 2, N_HEADS).astype(f32) + p['mlstm_b_i'][l].astype(f32)).transpose(2, 0, 3, 1)
    lf = jax.nn.log_sigmoid(mf.reshape(B, T, 2, N_HEADS).astype(f32) + p['mlstm_b_f'][l].astype(f32)).transpose(2, 0, 3, 1)
    om, m_f, m_b = bidir(lambda d, s, st: mlstm_scan(s, st), (qm, km, vm, ig[0], lf[0]), (qm, km, vm, ig[1], lf[1]), ml_st[0], ml_st[1])
    out_c = merge_heads(om) * jax.nn.sigmoid(mo.astype(f32))

    qr = heads(rq).astype(f32)
    kr = heads(rk).astype(f32)
    if latent:
        t = jnp.arange(T)
        pos_r = (t // GRID_W).astype(f32)
        pos_c = (t % GRID_W).astype(f32)
        qr = axial_rope(qr, pos_r, pos_c)
        kr = axial_rope(kr, pos_r, pos_c)
    qr = qr * scale
    vr = heads(rv).astype(f32)
    log_g = jax.nn.log_sigmoid(p['ret_decay'][l].astype(f32))
    orr, r_f, r_b = bidir(lambda d, s, st: retention_scan(s, st, log_g[d]), (qr, kr, vr), (qr, kr, vr), ret_st[0], ret_st[1])
    mu = jnp.mean(orr, axis=-1, keepdims=True)
    var = jnp.mean(jnp.square(orr - mu), axis=-1, keepdims=True)
    orr = (orr - mu) * lax.rsqrt(var + EPS) * p['ret_norm_w'][l].astype(f32)
    out_d = merge_heads(orr) * jax.nn.silu(rg.astype(f32))

    y = jnp.concatenate([out_a, out_b, out_c, out_d], axis=-1).astype(h.dtype) @ p['w_out'][l]
    if latent:
        return y, None
    new = {
        'na_k': kn, 'na_v': vn,
        'gla': jnp.stack([ga_f[0], ga_b[0]], axis=1),
        'mC': jnp.stack([m_f[0], m_b[0]], axis=1),
        'mn': jnp.stack([m_f[1], m_b[1]], axis=1),
        'mm': jnp.stack([m_f[2], m_b[2]], axis=1),
        'ret': jnp.stack([r_f[0], r_b[0]], axis=1),
    }
    return y, new

def layer(x, p, l, mod, ctx):
    g = p['norm_w'][l]
    mod = mod.astype(x.dtype)

    def half_ffn(x, j, s):
        h = modulate(rmsnorm(x, g[2 * s]), mod[:, 3 * s], mod[:, 3 * s + 1])
        y = swiglu(h, p['ffn_w1'][l, j], p['ffn_w3'][l, j], p['ffn_w2'][l, j])
        return x + 0.5 * mod[:, 3 * s + 2][:, None] * rmsnorm(y, g[2 * s + 1])

    x = half_ffn(x, 0, 0)
    h = modulate(rmsnorm(x, g[2]), mod[:, 3], mod[:, 4])
    y, new = token_mixing(h, p, l, ctx)
    x = x + mod[:, 5][:, None] * rmsnorm(y, g[3])
    x = half_ffn(x, 1, 2)
    return x, new

def setup_inputs(seed: int = 0) -> dict:
    key = jax.random.key(seed)
    ks = jax.random.split(key, 28)
    f32 = jnp.float32
    H, HD, GW, D = N_HEADS, HEAD_DIM, GROUP_WIDTH, D_MODEL

    def nrm(k, shape, s):
        return jax.random.normal(k, shape, f32) * s

    gamma = 1.0 - 2.0 ** (-5.0 - np.arange(N_HEADS))
    ret_logit = jnp.asarray(np.log(gamma / (1.0 - gamma)), f32)
    return {
        'x_prompt': nrm(ks[0], (BATCH, SEQ, D), 1.0),
        'x_sample': nrm(ks[1], (DEC_BATCH, DEC_SEQ, D), 1.0),
        'cache_na_k': nrm(ks[2], (DEC_BATCH, DEPTH, H, PAST_LEN, HD), 1.0),
        'cache_na_v': nrm(ks[3], (DEC_BATCH, DEPTH, H, PAST_LEN, HD), 1.0),
        'state_gla': nrm(ks[4], (DEC_BATCH, DEPTH, 2, H, HD, HD), 0.5),
        'state_mlstm_C': nrm(ks[5], (DEC_BATCH, DEPTH, 2, H, HD, HD), 0.5),
        'state_mlstm_n': nrm(ks[6], (DEC_BATCH, DEPTH, 2, H, HD), 0.5),
        'state_mlstm_m': nrm(ks[7], (DEC_BATCH, DEPTH, 2, H), 1.0),
        'state_ret': nrm(ks[8], (DEC_BATCH, DEPTH, 2, H, HD, HD), 0.5),
        'c': nrm(ks[9], (DEC_BATCH, D), 1.0),
        'c_ctx': nrm(ks[10], (D,), 1.0),
        'w_mod': nrm(ks[11], (DEPTH, D, N_MOD * D), 0.5 * D ** -0.5),
        'b_mod': nrm(ks[12], (DEPTH, N_MOD * D), 0.02),
        'norm_w': 1.0 + nrm(ks[13], (DEPTH, 6, D), 0.02),
        'ffn_w1': nrm(ks[14], (DEPTH, 2, D, D_FF), D ** -0.5),
        'ffn_w3': nrm(ks[15], (DEPTH, 2, D, D_FF), D ** -0.5),
        'ffn_w2': nrm(ks[16], (DEPTH, 2, D_FF, D), D_FF ** -0.5),
        'w_in': nrm(ks[17], (DEPTH, D, N_IN), D ** -0.5),
        'w_out': nrm(ks[18], (DEPTH, D, D), D ** -0.5),
        'gla_w_a2': nrm(ks[19], (DEPTH, 2, GLA_RANK, GW), GLA_RANK ** -0.5),
        'gla_b_a': nrm(ks[20], (DEPTH, 2, GW), 0.1),
        'gla_norm_w': 1.0 + nrm(ks[21], (DEPTH, HD), 0.02),
        'na_rpb': nrm(ks[22], (DEPTH, H, 2 * NA_KH - 1, 2 * NA_KW - 1), 0.1),
        'mlstm_b_i': nrm(ks[23], (DEPTH, 2, H), 0.1),
        'mlstm_b_f': jnp.linspace(3.0, 6.0, H, dtype=f32) + nrm(ks[24], (DEPTH, 2, H), 0.1),
        'ret_decay': ret_logit + nrm(ks[25], (DEPTH, 2, H), 0.05),
        'ret_norm_w': 1.0 + nrm(ks[26], (DEPTH, HD), 0.02),
    }

def reference(x_prompt, x_sample, cache_na_k, cache_na_v, state_gla, state_mlstm_C, state_mlstm_n, state_mlstm_m, state_ret, c, c_ctx, w_mod, b_mod, norm_w, ffn_w1, ffn_w3, ffn_w2, w_in, w_out, gla_w_a2, gla_b_a, gla_norm_w, na_rpb, mlstm_b_i, mlstm_b_f, ret_decay, ret_norm_w):
    p = {
        'norm_w': norm_w, 'ffn_w1': ffn_w1, 'ffn_w3': ffn_w3, 'ffn_w2': ffn_w2,
        'w_in': w_in, 'w_out': w_out, 'gla_w_a2': gla_w_a2, 'gla_b_a': gla_b_a,
        'gla_norm_w': gla_norm_w, 'na_rpb': na_rpb, 'mlstm_b_i': mlstm_b_i,
        'mlstm_b_f': mlstm_b_f, 'ret_decay': ret_decay, 'ret_norm_w': ret_norm_w,
    }

    def modulation(cvec, l):
        m = jax.nn.silu(cvec) @ w_mod[l] + b_mod[l]
        return m.reshape(cvec.shape[0], N_MOD, D_MODEL)

    xp = x_prompt
    states = []
    for l in range(DEPTH):
        xp, st = layer(xp, p, l, modulation(c_ctx[None], l), None)
        states.append(st)
    new_na_k = jnp.stack([s['na_k'] for s in states], axis=1)
    new_na_v = jnp.stack([s['na_v'] for s in states], axis=1)
    new_gla = jnp.stack([s['gla'] for s in states], axis=1)
    new_mC = jnp.stack([s['mC'] for s in states], axis=1)
    new_mn = jnp.stack([s['mn'] for s in states], axis=1)
    new_mm = jnp.stack([s['mm'] for s in states], axis=1)
    new_ret = jnp.stack([s['ret'] for s in states], axis=1)

    xs = x_sample
    for l in range(DEPTH):
        ctx = {
            'na_k': cache_na_k[:, l], 'na_v': cache_na_v[:, l], 'gla': state_gla[:, l],
            'mC': state_mlstm_C[:, l], 'mn': state_mlstm_n[:, l], 'mm': state_mlstm_m[:, l],
            'ret': state_ret[:, l],
        }
        xs, _ = layer(xs, p, l, modulation(c, l), ctx)

    return (xp, xs, new_na_k, new_na_v, new_gla, new_mC, new_mn, new_mm, new_ret)


_drawn_inputs = setup_inputs


def setup_inputs(seed=0):
    import zlib

    import numpy as np

    out = dict(_drawn_inputs(seed))
    spreads = {}
    factors = {'cache_na_k': 2.675,
     'state_gla': 8.0,
     'state_mlstm_C': 5.916,
     'state_mlstm_n': 3.862,
     'state_mlstm_m': 6.014,
     'state_ret': 8.0,
     'gla_norm_w': 8.0,
     'na_rpb': 8.0,
     'ret_norm_w': 8.0}
    for name, (base, spread) in spreads.items():
        noise = np.random.default_rng([zlib.crc32(name.encode()), seed]).standard_normal(out[name].shape)
        drawn = base * np.exp(spread * noise) if base else spread * noise
        out[name] = jnp.asarray(drawn.astype(out[name].dtype))
    for name, factor in factors.items():
        out[name] = (out[name] * factor).astype(out[name].dtype)
    return out
```

```python
import concourse.bass as bass
from concourse import mybir
from contextlib import ExitStack

FP = mybir.dt.float32
ALU = mybir.AluOpType
ACT = mybir.ActivationFunctionType
AXX = mybir.AxisListType.X

P = 128
DM = 1024
KT = DM // P
SEQ, DEC = 128, 512
NTOK = SEQ + DEC
NT = NTOK // P
HALF = NTOK // 2
DEPTH = 2
FF = 2816
FT = FF // P
HD = 64
NH = 4
GW = NH * HD
EPS = 1e-6
BANK = 512
SLOTS = 4
SLOT_W = FT * P
QSCALE = HD ** -0.5
TAU = 16.0
NEG = -1e30
ROWS, GRID_W, WIN = DEC // 64, 64, 16
SW = 2 * (HD + 1)

MOD_U = 3 * KT // 2
FFN_U = FT + KT
U_MOD = (0, MOD_U + FFN_U, 2 * MOD_U + FFN_U + 20)
U_UP = (MOD_U, 0, U_MOD[2] + MOD_U)
U_GATES = U_MOD[1] + MOD_U
U_C = U_GATES + 1
U_A = U_C + 4
U_D = U_A + 4
U_B = U_D + 4
U_OUT = U_B + 3
U_ALL = U_UP[2] + FFN_U
assert U_OUT + 4 == U_MOD[2] and U_ALL == 116

CONSTS = {}
_at = 0
for _name, _w in (("ident", P), ("ones", P), ("rope", NT * 2 * HD), ("namask", HD), ("causal", 2 * P),
                  ("anti", 2 * P), ("block", P), ("blockn", SW), ("diff", 2 * P), ("posrow", 2 * P),
                  ("poscol", 2), ("carry", NTOK)):
    CONSTS[_name] = (_at, _w)
    _at += _w
CONST_W = _at

PARAMS = {}
_at = 0
for _name, _w in (("bmod", 9 * KT), ("normw", 6 * KT), ("ba", 4), ("gb", 2), ("m0", 1), ("rd", 12),
                  ("gnw", HD), ("rnw", HD), ("kc", 2 * P), ("vc", GW)):
    PARAMS[_name] = (_at, _w)
    _at += _w
PARAM_W = _at


def build(nc, I, O):
    ctx = ExitStack()
    with ctx:
        def sb(name, words):
            return ctx.enter_context(nc.sbuf_tensor(name, [P, words], FP))

        sems = []

        def sem(name):
            s = ctx.enter_context(nc.semaphore(name))
            sems.append(s)
            return s

        xT = sb("xT", KT * NTOK)[:, :].rearrange("p (k n) -> p k n", k=KT)
        hT = sb("hT", KT * NTOK)[:, :].rearrange("p (k n) -> p k n", k=KT)
        ring = sb("ring", SLOTS * SLOT_W)
        const = sb("const", CONST_W)
        par = sb("par", PARAM_W)
        modS = sb("modS", 3 * KT * 2)[:, :].rearrange("p (m c) -> p m c", c=2)
        gs = sb("gs", KT * 2)[:, :].rearrange("p (m c) -> p m c", c=2)
        gg = sb("gg", KT * 2)[:, :].rearrange("p (m c) -> p m c", c=2)
        cond = sb("cond", KT * 2)[:, :].rearrange("p (m c) -> p m c", c=2)
        rstd = sb("rstd", NTOK)
        small = sb("small", 256)
        MIX_W = 5120 + 2560 + 5140 + 1280
        RPB_W = NH * 14 * HD
        TMP_W = 9136
        arena = sb("arena", MIX_W + RPB_W + TMP_W)
        ps = ctx.enter_context(nc.psum_tensor("ps", [P, 8 * BANK], FP))

        def C(name, parts=P):
            a, w = CONSTS[name]
            return const[0:parts, a:a + w]

        def W(name, parts=P):
            a, w = PARAMS[name]
            return par[0:parts, a:a + w]

        def area(a, w):
            return arena[:, a:a + w]

        def tiles(ap, n):
            return ap.rearrange("p (t n) -> p t n", t=n)

        aT = tiles(area(0, FT * NTOK), FT)
        yT = tiles(area(FT * NTOK, KT * NTOK), KT)
        catT = tiles(area(0, 5120), KT)
        FM = tiles(area(5120, 2560), 4)
        TM0 = 7680
        OT = tiles(area(12820, 1280), NT)
        rpb = area(MIX_W, RPB_W)
        T0 = MIX_W + RPB_W
        OTh = area(12820, 1280).rearrange("p (a e) -> p a e", e=HD)
        Tst = area(T0, 1300).rearrange("p (t f w) -> p t f w", t=NT, f=2)
        Sin = area(T0 + 1300, 1300).rearrange("p (t f w) -> p t f w", t=NT, f=2)
        Asb = [area(T0 + 2600 + 512 * i, 512).rearrange("p (a f i) -> p a f i", a=2, f=2) for i in (0, 1)]
        GX = area(T0 + 3624, NTOK)
        GY = area(T0 + 4264, NTOK)
        GM = area(T0 + 4904, NTOK)
        GF = area(T0 + 5544, NTOK)
        GK = area(T0 + 6184, NTOK)
        CT = area(T0 + 4904, 1300).rearrange("p (t h w) -> p t h w", t=NT, h=NH)
        GT = area(T0 + 6824, 1280).rearrange("p (t a r) -> p t a r", t=NT, a=4)
        WL = [area(T0 + 8104 + 512 * i, 512).rearrange("p (a f i) -> p a f i", a=2, f=2) for i in (0, 1)]
        Vc = area(TM0, 1300).rearrange("p (t h w) -> p t h w", t=NT, h=NH)
        Oc = area(TM0 + 1300, 1280)
        kTok = area(TM0 + 2580, 1280)
        ktC = area(TM0 + 3860, 1280)
        Wk = area(T0 + 4264, 1280)
        Bk = area(TM0 + 2560, 1280)
        QM = tiles(area(T0 + 6824, 1280), 2)
        KM = tiles(area(T0 + 5544, 1280), 2)
        wa2 = area(TM0 + 3840, 4 * P)
        Va = area(TM0, 1280)
        Ga = area(TM0 + 1280, 1280)
        RQK = tiles(area(TM0, 2560), NT)
        rot1 = tiles(area(T0 + 3624, 2560), NT)
        rot2 = tiles(area(T0 + 6184, 2560), NT)
        Vd = area(TM0 + 2560, 1280)
        Gd = area(TM0 + 3840, 1280)
        ktD = area(T0 + 5544, 1280)
        Dm = area(T0 + 8104, 1024).rearrange("p (z a f i) -> p z a f i", z=2, a=2, f=2)
        qdec = area(T0 + 4264, 512).rearrange("p (z f i) -> p z f i", z=2, f=2)
        SB = [area(T0 + NTOK * i, NTOK) for i in (0, 1)]
        PT = area(T0 + 1280, NTOK)

        ident, ones = C("ident"), C("ones")
        causal = C("causal").rearrange("p (z i) -> p z i", z=2)
        anti = C("anti").rearrange("p (z i) -> p z i", z=2)

        def pool_sem(name):
            return ctx.enter_context(nc.semaphore(name))

        rpb_loaded = pool_sem("rpb_loaded")
        wa2_loaded = pool_sem("wa2_loaded")
        init_loaded = pool_sem("init_loaded")
        st_out = pool_sem("st_out")
        na_out = pool_sem("na_out")
        m_out = pool_sem("m_out")

        loaded = [sem(f"slot{i}_loaded") for i in range(SLOTS)]
        unit_done = sem("unit_done")
        unit_evac = sem("unit_evac")
        par_loaded = sem("par_loaded")
        mod_ready = sem("mod_ready")
        sq_ready = sem("sq_ready")
        ss_done = sem("ss_done")
        rstd_ready = sem("rstd_ready")
        hmul_ready = sem("hmul_ready")
        h_ready = sem("h_ready")
        silu_done = sem("silu_done")
        x_ready = sem("x_ready")
        gate_pre = sem("gate_pre")
        gate_sp = sem("gate_sp")
        gate_log = sem("gate_log")
        gate_exp = sem("gate_exp")
        gate_t = sem("gate_t")
        gate_cols = sem("gate_cols")
        apre_done = sem("apre_done")
        asp_done = sem("asp_done")
        ad_ready = sem("ad_ready")
        ae_ready = sem("ae_ready")
        aqk_ready = sem("aqk_ready")
        akt_done = sem("akt_done")
        akt_ready = sem("akt_ready")
        lg_ready = sem("lg_ready")
        lg_sp = sem("lg_sp")
        dec_ready = sem("dec_ready")
        rot_ready = sem("rot_ready")
        rt_done = sem("rt_done")
        rt_evac = sem("rt_evac")
        kt_ready = sem("kt_ready")
        u_done = sem("u_done")
        t_done = sem("t_done")
        s_ready = sem("s_ready")
        p_done = sem("p_done")
        wl_done = sem("wl_done")
        w_ready = sem("w_ready")
        a_done = sem("a_done")
        o_done = sem("o_done")
        ot_done = sem("ot_done")
        act_gate = sem("act_gate")
        nrm_in = sem("nrm_in")
        nrm_out = sem("nrm_out")
        fin_ready = sem("fin_ready")
        cat_t = sem("cat_t")
        cat_done = sem("cat_done")
        na_s = sem("na_s")
        na_read = sem("na_read")
        na_max = sem("na_max")
        na_e = sem("na_e")
        na_pt = sem("na_pt")
        na_ptc = sem("na_ptc")
        na_o = sem("na_o")
        na_oc = sem("na_oc")
        start = sem("start_loads")
        cond_ready = sem("cond_ready")
        y_out = sem("y_out")

        UD = lambda n: n + 1 + SLOTS
        EV = lambda n: n + 1 + 2
        slot = lambda n: n % SLOTS
        use = lambda n: 16 * (n // SLOTS + 1)
        half = lambda n: (n % 2) * 4 * BANK
        G_C, G_A, G_D = 0, 1, 2
        R = lambda g, z, t: (g * 2 + z) * NT + t + 1
        Z = lambda g, z: g * 2 + z + 1
        HEADS = [(h // 2, h % 2) for h in range(NH)]
        order = lambda z: (1, 2, 3, 4) if z == 0 else (4, 3, 2, 1)

        def acc(base):
            return ps[:, base:base + 2 * BANK].rearrange("p (a n) -> p a n", a=2)[:, :, 0:HALF]

        def halves(ap):
            return ap.rearrange("p (a n) -> p a n", a=2)

        def slot_ap(n, words):
            return ring[:, slot(n) * SLOT_W:slot(n) * SLOT_W + words]

        with nc.Block() as block:
            @block.sync
            def _(sp):
                sp.dma_start(const[:, :], I["const"]).then_inc(start, 16)
                sp.dma_start(xT, I["x"]).then_inc(start, 16)
                sp.dma_start(cond, I["cond"]).then_inc(start, 16)
                sp.wait_ge(start, 48)

            @block.scalar
            def _(act):
                act.wait_ge(start, 48)
                act.activation(cond, cond, ACT.Silu).then_inc(cond_ready, 1)
                act.wait_ge(cond_ready, 1)

        with nc.Fori(0, DEPTH) as l:
            with nc.Block() as block:
                @block.sync
                def _(sp):
                    sp.dma_start(par[:, :], I["par"][l]).then_inc(par_loaded, 16)

                    def load(n, i4, words, src):
                        sp.wait_ge(unit_done, i4 * 4 + (n + 1))
                        sp.dma_start(slot_ap(n, words), src).then_inc(loaded[slot(n)], 16)

                    def mod_units(s):
                        with sp.Fori(0, MOD_U // 4) as i:
                            for u in range(4):
                                load(U_MOD[s] + u, i, KT * 256, I["w_mod"][l, i * 4 + (s * MOD_U + u)])

                    def ffn_units(s, j):
                        n = U_UP[s]
                        with sp.Fori(0, FT // 4) as i:
                            for u in range(4):
                                load(n + u, i, 2 * DM, I["w13"][l, i * 4 + (j * FT + u)])
                        for f in range(FT // 4 * 4, FT):
                            load(n + f, 0, 2 * DM, I["w13"][l, j * FT + f])
                        n += FT
                        with sp.Fori(0, KT // 4) as i:
                            for u in range(4):
                                load(n + u, i, SLOT_W, I["w2"][l, i * 4 + (j * KT + u)])

                    mod_units(0)
                    ffn_units(0, 0)
                    mod_units(1)
                    load(U_GATES, 0, KT * 160, I["w_gates"][l])
                    for q in range(15):
                        load(U_C + q, 0, KT * 256, I["w_in"][l, q])
                    for q in range(4):
                        load(U_OUT + q, 0, KT * 256, I["w_out"][l, q])
                    mod_units(2)
                    ffn_units(2, 1)

                @block.gpsimd
                def _(pool):
                    pool.wait_ge(h_ready, 2 * KT)
                    pool.dma_start(rpb, I["rpb"][l]).then_inc(rpb_loaded, 16)
                    outs = (O["mc"], O["gla"], O["ret"])
                    for g in (G_C, G_A, G_D):
                        w = SW if g == G_C else P
                        if g == G_A:
                            pool.wait_ge(cat_done, 1)
                            pool.dma_start(wa2[64:96, :], I["wa2"][l]).then_inc(wa2_loaded, 16)
                        for z in range(2):
                            if Z(g, z) > 1:
                                pool.wait_ge(o_done, R(g, z, -1))
                            src = I["st_c"][l, z] if g == G_C else I["st_ad"][l, 0 if g == G_A else 1, z]
                            pool.dma_start(Sin[:, order(z)[0], :, 0:w], src).then_inc(init_loaded, 16)
                            pool.wait_ge(t_done, R(g, z, 0))
                            pool.dma_start(outs[g][l, z], Tst[:, 0, :, 0:w]).then_inc(st_out, 16)
                            if g == G_C and z == 0:
                                pool.wait_ge(gate_log, 1)
                                pool.dma_start(O["mm"][l], small[0:64, 0:1]).then_inc(m_out, 16)
                    pool.wait_ge(unit_evac, EV(U_B + 2))
                    pool.dma_start(O["nak"][l], FM[:, 2:4, 0:P]).then_inc(na_out, 16)
                    pool.dma_start(O["nav"][l], Va[:, 0:GW]).then_inc(na_out, 16)
                    pool.wait_ge(na_out, l * 32 + (32))
                    pool.wait_ge(st_out, l * 96 + (6 * 16))
                    pool.wait_ge(m_out, l * 16 + (16))

                @block.tensor
                def _(pe):
                    mm = pe.matmul
                    pe.sem_inc(unit_done, SLOTS)

                    def claim(n, i4=0):
                        pe.wait_ge(loaded[slot(n)], i4 * 16 + use(n))
                        pe.wait_ge(unit_evac, i4 * 4 + (n + 1))
                        return half(n)

                    def mod(s):
                        with pe.Fori(0, MOD_U // 4) as i:
                            for u in range(4):
                                n = U_MOD[s] + u
                                base = claim(n, i)
                                w = tiles(slot_ap(n, KT * 256), KT)
                                for m in range(2):
                                    for k in range(KT):
                                        last = mm(ps[:, base + 2 * m:base + 2 * m + 2], w[:, k, m * P:(m + 1) * P],
                                                  cond[:, k, :], start=k == 0, stop=k == KT - 1)
                                last.then_inc(unit_done, 1)

                    def sums(v, n):
                        pe.wait_ge(unit_evac, EV(n - 1))
                        sq = yT if v % 2 == 0 else hT
                        for k in range(KT):
                            pe.wait_ge(sq_ready, KT * v + k + 1)
                            for a in range(2):
                                last = mm(ps[:, a * BANK:a * BANK + HALF], ones, sq[:, k, a * HALF:(a + 1) * HALF],
                                          start=k == 0, stop=k == KT - 1)
                        last.then_inc(ss_done, 1)
                        pe.wait_ge(rstd_ready, v + 1)

                    def feature_major(base, w, x, cols=P):
                        for a in range(2):
                            for k in range(len(w)):
                                last = mm(ps[0:cols, base + a * BANK:base + a * BANK + HALF], w[k],
                                          x[:, k, a * HALF:(a + 1) * HALF], start=k == 0, stop=k == len(w) - 1)
                        return last

                    def up(n, i4):
                        base = claim(n, i4)
                        w = slot_ap(n, 2 * DM).rearrange("p (b k c) -> p b k c", b=2, k=KT)
                        for b in range(2):
                            last = feature_major(base + 2 * b * BANK, [w[:, b, k, :] for k in range(KT)], hT)
                        last.then_inc(unit_done, 1)

                    def down(n, i4):
                        base = claim(n, i4)
                        w = tiles(slot_ap(n, SLOT_W), FT)
                        feature_major(base, [w[:, f, :] for f in range(FT)], aT).then_inc(unit_done, 1)

                    def ffn(s):
                        n = U_UP[s]
                        pe.wait_ge(h_ready, KT * (s + 1))
                        with pe.Fori(0, FT // 4) as i:
                            for u in range(4):
                                up(n + u, i)
                        for f in range(FT // 4 * 4, FT):
                            up(n + f, 0)
                        n += FT
                        pe.wait_ge(unit_evac, EV(n - 1))
                        with pe.Fori(0, KT // 4) as i:
                            for u in range(4):
                                down(n + u, i)

                    def features(n, x=hT):
                        base = claim(n)
                        w = tiles(slot_ap(n, KT * 256), KT)
                        for m in range(2):
                            last = feature_major(base + 2 * m * BANK, [w[:, k, m * P:(m + 1) * P] for k in range(KT)], x)
                        last.then_inc(unit_done, 1)

                    def tokens(n):
                        base = claim(n)
                        w = tiles(slot_ap(n, KT * 256), KT)
                        for t in range(NT):
                            for k in range(KT):
                                last = mm(ps[:, base + t * GW:base + (t + 1) * GW], hT[:, k, t * P:(t + 1) * P],
                                          w[:, k, :], start=k == 0, stop=k == KT - 1)
                        last.then_inc(unit_done, 1)

                    def gates():
                        base = claim(U_GATES)
                        w = tiles(slot_ap(U_GATES, KT * 160), KT)
                        feature_major(base, [w[:, k, 0:96] for k in range(KT)], hT, 96)
                        feature_major(base + 2 * BANK, [w[:, k, 96:160] for k in range(KT)], hT, 64)\
                            .then_inc(unit_done, 1)

                    def tr(col, src, rows=P):
                        return pe.transpose(ps[:, col:col + rows], src, ident[0:rows, 0:rows])

                    def scan_group(g, z, k2, q2, qi, kt, v, vw):
                        for t in range(NT):
                            if t >= 2:
                                pe.wait_ge(t_done, R(g, z, t - 2))
                            for f in range(2):
                                c = (t % 2) * BANK + f * 2 * vw
                                last = mm(ps[:, c:c + 2 * vw], kt[:, t, f * P:(f + 1) * P],
                                          v[:, t, 2 * f * vw:2 * (f + 1) * vw], start=True, stop=True)
                            last.then_inc(u_done, 1)

                        def scores(t):
                            if t >= 2:
                                pe.wait_ge(a_done, R(g, z, t - 2))
                            b = (2 + 2 * (t % 2)) * BANK
                            if g == G_C:
                                for f, a in HEADS:
                                    row = z * 32 + 2 * f + a
                                    c = b + a * BANK + GW + f * P
                                    mm(ps[:, c:c + P], ident[:, row:row + 1].to_broadcast([P, P]),
                                       GY[:, t * P:(t + 1) * P], start=True, stop=True)
                            for f, a in HEADS:
                                rows = slice(a * HD, (a + 1) * HD)
                                c = b + a * BANK + f * P
                                last = mm(ps[:, c:c + P], k2[rows, f, t * P:(t + 1) * P],
                                          q2[rows, f, t * P:(t + 1) * P], start=True, stop=True)
                            last.then_inc(p_done, 1)

                        def output(t):
                            pe.wait_ge(a_done, R(g, z, t))
                            if t == 1:
                                pe.wait_ge(s_ready, Z(g, z))
                            if t >= 2:
                                pe.wait_ge(ot_done, R(g, z, t - 2))
                            o = (6 + t % 2) * BANK
                            own = t == 0 or g == G_C
                            for h, (f, a) in enumerate(HEADS):
                                last = mm(ps[:, o + h * vw:o + (h + 1) * vw], Asb[t % 2][:, a, f, :],
                                          v[:, t, h * vw:(h + 1) * vw], start=h == 0, stop=own,
                                          skip_group_check=True)
                            if t:
                                for f in range(2):
                                    c = o + f * P if g != G_C else (t % 2) * BANK + f * SW
                                    s = (Tst if g == G_A else Sin)[:, t, f, 0:2 * vw]
                                    last = mm(ps[:, c:c + 2 * vw], qi[:, f, t * P:(t + 1) * P], s,
                                              start=g == G_C and f == 0, stop=True, skip_group_check=True)
                            last.then_inc(o_done, 1)

                        scores(0)
                        for t in range(NT):
                            if t + 1 < NT:
                                scores(t + 1)
                            output(t)

                    def concat(c):
                        pe.wait_ge(fin_ready, c)
                        for f in range(2):
                            for t in range(NT):
                                last = tr((f * NT + t) * P, OT[:, t, f * P:(f + 1) * P])
                        last.then_inc(cat_t, 1)
                        pe.wait_ge(cat_done, c)

                    mod(0)
                    sums(0, U_UP[0])
                    ffn(0)
                    sums(1, U_UP[0] + FFN_U)
                    mod(1)
                    sums(2, U_GATES)
                    pe.wait_ge(h_ready, KT * 2)
                    gates()

                    features(U_C)
                    features(U_C + 1)
                    tokens(U_C + 2)
                    tokens(U_C + 3)
                    pe.wait_ge(unit_evac, EV(U_C + 3))
                    pe.wait_ge(gate_exp, 1)
                    for t in range(NT):
                        for a, rows in enumerate((GX, GF, GM, GK)):
                            tr((t * 4 + a) * 64, rows[0:64, t * P:(t + 1) * P], 64)
                    for t in range(NT):
                        for f in range(2):
                            tr(4 * BANK + (t * 2 + f) * P, FM[:, 2 + f, t * P:(t + 1) * P])
                    for z in range(2):
                        for f in range(2):
                            c = 7 * BANK + (z * 2 + f) * NT
                            for a in range(2):
                                row = z * 32 + 2 * f + a
                                last = mm(ps[a * HD:(a + 1) * HD, c:c + NT],
                                          ident[0:64, row:row + 1].to_broadcast([64, HD]),
                                          small[0:64, 16:16 + NT], start=True, stop=True)
                    last.then_inc(gate_t, 1)
                    for z in range(2):
                        pe.wait_ge(kt_ready, z + 1)
                        if z:
                            pe.wait_ge(ot_done, R(G_C, 0, NT - 1))
                        scan_group(G_C, z, FM[:, 2:4, :], FM[:, 0:2, :], FM[:, 0:2, :], tiles(ktC, NT),
                                   Vc.rearrange("p t h w -> p t (h w)"), HD + 1)
                    pe.wait_ge(ot_done, R(G_C, 1, NT - 1))
                    concat(1)

                    features(U_A)
                    features(U_A + 1)
                    tokens(U_A + 2)
                    tokens(U_A + 3)
                    pe.wait_ge(unit_evac, EV(U_A + 3))
                    pe.wait_ge(wa2_loaded, l * 16 + (16))
                    for z in range(2):
                        if z:
                            pe.wait_ge(ot_done, R(G_A, 0, NT - 1))
                        for f in range(2):
                            for a in range(2):
                                c = (2 * f + a) * BANK
                                last = mm(ps[:, c:c + HALF], wa2[64:96, (2 * z + f) * P:(2 * z + f + 1) * P],
                                          GX[64:96, a * HALF:(a + 1) * HALF], start=True, stop=True)
                        last.then_inc(apre_done, 1)
                        pe.wait_ge(aqk_ready, z + 1)
                        for t in range(NT):
                            for f in range(2):
                                last = tr((t * 2 + f) * P, KM[:, f, t * P:(t + 1) * P])
                        last.then_inc(akt_done, 1)
                        pe.wait_ge(akt_ready, z + 1)
                        scan_group(G_A, z, KM, QM, QM, tiles(Bk, NT), tiles(Va, NT), HD)
                    pe.wait_ge(ot_done, R(G_A, 1, NT - 1))
                    concat(2)

                    for q in range(4):
                        tokens(U_D + q)
                    pe.wait_ge(unit_evac, EV(U_D + 3))
                    pe.wait_ge(rot_ready, 1)
                    for t in range(NT):
                        if t >= 2:
                            pe.wait_ge(rt_evac, t - 1)
                        for f in range(4):
                            last = tr((t % 2) * BANK + f * P, RQK[:, t, f * P:(f + 1) * P])
                        last.then_inc(rt_done, 1)
                    pe.wait_ge(rt_evac, NT)
                    for z in range(2):
                        pe.wait_ge(kt_ready, 2 + z + 1)
                        if z:
                            pe.wait_ge(ot_done, R(G_D, 0, NT - 1))
                        scan_group(G_D, z, FM[:, 2:4, :], FM[:, 0:2, :], QM, tiles(ktD, NT), tiles(Vd, NT), HD)
                    pe.wait_ge(ot_done, R(G_D, 1, NT - 1))
                    concat(3)

                    features(U_B)
                    features(U_B + 1)
                    tokens(U_B + 2)
                    pe.wait_ge(unit_evac, EV(U_B + 2))
                    kc = tiles(W("kc"), 2)
                    vc = W("vc")
                    vb = tiles(Va, NT)

                    def na_scores(b):
                        t, h = b // NH, b % NH
                        f, a = HEADS[h]
                        if b >= 2:
                            pe.wait_ge(na_read, b - 1)
                        rows = slice(a * HD, (a + 1) * HD)
                        c = a * 2 * BANK
                        q = FM[rows, f, t * P:(t + 1) * P]
                        if t == 0:
                            last = mm(ps[:, c:c + P], q, FM[rows, 2 + f, 0:P], start=True, stop=True)
                        else:
                            mm(ps[:, c:c + DEC], q, FM[rows, 2 + f, P:NTOK], start=True, stop=True)
                            last = mm(ps[:, c + BANK:c + BANK + P], q, kc[rows, f, :], start=True, stop=True)
                        last.then_inc(na_s, 1)

                    def na_values(b):
                        t, h = b // NH, b % NH
                        n = 1 if t == 0 else NT
                        pe.wait_ge(na_e, b + 1)
                        if b:
                            pe.wait_ge(na_ptc, b)
                        for j in range(n):
                            last = tr(4 * BANK + j * P, SB[b % 2][:, j * P:(j + 1) * P])
                        last.then_inc(na_pt, 1)
                        pe.wait_ge(na_ptc, b + 1)
                        if b >= 2:
                            pe.wait_ge(na_oc, b - 1)
                        o = (6 + b % 2) * BANK
                        for j in range(n):
                            v = vb[:, 0, :] if t == 0 else vb[:, 1 + j, :] if j < NT - 1 else vc
                            last = mm(ps[:, o:o + HD], PT[:, j * P:(j + 1) * P], v[:, h * HD:(h + 1) * HD],
                                      start=j == 0, stop=j == n - 1)
                        last.then_inc(na_o, 1)

                    na_scores(0)
                    for b in range(NT * NH):
                        if b + 1 < NT * NH:
                            na_scores(b + 1)
                        na_values(b)
                    pe.wait_ge(na_oc, NT * NH)
                    concat(4)

                    for q in range(4):
                        features(U_OUT + q, catT)
                    sums(3, U_MOD[2])
                    mod(2)
                    sums(4, U_UP[2])
                    ffn(2)
                    sums(5, U_ALL)

                @block.scalar
                def _(act):
                    def fn(out, in_, f, **kw):
                        return act.activation(out, in_, f, **kw)

                    def ln_exp():
                        act.preload_act_table_set("natural_log_exp_and_others")

                    def norm(v, n0, per):
                        for k in range(KT):
                            if v % 2 == 0:
                                if v:
                                    act.wait_ge(x_ready, KT * (v // 2 - 1) + k + 1)
                                last = fn(yT[:, k, :], xT[:, k, :], ACT.Square)
                            else:
                                act.wait_ge(unit_evac, EV(n0 + k // per))
                                last = fn(hT[:, k, :], yT[:, k, :], ACT.Square)
                            last.then_inc(sq_ready, 1)
                        ln_exp()
                        act.wait_ge(ss_done, v + 1)
                        fn(halves(rstd[:, :]), acc(0), ACT.Ln, scale=1.0 / DM, bias=eps)
                        act.drain()
                        fn(rstd[:, :], rstd[:, :], ACT.Exp, scale=-0.5).then_inc(rstd_ready, 1)

                    def modulate(s):
                        act.wait_ge(mod_ready, s + 1)
                        for k in range(KT):
                            act.wait_ge(hmul_ready, KT * s + k + 1)
                            for c, cols in enumerate((slice(0, SEQ), slice(SEQ, NTOK))):
                                last = fn(hT[:, k, cols], hT[:, k, cols], ACT.Identity,
                                          bias=modS[:, k, c:c + 1], scale=gs[:, k, c:c + 1])
                            last.then_inc(h_ready, 1)

                    def ffn(s, j):
                        n = U_UP[s]

                        def one(u, i4, f):
                            act.wait_ge(unit_done, i4 * 4 + UD(n + u))
                            fn(f, acc(half(n + u)), ACT.Silu).then_inc(silu_done, 1)

                        act.preload_act_table_set("silu_and_others")
                        if s:
                            act.wait_ge(na_out, l * 32 + (32))
                        with act.Fori(0, FT // 4) as i:
                            for u in range(4):
                                one(u, i, arena[:, bass.ds(i * (4 * NTOK) + u * NTOK, NTOK)]
                                    .rearrange("p (a n) -> p a n", a=2))
                        for f in range(FT // 4 * 4, FT):
                            one(f, 0, halves(aT[:, f, :]))

                    def three(dst, base):
                        for a in (0, 512, 1024):
                            w = min(512, 1280 - a)
                            last = fn(dst[:, a:a + w], ps[:, base + a:base + a + w], ACT.Copy)
                        return last

                    def softplus(buf, n):
                        act.drain()
                        fn(buf, buf, ACT.Exp, scale=-1.0)
                        act.drain()
                        return fn(buf, buf, ACT.Ln, bias=1.0)

                    def head_rstd(c):
                        ln_exp()
                        act.wait_ge(nrm_in, c)
                        fn(small[:, 64:84], small[:, 64:84], ACT.Ln, scale=1.0 / HD, bias=eps)
                        act.drain()
                        fn(small[:, 64:84], small[:, 64:84], ACT.Exp, scale=-0.5).then_inc(nrm_out, 1)

                    def concat(c, kt):
                        act.wait_ge(cat_t, c)
                        three(catT[:, kt:kt + 2, :].rearrange("p k n -> p (k n)"), 0).then_inc(cat_done, 1)

                    eps = small[:, 255:256]
                    norm(0, 0, 1)
                    modulate(0)
                    ffn(0, 0)
                    norm(1, U_UP[0] + FT, 1)
                    norm(2, 0, 1)
                    modulate(1)

                    ln_exp()
                    act.wait_ge(gate_pre, 1)
                    fn(GK[0:64, :], GY[0:64, :], ACT.Abs)
                    softplus(GK[0:64, :], 64).then_inc(gate_sp, 1)
                    act.wait_ge(gate_log, 1)
                    fn(GF[0:64, :], GF[0:64, :], ACT.Exp)
                    fn(GK[0:64, :], GK[0:64, :], ACT.Exp)
                    fn(small[0:64, 16:21], small[0:64, 16:21], ACT.Exp)
                    fn(GM[0:64, :], GM[0:64, :], ACT.Exp, scale=-1.0).then_inc(gate_exp, 1)
                    act.wait_ge(gate_t, 1)
                    three(area(T0 + 6824, 1280), 0)
                    three(kTok, 4 * BANK)
                    fn(small[:, 24:44], ps[:, 7 * BANK:7 * BANK + 20], ACT.Copy).then_inc(gate_cols, 1)
                    for z in range(2):
                        for t in range(NT):
                            act.wait_ge(wl_done, z * NT + t + 1)
                            fn(WL[t % 2], WL[t % 2], ACT.Exp).then_inc(w_ready, 1)
                    act.wait_ge(unit_evac, EV(U_C + 3))
                    fn(Oc, Oc, ACT.Sigmoid).then_inc(act_gate, 1)
                    concat(1, 4)

                    ln_exp()
                    for z in range(2):
                        act.wait_ge(apre_done, z + 1)
                        for f in range(2):
                            b = W("ba")[:, 2 * z + f:2 * z + f + 1]
                            fn(halves(Wk[:, f * NTOK:(f + 1) * NTOK]), acc(2 * f * BANK), ACT.Abs, bias=b)
                            fn(halves(QM[:, f, :]), acc(2 * f * BANK), ACT.Identity, bias=b)
                        softplus(Wk, P).then_inc(asp_done, 1)
                        act.wait_ge(ad_ready, z + 1)
                        fn(QM.rearrange("p f n -> p (f n)"), Wk, ACT.Exp, scale=1.0 / TAU)
                        fn(KM.rearrange("p f n -> p (f n)"), Wk, ACT.Exp, scale=-1.0 / TAU)
                        fn(small[:, 96:126], small[:, 96:126], ACT.Exp, scale=1.0 / TAU).then_inc(ae_ready, 1)
                        act.wait_ge(akt_done, z + 1)
                        three(Bk, 0).then_inc(akt_ready, 1)
                    act.wait_ge(unit_evac, EV(U_A + 3))
                    head_rstd(1)
                    fn(Ga, Ga, ACT.Silu).then_inc(act_gate, 1)
                    concat(2, 0)

                    ln_exp()
                    act.wait_ge(par_loaded, 16)
                    lg = small[:, 128:140]
                    act.wait_ge(lg_ready, 1)
                    fn(small[:, 144:156], W("rd"), ACT.Abs)
                    softplus(small[:, 144:156], P).then_inc(lg_sp, 1)
                    act.wait_ge(lg_ready, 2)
                    diff = C("diff").rearrange("p (z i) -> p z i", z=2)
                    prow = C("posrow").rearrange("p (z i) -> p z i", z=2)
                    for z in range(2):
                        for h, (f, a) in enumerate(HEADS):
                            fn(Dm[:, z, a, f, :], diff[:, z, :], ACT.Exp, scale=lg[:, 4 * z + h:4 * z + h + 1])
                        for f in range(2):
                            fn(qdec[:, z, f, :], prow[:, z, :], ACT.Exp, scale=lg[:, 8 + 2 * z + f:9 + 2 * z + f])
                    fn(small[:, 160:168], small[:, 160:168], ACT.Exp)
                    fn(small[:, 168:172], lg[:, 8:12], ACT.Exp, scale=float(P)).then_inc(dec_ready, 1)
                    for t in range(NT):
                        act.wait_ge(rt_done, t + 1)
                        b = (t % 2) * BANK
                        fn(FM[:, :, t * P:(t + 1) * P], tiles(ps[:, b:b + BANK], 4), ACT.Copy).then_inc(rt_evac, 1)
                    act.wait_ge(unit_evac, EV(U_D + 3))
                    head_rstd(2)
                    fn(Gd, Gd, ACT.Silu).then_inc(act_gate, 1)
                    concat(3, 6)

                    ln_exp()

                    def probs(b):
                        n = P if b < NH else NTOK
                        act.wait_ge(na_max, b + 1)
                        fn(SB[b % 2][:, 0:n], SB[b % 2][:, 0:n], ACT.Exp, bias=small[:, 176 + b:177 + b],
                           accum_out=small[:, 200 + b:201 + b]).then_inc(na_e, 1)

                    def turned(b):
                        n = P if b < NH else NTOK
                        act.wait_ge(na_pt, b + 1)
                        if b:
                            act.wait_ge(na_o, b)
                        for a in range(0, n, BANK):
                            w = min(BANK, n - a)
                            last = fn(PT[:, a:a + w], ps[:, 4 * BANK + a:4 * BANK + a + w], ACT.Copy)
                        last.then_inc(na_ptc, 1)

                    probs(0)
                    for b in range(NT * NH):
                        if b + 1 < NT * NH:
                            probs(b + 1)
                        turned(b)
                    concat(4, 2)

                    norm(3, U_OUT, 2)
                    norm(4, 0, 1)
                    modulate(2)
                    ffn(2, 1)
                    norm(5, U_UP[2] + FT, 1)

                @block.vector
                def _(dve):
                    V = nc.vector
                    dve.sem_inc(unit_evac, 2)
                    V.memset(small[:, 0:255], 0.0)
                    V.memset(small[:, 255:256], EPS)
                    dve.wait_ge(par_loaded, 16)
                    bmod = W("bmod")
                    normw = tiles(W("normw"), 6)

                    def mod(s):
                        with dve.Fori(0, MOD_U // 4) as i:
                            for u in range(4):
                                n = U_MOD[s] + u
                                dve.wait_ge(unit_done, i * 4 + UD(n))
                                m = i * 8 + 2 * u
                                V.tensor_tensor(modS[:, bass.ds(m, 2), :],
                                                tiles(ps[:, half(n):half(n) + 4], 2),
                                                par[:, bass.ds(m + (PARAMS["bmod"][0] + s * 3 * KT), 2)]
                                                .unsqueeze(2).to_broadcast([P, 2, 2]),
                                                ALU.add).then_inc(unit_evac, 1)
                        dve.drain()
                        g = lambda i: normw[:, i, :].unsqueeze(2).to_broadcast([P, KT, 2])
                        V.scalar_tensor_tensor(gg, modS[:, 2 * KT:3 * KT, :], 1.0 if s == 1 else 0.5, g(2 * s + 1),
                                               ALU.mult, ALU.mult)
                        V.scalar_tensor_tensor(gs, modS[:, KT:2 * KT, :], 1.0, g(2 * s), ALU.add, ALU.mult)\
                            .then_inc(mod_ready, 1)

                    def norm_in(s):
                        dve.wait_ge(rstd_ready, 2 * s + 1)
                        for k in range(KT):
                            V.tensor_tensor(hT[:, k, :], xT[:, k, :], rstd[:, :], ALU.mult).then_inc(hmul_ready, 1)

                    def norm_out(s):
                        dve.wait_ge(rstd_ready, 2 * s + 2)
                        for k in range(KT):
                            V.tensor_tensor(yT[:, k, :], yT[:, k, :], rstd[:, :], ALU.mult)
                        dve.drain()
                        for k in range(KT):
                            for c, cols in enumerate((slice(0, SEQ), slice(SEQ, NTOK))):
                                last = V.scalar_tensor_tensor(xT[:, k, cols], yT[:, k, cols], gg[:, k, c:c + 1],
                                                              xT[:, k, cols], ALU.mult, ALU.add)
                            last.then_inc(x_ready, 1)

                    def ffn(s, j):
                        n = U_UP[s]

                        def one(u, i4, f):
                            dve.wait_ge(silu_done, i4 * 4 + (j * FT + u + 1))
                            V.tensor_tensor(f, f, acc(half(n + u) + 2 * BANK), ALU.mult).then_inc(unit_evac, 1)

                        with dve.Fori(0, FT // 4) as i:
                            for u in range(4):
                                one(u, i, arena[:, bass.ds(i * (4 * NTOK) + u * NTOK, NTOK)]
                                    .rearrange("p (a n) -> p a n", a=2))
                        for f in range(FT // 4 * 4, FT):
                            one(f, 0, halves(aT[:, f, :]))
                        n += FT
                        with dve.Fori(0, KT // 4) as i:
                            for u in range(4):
                                dve.wait_ge(unit_done, i * 4 + UD(n + u))
                                V.tensor_copy(arena[:, bass.ds(i * (4 * NTOK) + (FT + u) * NTOK, NTOK)]
                                              .rearrange("p (a n) -> p a n", a=2),
                                              acc(half(n + u))).then_inc(unit_evac, 1)

                    def evac_features(n, dst, scale=None):
                        dve.wait_ge(unit_done, UD(n))
                        src = ps[:, half(n):half(n) + 4 * BANK].rearrange("p (a n) -> p a n", a=4)[:, :, 0:HALF]
                        dst = dst.rearrange("p k n -> p (k n)").rearrange("p (a n) -> p a n", a=4)
                        if scale is None:
                            last = V.tensor_copy(dst, src)
                        else:
                            last = V.tensor_scalar(dst, src, scale, None, ALU.mult)
                        last.then_inc(unit_evac, 1)

                    def evac_tokens(n, dst, scale=1.0):
                        dve.wait_ge(unit_done, UD(n))
                        src = ps[:, half(n):half(n) + NT * GW]
                        if len(dst.shape) == 4:
                            src = src.rearrange("p (t h e) -> p t h e", t=NT, h=NH)
                        else:
                            src = tiles(src, NT)
                        V.tensor_scalar(dst, src, scale, None, ALU.mult).then_inc(unit_evac, 1)

                    def scan_group(g, z, bmask, decay):
                        w = SW if g == G_C else P
                        if Z(g, z) > 1:
                            dve.wait_ge(st_out, l * 96 + (16 * (Z(g, z) - 1)))
                        for t in range(NT):
                            dve.wait_ge(u_done, R(g, z, t))
                            u = tiles(ps[:, (t % 2) * BANK:(t % 2) * BANK + 2 * w], 2)
                            if g == G_A:
                                for f in range(2):
                                    last = V.scalar_tensor_tensor(Tst[:, t, f, 0:w], u[:, f, :],
                                                                  small[:, 106 + f * NT + t:107 + f * NT + t],
                                                                  bmask, ALU.mult, ALU.mult)
                            else:
                                last = V.tensor_tensor(Tst[:, t, :, 0:w], u,
                                                       bmask.unsqueeze(1).to_broadcast([P, 2, w]), ALU.mult)
                            last.then_inc(t_done, 1)
                        o = order(z)
                        for a, b in zip(o[:-1], o[1:]):
                            dve.drain()
                            if a == o[0]:
                                dve.wait_ge(init_loaded, l * 96 + (16 * Z(g, z)))
                            for f in range(2):
                                last = V.scalar_tensor_tensor(Sin[:, b, f, 0:w], Sin[:, a, f, 0:w], decay(f, a),
                                                              Tst[:, a, f, 0:w], ALU.mult, ALU.add)
                        if g == G_A:
                            dve.drain()
                            for f in range(2):
                                last = V.tensor_tensor(Tst[:, 1:NT, f, 0:w], Sin[:, 1:NT, f, 0:w],
                                                       small[:, 117 + f * NT:121 + f * NT].unsqueeze(2)
                                                       .to_broadcast([P, NT - 1, w]), ALU.mult)
                        last.then_inc(s_ready, 1)

                        def attention(t):
                            dve.wait_ge(p_done, R(g, z, t))
                            b = (2 + 2 * (t % 2)) * BANK
                            both = ps[:, b:b + 2 * BANK].rearrange("p (a q f i) -> p a q f i", a=2, q=2, f=2)
                            pr, lw = both[:, :, 0, :, :], both[:, :, 1, :, :]
                            if t >= 2:
                                dve.wait_ge(o_done, R(g, z, t - 2))
                            elif Z(g, z) > 1:
                                dve.wait_ge(o_done, R(g, z, -1))
                            if g == G_C:
                                for f, a in HEADS:
                                    last = V.scalar_tensor_tensor(
                                        WL[t % 2][:, a, f, :], lw[:, a, f, :],
                                        GT[:, t, 0, z * 32 + 2 * f + a:z * 32 + 2 * f + a + 1],
                                        anti[:, z, :], ALU.add, ALU.add)
                                last.then_inc(wl_done, 1)
                                if t:
                                    output(t - 1)
                                dve.wait_ge(w_ready, z * NT + t + 1)
                                m = WL[t % 2]
                            elif g == G_A:
                                m = causal[:, z, :].unsqueeze(1).unsqueeze(1).to_broadcast([P, 2, 2, P])
                            else:
                                m = Dm[:, z]
                            V.tensor_tensor(Asb[t % 2], pr, m, ALU.mult).then_inc(a_done, 1)

                        def output(t):
                            dve.wait_ge(o_done, R(g, z, t))
                            o = (6 + t % 2) * BANK
                            if g == G_C:
                                out = tiles(ps[:, o:o + 2 * SW], NH)
                                if t == 0:
                                    V.tensor_copy(CT[:, t], out).then_inc(ot_done, 1)
                                else:
                                    inter = tiles(ps[:, (t % 2) * BANK:(t % 2) * BANK + 2 * SW], NH)
                                    V.tensor_tensor(CT[:, t], inter,
                                                    GT[:, t, 1, z * 32:z * 32 + NH].unsqueeze(2)
                                                    .to_broadcast([P, NH, HD + 1]), ALU.mult)
                                    dve.drain()
                                    V.tensor_tensor(CT[:, t], CT[:, t], out, ALU.add).then_inc(ot_done, 1)
                            elif z == 0:
                                V.tensor_copy(OT[:, t, :], ps[:, o:o + GW]).then_inc(ot_done, 1)
                            else:
                                V.tensor_tensor(OT[:, t, :], OT[:, t, :], ps[:, o:o + GW], ALU.add)\
                                    .then_inc(ot_done, 1)

                        for t in range(NT):
                            attention(t)
                            if t and g != G_C:
                                output(t - 1)
                        output(NT - 1)

                    def head_norm(c, w, gate, centred):
                        heads = [P, NT * NH, HD]
                        sq = Tq
                        dve.drain()
                        if centred:
                            V.reduce_sum(small[:, 64:84], OTh, axis=AXX)
                            dve.drain()
                            V.tensor_scalar(small[:, 64:84], small[:, 64:84], 1.0 / HD, None, ALU.mult)
                            dve.drain()
                            V.tensor_tensor(OTh, OTh, small[:, 64:84].unsqueeze(2).to_broadcast(heads), ALU.subtract)
                            dve.drain()
                        dve.wait_ge(st_out, l * 96 + (16 * 2 * (c + 1)))
                        V.tensor_tensor(sq, OTh, OTh, ALU.mult)
                        dve.drain()
                        V.reduce_sum(small[:, 64:84], sq, axis=AXX).then_inc(nrm_in, 1)
                        dve.wait_ge(nrm_out, c)
                        V.tensor_tensor(OTh, OTh, small[:, 64:84].unsqueeze(2).to_broadcast(heads), ALU.mult)
                        dve.drain()
                        V.tensor_tensor(OTh, OTh, w.unsqueeze(1).to_broadcast(heads), ALU.mult)
                        dve.drain()
                        dve.wait_ge(act_gate, c + 1)
                        V.tensor_tensor(OTh, OTh, gate.rearrange("p (a e) -> p a e", e=HD), ALU.mult)\
                            .then_inc(fin_ready, 1)

                    Tq = area(T0, 1280).rearrange("p (a e) -> p a e", e=HD)

                    mod(0)
                    norm_in(0)
                    ffn(0, 0)
                    norm_out(0)
                    mod(1)
                    norm_in(1)

                    dve.wait_ge(unit_done, UD(U_GATES))
                    b0 = half(U_GATES)
                    gb = W("gb")
                    V.memset(GY[64:128, :], 0.0)
                    V.memset(GM[0:64, :], 0.0)
                    V.memset(GF[0:64, :], 0.0)
                    V.tensor_scalar(halves(GX[0:96, :]), acc(b0)[0:96], gb[0:96, 0:1], None, ALU.add)
                    V.tensor_scalar(halves(GY[0:64, :]), acc(b0 + 2 * BANK)[0:64], gb[0:64, 1:2], None, ALU.add)\
                        .then_inc(unit_evac, 1)
                    dve.drain()
                    dve.sem_inc(gate_pre, 1)
                    V.memset(area(TM0, 1300), 1.0)
                    evac_features(U_C, FM[:, 0:2, :], QSCALE)
                    evac_features(U_C + 1, FM[:, 2:4, :])
                    evac_tokens(U_C + 2, Vc[:, :, :, 0:HD])
                    evac_tokens(U_C + 3, tiles(Oc, NT))
                    dve.wait_ge(gate_sp, 1)
                    V.tensor_scalar(GY[0:64, :], GY[0:64, :], 0.0, None, ALU.min)
                    dve.drain()
                    V.tensor_tensor(GY[0:64, :], GY[0:64, :], GK[0:64, :], ALU.subtract)
                    dve.drain()
                    m0 = W("m0")
                    carry = C("carry")
                    for z, rows in enumerate((slice(0, NH), slice(32, 32 + NH))):
                        for cols, init in (((0, SEQ), 0.0), ((SEQ, NTOK), m0[rows, :])):
                            s = slice(*cols) if z == 0 else slice(cols[1] - 1, cols[0] - 1 if cols[0] else None, -1)
                            V.tensor_tensor_scan(out=GM[rows, s], data0=GY[rows, s], data1=GX[rows, s], initial=init,
                                                 op0=ALU.add, op1=ALU.max)
                        s = slice(None) if z == 0 else slice(None, None, -1)
                        V.tensor_tensor_scan(out=GF[rows, s], data0=carry[rows, :], data1=GY[rows, s], initial=0.0,
                                             op0=ALU.mult, op1=ALU.add)
                    dve.drain()
                    mlast, mprev, rlast, wprev = (small[0:64, a:a + NT] for a in (0, 5, 10, 16))
                    r0, r1 = slice(0, NH), slice(32, 32 + NH)
                    V.tensor_copy(mlast[r0], GM[r0, P - 1::P])
                    V.tensor_copy(small[32:36, 0:NT], GM[r1, 0::P])
                    V.tensor_copy(small[r0, 6:7], m0[r0])
                    V.tensor_copy(small[r1, 9:10], m0[r1])
                    V.tensor_copy(small[r0, 7:10], GM[r0, 2 * P - 1:4 * P:P])
                    V.tensor_copy(small[r1, 6:9], GM[r1, 2 * P:4 * P + 1:P])
                    V.tensor_tensor(GY[0:64, :], GF[0:64, :], GM[0:64, :], ALU.subtract)
                    V.tensor_tensor(GX[0:64, :], GX[0:64, :], GF[0:64, :], ALU.subtract)
                    dve.drain()
                    V.tensor_copy(rlast[r0], GY[r0, P - 1::P])
                    V.tensor_copy(small[32:36, 10:10 + NT], GY[r1, 0::P])
                    dve.drain()
                    V.tensor_tensor(tiles(GF[0:64, :], NT), tiles(GY[0:64, :], NT),
                                    mprev.unsqueeze(2).to_broadcast([64, NT, P]), ALU.add)
                    V.tensor_tensor(tiles(GK[0:64, :], NT), tiles(GX[0:64, :], NT),
                                    rlast.unsqueeze(2).to_broadcast([64, NT, P]), ALU.add)
                    V.tensor_tensor(wprev, rlast, mprev, ALU.add).then_inc(gate_log, 1)
                    dve.wait_ge(gate_cols, 1)
                    for z in range(2):
                        if z:
                            dve.wait_ge(u_done, R(G_C, 0, NT - 1))
                        V.tensor_tensor(ktC.rearrange("p (t h e) -> p t h e", t=NT, h=NH),
                                        kTok.rearrange("p (t h e) -> p t h e", t=NT, h=NH),
                                        GT[:, :, 3, z * 32:z * 32 + NH].unsqueeze(3).to_broadcast([P, NT, NH, HD]),
                                        ALU.mult).then_inc(kt_ready, 1)
                        scan_group(G_C, z, C("blockn"),
                                   lambda f, t: small[:, 24 + (2 * z + f) * NT + t:25 + (2 * z + f) * NT + t])
                        dve.drain()
                        den = CT[:, :, :, HD]
                        d = small[:, 44:64]
                        dt = tiles(d, NT)
                        V.scalar_tensor_tensor(dt, den, -1.0, den, ALU.mult, ALU.max)
                        dve.drain()
                        V.tensor_tensor(dt, dt, GT[:, :, 2, z * 32:z * 32 + NH], ALU.max)
                        dve.drain()
                        V.reciprocal(d, d)
                        dve.drain()
                        num, inv = CT[:, :, :, 0:HD], dt.unsqueeze(3).to_broadcast([P, NT, NH, HD])
                        o4 = OT.rearrange("p t (h e) -> p t h e", h=NH)
                        if z == 0:
                            V.tensor_tensor(o4, num, inv, ALU.mult)
                        else:
                            V.tensor_tensor(num, num, inv, ALU.mult)
                            dve.drain()
                            V.tensor_tensor(o4, o4, num, ALU.add)
                        dve.drain()
                    dve.wait_ge(act_gate, 1)
                    V.tensor_tensor(OT, OT, tiles(Oc, NT), ALU.mult).then_inc(fin_ready, 1)

                    evac_features(U_A, FM[:, 0:2, :], QSCALE)
                    evac_features(U_A + 1, FM[:, 2:4, :])
                    evac_tokens(U_A + 2, tiles(Va, NT))
                    evac_tokens(U_A + 3, tiles(Ga, NT))
                    for z in range(2):
                        dve.wait_ge(asp_done, z + 1)
                        V.scalar_tensor_tensor(Wk, QM.rearrange("p f n -> p (f n)"), 0.0, Wk, ALU.min, ALU.subtract)
                        dve.drain()
                        s = slice(None) if z == 0 else slice(None, None, -1)
                        for f in range(2):
                            V.tensor_tensor_scan(out=tiles(Bk, 2)[:, f, s], data0=carry, data1=tiles(Wk, 2)[:, f, s],
                                                 initial=0.0, op0=ALU.mult, op1=ALU.add)
                        dve.drain()
                        b3 = tiles(Bk, 2 * NT)
                        mid, end = (b3[:, :, 63], b3[:, :, P - 1]) if z == 0 else (b3[:, :, 64], b3[:, :, 0])
                        V.tensor_tensor(tiles(Wk, 2 * NT), b3, mid.unsqueeze(2).to_broadcast([P, 2 * NT, P]),
                                        ALU.subtract)
                        V.tensor_copy(small[:, 96:106], end)
                        V.tensor_tensor(small[:, 106:116], end, mid, ALU.subtract)
                        V.tensor_copy(small[:, 116:126], mid).then_inc(ad_ready, 1)
                        dve.wait_ge(ae_ready, z + 1)
                        V.tensor_tensor(QM, QM, FM[:, 0:2, :], ALU.mult)
                        V.tensor_tensor(KM, KM, FM[:, 2:4, :], ALU.mult).then_inc(aqk_ready, 1)
                        scan_group(G_A, z, C("block"),
                                   lambda f, t: small[:, 96 + f * NT + t:97 + f * NT + t])
                    head_norm(1, W("gnw"), Ga, False)

                    dve.sem_inc(lg_ready, 1)
                    evac_tokens(U_D, RQK[:, :, 0:GW], QSCALE)
                    evac_tokens(U_D + 1, RQK[:, :, GW:2 * GW])
                    evac_tokens(U_D + 2, tiles(Vd, NT))
                    evac_tokens(U_D + 3, tiles(Gd, NT))
                    dve.drain()
                    rope = C("rope").rearrange("p (t s e) -> p t s e", t=NT, s=2)
                    for t in range(NT):
                        x8 = tiles(RQK[:, t, :], 2 * NH)
                        V.tensor_tensor(tiles(rot1[:, t, :], 2 * NH), x8,
                                        rope[:, t, 0, :].unsqueeze(1).to_broadcast([P, 2 * NH, HD]), ALU.mult)
                        x5 = RQK[:, t, :].rearrange("p (h a b e) -> p h a b e", h=2 * NH, a=2, b=2)
                        r5 = rot2[:, t, :].rearrange("p (h a b e) -> p h a b e", h=2 * NH, a=2, b=2)
                        s5 = rope[:, t, 1, :].rearrange("p (a b e) -> p a b e", a=2, b=2)
                        for b in range(2):
                            V.tensor_tensor(r5[:, :, :, b, :], x5[:, :, :, 1 - b, :],
                                            s5[:, :, b, :].unsqueeze(1).to_broadcast([P, 2 * NH, 2, 16]), ALU.mult)
                    dve.drain()
                    V.tensor_tensor(RQK, rot1, rot2, ALU.add).then_inc(rot_ready, 1)
                    dve.wait_ge(lg_sp, 1)
                    lg = small[:, 128:140]
                    V.tensor_scalar(lg, W("rd"), 0.0, None, ALU.min)
                    dve.drain()
                    V.tensor_tensor(lg, lg, small[:, 144:156], ALU.subtract)
                    dve.drain()
                    pc = C("poscol")
                    for z in range(2):
                        last = V.tensor_scalar(small[:, 160 + 4 * z:164 + 4 * z], lg[:, 4 * z:4 * z + 4],
                                               pc[:, z:z + 1], None, ALU.mult)
                    last.then_inc(lg_ready, 1)
                    dve.wait_ge(dec_ready, 1)
                    dm = Dm.rearrange("p z a f i -> p z (a f) i")
                    V.tensor_tensor(dm, dm, causal.unsqueeze(2).to_broadcast([P, 2, 4, P]), ALU.mult)
                    dve.wait_ge(rt_evac, NT)
                    for z in range(2):
                        if z:
                            dve.wait_ge(o_done, R(G_D, 0, NT - 1))
                        V.tensor_tensor(ktD.rearrange("p (t h e) -> p t h e", t=NT, h=NH),
                                        RQK[:, :, GW:2 * GW].rearrange("p t (h e) -> p t h e", h=NH),
                                        small[:, 160 + 4 * z:164 + 4 * z].unsqueeze(1).unsqueeze(3)
                                        .to_broadcast([P, NT, NH, HD]), ALU.mult)
                        V.tensor_tensor(QM.rearrange("p f (t i) -> p f t i", t=NT),
                                        FM[:, 0:2, :].rearrange("p f (t i) -> p f t i", t=NT),
                                        qdec[:, z].unsqueeze(2).to_broadcast([P, 2, NT, P]), ALU.mult)\
                            .then_inc(kt_ready, 1)
                        scan_group(G_D, z, C("block"), lambda f, t: small[:, 168 + 2 * z + f:169 + 2 * z + f])
                    head_norm(2, W("rnw"), Gd, True)

                    evac_features(U_B, FM[:, 0:2, :], QSCALE)
                    evac_features(U_B + 1, FM[:, 2:4, :])
                    evac_tokens(U_B + 2, tiles(Va, NT))
                    dve.wait_ge(rpb_loaded, l * 16 + (16))
                    r3 = rpb.rearrange("p (m c) -> p m c", c=HD)
                    V.tensor_tensor(r3, r3, C("namask").unsqueeze(1).to_broadcast([P, 14 * NH, HD]), ALU.add)
                    dve.drain()

                    def na_in(b):
                        t, h = b // NH, b % NH
                        c = (h % 2) * 2 * BANK
                        s = SB[b % 2]
                        dve.wait_ge(na_s, b + 1)
                        if b >= 2:
                            dve.wait_ge(na_pt, b - 1)
                        if t == 0:
                            V.tensor_copy(s[:, 0:P], ps[:, c:c + P]).then_inc(na_read, 1)
                            n = P
                        else:
                            m = (h * 14 + 6 - 2 * (t - 1)) * HD
                            V.tensor_tensor(s[:, 0:DEC], ps[:, c:c + DEC], rpb[:, m:m + DEC], ALU.add)
                            V.tensor_copy(s[:, DEC:NTOK], ps[:, c + BANK:c + BANK + P]).then_inc(na_read, 1)
                            n = NTOK
                        dve.drain()
                        V.tensor_reduce(out=small[:, 176 + b:177 + b], in_=s[:, 0:n], op=ALU.max, axis=AXX,
                                        negate=True).then_inc(na_max, 1)

                    def na_outp(b):
                        t, h = b // NH, b % NH
                        dve.wait_ge(na_o, b + 1)
                        V.reciprocal(small[:, 220 + b:221 + b], small[:, 200 + b:201 + b])
                        dve.drain()
                        o = (6 + b % 2) * BANK
                        last = V.tensor_scalar(OT[:, t, h * HD:(h + 1) * HD], ps[:, o:o + HD],
                                               small[:, 220 + b:221 + b], None, ALU.mult)
                        last.then_inc(na_oc, 1)

                    na_in(0)
                    for b in range(NT * NH):
                        if b + 1 < NT * NH:
                            na_in(b + 1)
                        na_outp(b)
                    dve.drain()
                    dve.sem_inc(fin_ready, 1)

                    for q in range(4):
                        evac_features(U_OUT + q, yT[:, 2 * q:2 * q + 2, :])
                    norm_out(1)
                    mod(2)
                    norm_in(2)
                    ffn(2, 1)
                    norm_out(2)

            nums = sorted(s.num for s in sems)
            assert nums == list(range(nums[0], nums[-1] + 1))
            nc.sync.sem_clear(range(nums[0], nums[-1] + 1))
            nc.all_engine_barrier()

        with nc.Block() as block:
            @block.sync
            def _(sp):
                sp.dma_start(O["y"], xT).then_inc(y_out, 16)
                sp.wait_ge(y_out, 16)


def constants():
    import numpy as np

    c = np.zeros((P, CONST_W), np.float32)

    def put(name, a):
        at, w = CONSTS[name]
        c[:, at:at + w] = np.asarray(a, np.float64).reshape(-1, w)

    i = np.arange(P)
    put("ident", np.eye(P))
    put("ones", np.ones((P, P)))
    tok = np.arange(DEC)
    inv = 10000.0 ** (-np.arange(16, dtype=np.float32) / 16)
    ang = np.stack([(tok // GRID_W)[:, None] * inv, (tok % GRID_W)[:, None] * inv], 1)
    cs = np.concatenate([np.ones((SEQ, 2, 16)), np.cos(ang.astype(np.float32))])
    sn = np.concatenate([np.zeros((SEQ, 2, 16)), np.sin(ang.astype(np.float32))])
    table = np.stack([np.stack([cs, cs], 2), np.stack([-sn, sn], 2)], 1)
    put("rope", table.reshape(NT, P, 2 * HD).transpose(1, 0, 2))
    q, k = np.arange(GRID_W)[:, None], np.arange(GRID_W)[None]
    lo = np.clip(q - WIN // 2, 0, GRID_W - WIN)
    put("namask", np.tile(np.where((k >= lo) & (k < lo + WIN), 0.0, NEG), (2, 1)))
    j = i[:, None]
    causal = np.stack([i[None] >= j, i[None] <= j], 1)
    put("causal", causal)
    put("anti", np.where(causal, 0.0, NEG))
    put("block", (i[:, None] // HD == i[None] // HD))
    put("blockn", (i[:, None] // HD == np.arange(SW)[None] // (HD + 1)))
    put("diff", np.stack([np.maximum(i[None] - j, 0), np.maximum(j - i[None], 0)], 1))
    put("posrow", np.broadcast_to(np.stack([i + 1, P - i]), (P, 2, P)))
    put("poscol", np.stack([P - 1 - i, i], 1))
    put("carry", np.broadcast_to(np.arange(NTOK) % P != 0, (P, NTOK)))
    return c


def lay_out(v):
    import numpy as np

    f = np.float32

    def blocks(w, cols):
        n = w.shape[-1] // cols
        return np.ascontiguousarray(w.reshape(DEPTH, KT, P, n, cols).transpose(0, 3, 2, 1, 4)).reshape(
            DEPTH, n, P, KT * cols)

    d = {"const": constants()}
    x = np.concatenate([v["x_prompt"][0], v["x_sample"][0]])
    d["x"] = np.ascontiguousarray(x.T.reshape(KT, P, NTOK).transpose(1, 0, 2))
    d["cond"] = np.ascontiguousarray(np.stack([v["c_ctx"], v["c"][0]], 1).reshape(KT, P, 2).transpose(1, 0, 2))
    d["w_mod"] = blocks(v["w_mod"], 256)
    w1, w3 = (v[n].reshape(DEPTH, 2, KT, P, FT, P).transpose(0, 1, 4, 3, 2, 5) for n in ("ffn_w1", "ffn_w3"))
    d["w13"] = np.stack([w1, w3], 4).reshape(DEPTH, 2 * FT, P, 2 * DM)
    d["w2"] = np.ascontiguousarray(v["ffn_w2"].reshape(DEPTH, 2, FT, P, KT, P).transpose(0, 1, 4, 3, 2, 5)).reshape(
        DEPTH, 2 * KT, P, SLOT_W)
    names = ["gq", "gk", "gv", "gg", "ga", "nq", "nk", "nv", "mq", "mk", "mv", "mo", "mi", "mf", "rq", "rk", "rv", "rg"]
    sizes = [GW] * 4 + [32] + [GW] * 7 + [8, 8] + [GW] * 4
    at = np.concatenate([[0], np.cumsum(sizes)])
    col = {n: v["w_in"][:, :, at[i]:at[i + 1]] for i, n in enumerate(names)}
    d["w_in"] = blocks(np.concatenate([col[n] for n in (
        "mq", "mk", "mv", "mo", "gq", "gk", "gv", "gg", "rq", "rk", "rv", "rg", "nq", "nk", "nv")], -1), 256)
    g = np.zeros((DEPTH, DM, 160), f)
    g[:, :, 64:96] = col["ga"]
    for z in range(2):
        g[:, :, z * 32:z * 32 + NH] = col["mi"][:, :, z * NH:(z + 1) * NH]
        g[:, :, 96 + z * 32:96 + z * 32 + NH] = col["mf"][:, :, z * NH:(z + 1) * NH]
    d["w_gates"] = blocks(g, 160)[:, 0]
    d["w_out"] = blocks(v["w_out"], 256)

    p = np.zeros((DEPTH, P, PARAM_W), f)

    def part(name):
        a, w = PARAMS[name]
        return p[:, :, a:a + w]

    part("bmod")[:] = v["b_mod"].reshape(DEPTH, 9 * KT, P).transpose(0, 2, 1)
    part("normw")[:] = v["norm_w"].reshape(DEPTH, 6 * KT, P).transpose(0, 2, 1)
    part("ba")[:] = v["gla_b_a"].reshape(DEPTH, 4, P).transpose(0, 2, 1)
    d["wa2"] = wa2 = np.zeros((DEPTH, 32, 4 * P), f)
    for z in range(2):
        part("gb")[:, z * 32:z * 32 + NH, 0] = v["mlstm_b_i"][:, z]
        part("gb")[:, z * 32:z * 32 + NH, 1] = v["mlstm_b_f"][:, z]
        part("m0")[:, z * 32:z * 32 + NH, 0] = v["state_mlstm_m"][0, :, z]
        wa2[:, z * 16:(z + 1) * 16, z * 2 * P:(z + 1) * 2 * P] = v["gla_w_a2"][:, z]
    part("rd")[:, :, 0:8] = v["ret_decay"].reshape(DEPTH, 1, 8)
    part("rd")[:, :, 8:12] = np.repeat(v["ret_decay"].reshape(DEPTH, 4, 2), HD, axis=2).transpose(0, 2, 1)
    part("gnw")[:] = v["gla_norm_w"][:, None]
    part("rnw")[:] = v["ret_norm_w"][:, None]
    part("kc")[:] = v["cache_na_k"][0].reshape(DEPTH, 2, 2, P, HD).transpose(0, 2, 4, 1, 3).reshape(DEPTH, P, 2 * P)
    part("vc")[:] = v["cache_na_v"][0].transpose(0, 2, 1, 3).reshape(DEPTH, P, GW)
    d["par"] = p

    st = np.zeros((DEPTH, 2, 2, P, 2, P), f)
    sc = np.zeros((DEPTH, 2, P, 2, SW), f)
    for h in range(NH):
        fa, a = h // 2, h % 2
        rows, cols = slice(a * HD, (a + 1) * HD), slice(a * HD, (a + 1) * HD)
        st[:, 0, :, rows, fa, cols] = v["state_gla"][0, :, :, h]
        st[:, 1, :, rows, fa, cols] = v["state_ret"][0, :, :, h]
        sc[:, :, rows, fa, a * (HD + 1):a * (HD + 1) + HD] = v["state_mlstm_C"][0, :, :, h]
        sc[:, :, rows, fa, a * (HD + 1) + HD] = v["state_mlstm_n"][0, :, :, h]
    d["st_ad"], d["st_c"] = st, sc
    r = np.zeros((DEPTH, NH, 15, 2 * HD - 1), f)
    r[:, :, :, HD - WIN:HD + WIN - 1] = v["na_rpb"]
    d["rpb"] = np.stack([r[:, :, 1 - row:15 - row, HD - 1 - q:2 * HD - 1 - q].reshape(DEPTH, -1)
                         for row in range(2) for q in range(GRID_W)], 1)
    return d


OUTS = {"y": (P, KT, NTOK), "nak": (DEPTH, P, 2, P), "nav": (DEPTH, P, GW), "gla": (DEPTH, 2, P, 2, P),
        "ret": (DEPTH, 2, P, 2, P), "mc": (DEPTH, 2, P, 2, SW), "mm": (DEPTH, 64, 1)}


def kernel(**inputs):
    import numpy as np
    import concourse.bacc as bacc
    from concourse.bass_utils import run_bass_kernel_spmd

    arrays = lay_out({k: np.asarray(a) for k, a in inputs.items()})
    nc = bacc.Bacc("TRN2", target_bir_lowering=False, num_devices=1)
    I = {k: nc.dram_tensor("in_" + k, a.shape, FP, kind="ExternalInput").ap() for k, a in arrays.items()}
    O = {k: nc.dram_tensor("out_" + k, s, FP, kind="ExternalOutput").ap() for k, s in OUTS.items()}
    build(nc, I, O)
    r = run_bass_kernel_spmd(nc, [{"in_" + k: a for k, a in arrays.items()}], core_ids=[0]).results[0]
    o = {k: np.asarray(r["out_" + k]) for k in OUTS}

    y = o["y"].transpose(2, 1, 0).reshape(NTOK, DM)
    nak = o["nak"].reshape(DEPTH, 2, HD, 2, P).transpose(0, 3, 1, 4, 2).reshape(1, DEPTH, NH, P, HD)
    nav = o["nav"].reshape(DEPTH, P, NH, HD).transpose(0, 2, 1, 3)[None]

    def heads(s, w, lo, hi):
        b = [s[:, :, a * HD:(a + 1) * HD, f, a * w + lo:a * w + hi] for f in range(2) for a in range(2)]
        return np.ascontiguousarray(np.stack(b, 2))[None]

    mm = np.stack([o["mm"][:, 0:NH, 0], o["mm"][:, 32:32 + NH, 0]], 1)[None]
    return (np.ascontiguousarray(y[:SEQ])[None], np.ascontiguousarray(y[SEQ:])[None],
            np.ascontiguousarray(nak), np.ascontiguousarray(nav),
            heads(o["gla"], HD, 0, HD), heads(o["mc"], HD + 1, 0, HD), heads(o["mc"], HD + 1, HD, HD + 1)[..., 0],
            np.ascontiguousarray(mm), heads(o["ret"], HD, 0, HD))
```

```python
import concourse.bass as bass
from concourse import mybir
from contextlib import ExitStack

FP = mybir.dt.float32
FR = mybir.dt.float32r
ALU = mybir.AluOpType
ACT = mybir.ActivationFunctionType
AXX = mybir.AxisListType.X

P = 128
DM = 1024
KT = DM // P
SEQ, DEC = 128, 512
NTOK = SEQ + DEC
NT = NTOK // P
HALF = NTOK // 2
DEPTH = 2
FF = 2816
FT = FF // P
HD = 64
NH = 4
GW = NH * HD
EPS = 1e-6
BANK = 512
GF_T = FT // 2
SLOTS = 2
SLOT_W = 2 * DM
QSCALE = HD ** -0.5
TAU = 16.0
NEG = -1e30
ROWS, GRID_W, WIN = DEC // 64, 64, 16
SW = 2 * (HD + 1)

MOD_U = 3 * KT // 2
U_FFN = (MOD_U, 0, 94)
GRP_U = (GF_T + MOD_U + KT, 0, GF_T + KT)
U_GATES = U_FFN[0] + 2 * GRP_U[0]
U_C = U_GATES + 1
U_A = U_C + 4
U_D = U_A + 4
U_B = U_D + 4
U_OUT = U_B + 3
U_ALL = U_FFN[2] + 2 * GRP_U[2]
assert U_OUT + 4 == U_FFN[2] and U_ALL == 132
MODS = set(range(MOD_U))
for _g in range(2):
    _n = U_FFN[0] + _g * GRP_U[0]
    MODS |= {_n + 2 * _m for _m in range(MOD_U)}
SPLIT = [n for n in range(U_ALL) if n not in MODS]

CONSTS = {}
_at = 0
for _name, _w in (("ident", P), ("ones", P), ("rope", NT * 2 * HD), ("namask", HD), ("causal", 2 * P),
                  ("anti", 2 * P), ("block", P), ("blockn", SW), ("diff", 2 * P), ("posrow", 2 * P),
                  ("poscol", 2), ("carry", NTOK)):
    CONSTS[_name] = (_at, _w)
    _at += _w
CONST_W = _at

PARAMS = {}
_at = 0
for _name, _w in (("bmod", 9 * KT), ("normw", 6 * KT), ("ba", 4), ("gb", 2), ("m0", 1), ("rd", 12),
                  ("gnw", HD), ("rnw", HD), ("kc", 2 * P), ("vc", GW)):
    PARAMS[_name] = (_at, _w)
    _at += _w
PARAM_W = _at


def build(nc, I, O):
    ctx = ExitStack()
    with ctx:
        def sb(name, words):
            return ctx.enter_context(nc.sbuf_tensor(name, [P, words], FP))

        sems = []

        def sem(name):
            s = ctx.enter_context(nc.semaphore(name))
            sems.append(s)
            return s

        xT = sb("xT", KT * NTOK)[:, :].rearrange("p (k n) -> p k n", k=KT)
        raw = sb("raw", SLOTS * SLOT_W)
        const = sb("const", CONST_W)
        par = sb("par", PARAM_W)
        modS = sb("modS", 9 * KT * 2)[:, :].rearrange("p (m c) -> p m c", c=2)
        gs_all = sb("gs", 3 * KT * 2)[:, :].rearrange("p (s m c) -> p s m c", s=3, c=2)
        gg_all = sb("gg", 3 * KT * 2)[:, :].rearrange("p (s m c) -> p s m c", s=3, c=2)
        cond = sb("cond", KT * 2)[:, :].rearrange("p (m c) -> p m c", c=2)
        mrow = sb("mrow", 256)
        rstd = sb("rstd", NTOK)
        small = sb("small", 256)

        def split_sb(name, words):
            return ctx.enter_context(nc.sbuf_tensor(name, [P, 2, words], FR))

        h2 = split_sb("h2", KT * NTOK)[:, :, :].rearrange("p s (k n) -> p s k n", k=KT)
        w_split = [split_sb(f"wsplit{i}", SLOT_W) for i in range(SLOTS)]
        ARENA_W = 20020
        arena_at = -(-nc.sbuf_base // 32) * 32
        arena = sb("arena", ARENA_W)
        a2 = nc.alloc_sbuf_tensor_at("hidden", [P, 2, GF_T * NTOK], FR, offset=arena_at)[:, :, :]\
            .rearrange("p s (k n) -> p s k n", k=GF_T)
        ps = ctx.enter_context(nc.psum_tensor("ps", [P, 8 * BANK], FP))

        def C(name, parts=P):
            a, w = CONSTS[name]
            return const[0:parts, a:a + w]

        def W(name, parts=P):
            a, w = PARAMS[name]
            return par[0:parts, a:a + w]

        def area(a, w):
            return arena[:, a:a + w]

        def tiles(ap, n):
            return ap.rearrange("p (t n) -> p t n", t=n)

        sqb = area(2 * GF_T * NTOK, NTOK)
        yT = tiles(area(ARENA_W - KT * NTOK, KT * NTOK), KT)
        OT = tiles(area(0, 1280), NT)
        FM = tiles(area(1280, 2560), 4)
        TM0 = 3840
        T0 = TM0 + 5140
        catP = [tiles(area(ARENA_W - 1280 * (i + 1), 1280), 2) for i in range(4)]
        CAT_K = [4, 0, 6, 2]
        OTh = area(0, 1280).rearrange("p (a e) -> p a e", e=HD)
        Tst = area(T0, 1300).rearrange("p (t f w) -> p t f w", t=NT, f=2)
        Sin = area(T0 + 1300, 1300).rearrange("p (t f w) -> p t f w", t=NT, f=2)
        Asb = [area(T0 + 2600 + 512 * i, 512).rearrange("p (a f i) -> p a f i", a=2, f=2) for i in (0, 1)]
        GX = area(T0 + 3624, NTOK)
        GY = area(T0 + 4264, NTOK)
        GM = area(T0 + 4904, NTOK)
        GF = area(T0 + 5544, NTOK)
        GK = area(T0 + 6184, NTOK)
        CT = area(T0 + 4904, 1300).rearrange("p (t h w) -> p t h w", t=NT, h=NH)
        GT = area(T0 + 6824, 1280).rearrange("p (t a r) -> p t a r", t=NT, a=4)
        WL = [area(T0 + 8104 + 512 * i, 512).rearrange("p (a f i) -> p a f i", a=2, f=2) for i in (0, 1)]
        Vc = area(TM0, 1300).rearrange("p (t h w) -> p t h w", t=NT, h=NH)
        Oc = area(TM0 + 1300, 1280)
        kTok = area(TM0 + 2580, 1280)
        ktC = area(TM0 + 3860, 1280)
        Wk = area(T0 + 4264, 1280)
        Bk = area(TM0 + 2560, 1280)
        QM = tiles(area(T0 + 6824, 1280), 2)
        KM = tiles(area(T0 + 5544, 1280), 2)
        wa2 = area(TM0 + 3840, 4 * P)
        Va = area(TM0, 1280)
        Ga = area(TM0 + 1280, 1280)
        RQK = tiles(area(TM0, 2560), NT)
        rot1 = tiles(area(T0, 2560), NT)
        rot2 = tiles(area(T0 + 2560, 2560), NT)
        Vd = area(TM0 + 2560, 1280)
        Gd = area(TM0 + 3840, 1280)
        ktD = area(T0 + 5160, 1280)
        QD = tiles(area(T0 + 6440, 1280), 2)
        Dm = area(T0 + 3624, 1024).rearrange("p (z a f i) -> p z a f i", z=2, a=2, f=2)
        qdec = area(T0 + 4648, 512).rearrange("p (z f i) -> p z f i", z=2, f=2)
        SB = [area(T0 + NTOK * i, NTOK) for i in (0, 1)]
        PT = area(T0 + 1280, NTOK)
        rpb = area(T0 + 1920, NH * 14 * HD)

        ident, ones = C("ident"), C("ones")
        causal = C("causal").rearrange("p (z i) -> p z i", z=2)
        anti = C("anti").rearrange("p (z i) -> p z i", z=2)

        rpb_loaded = sem("rpb_loaded")
        wa2_loaded = sem("wa2_loaded")
        loaded = [sem(f"slot{i}_loaded") for i in range(SLOTS)]
        pool_hi = sem("pool_hi")
        split_done = sem("split_done")
        mrow_ready = sem("mrow_ready")
        turn_begun = sem("turn_begun")
        split_begun = sem("split_begun")
        mtr_done = sem("mtr_done")
        a_hi = sem("a_hi")
        a_lo = sem("a_lo")
        acc_add = sem("acc_add")
        y_scaled = sem("y_scaled")
        y_norm = sem("y_norm")
        h_hi = sem("h_hi")
        cat_hi = sem("cat_hi")
        cat_split = sem("cat_split")
        init_loaded = sem("init_loaded")
        st_out = sem("st_out")
        na_out = sem("na_out")
        m_out = sem("m_out")
        unit_done = sem("unit_done")
        unit_evac = sem("unit_evac")
        par_loaded = sem("par_loaded")
        mod_ready = sem("mod_ready")
        sq_ready = sem("sq_ready")
        ss_done = sem("ss_done")
        rstd_ready = sem("rstd_ready")
        hmul_ready = sem("hmul_ready")
        h_ready = sem("h_ready")
        silu_done = sem("silu_done")
        x_ready = sem("x_ready")
        gate_pre = sem("gate_pre")
        gate_sp = sem("gate_sp")
        gate_log = sem("gate_log")
        gate_exp = sem("gate_exp")
        gate_t = sem("gate_t")
        gate_cols = sem("gate_cols")
        apre_done = sem("apre_done")
        asp_done = sem("asp_done")
        ad_ready = sem("ad_ready")
        ae_ready = sem("ae_ready")
        aqk_ready = sem("aqk_ready")
        akt_done = sem("akt_done")
        akt_ready = sem("akt_ready")
        lg_ready = sem("lg_ready")
        lg_sp = sem("lg_sp")
        dec_ready = sem("dec_ready")
        rot_ready = sem("rot_ready")
        rt_done = sem("rt_done")
        rt_evac = sem("rt_evac")
        kt_ready = sem("kt_ready")
        u_done = sem("u_done")
        t_done = sem("t_done")
        s_ready = sem("s_ready")
        p_done = sem("p_done")
        wl_done = sem("wl_done")
        w_ready = sem("w_ready")
        a_done = sem("a_done")
        o_done = sem("o_done")
        ot_done = sem("ot_done")
        act_gate = sem("act_gate")
        nrm_in = sem("nrm_in")
        nrm_out = sem("nrm_out")
        fin_ready = sem("fin_ready")
        cat_t = sem("cat_t")
        cat_done = sem("cat_done")
        na_s = sem("na_s")
        na_read = sem("na_read")
        na_max = sem("na_max")
        na_e = sem("na_e")
        na_pt = sem("na_pt")
        na_ptc = sem("na_ptc")
        na_o = sem("na_o")
        na_oc = sem("na_oc")
        start = sem("start_loads")
        cond_ready = sem("cond_ready")
        y_out = sem("y_out")

        UD = lambda n: n + 1 + SLOTS
        EV = lambda n: n + 1 + 2
        slot = lambda n: n % SLOTS
        use = lambda n: 16 * (n // SLOTS + 1)
        SD = lambda n: SPLIT.index(n) + 1
        half = lambda n: (n % 2) * 4 * BANK
        G_C, G_A, G_D = 0, 1, 2
        R = lambda g, z, t: (g * 2 + z) * NT + t + 1
        Z = lambda g, z: g * 2 + z + 1
        HEADS = [(h // 2, h % 2) for h in range(NH)]
        order = lambda z: (1, 2, 3, 4) if z == 0 else (4, 3, 2, 1)

        def acc(base):
            return ps[:, base:base + 2 * BANK].rearrange("p (a n) -> p a n", a=2)[:, :, 0:HALF]

        def halves(ap):
            return ap.rearrange("p (a n) -> p a n", a=2)

        def slot_ap(n, words):
            return raw[:, slot(n) * SLOT_W:slot(n) * SLOT_W + words]

        def split_ap(n, words):
            return w_split[SPLIT.index(n) % SLOTS][:, :, 0:words]

        with nc.Block() as block:
            @block.sync
            def _(sp):
                sp.dma_start(const[:, :], I["const"]).then_inc(start, 16)
                sp.dma_start(xT, I["x"]).then_inc(start, 16)
                sp.dma_start(cond, I["cond"]).then_inc(start, 16)
                sp.wait_ge(start, 48)

            @block.scalar
            def _(act):
                act.wait_ge(start, 48)
                act.activation(cond, cond, ACT.Silu).then_inc(cond_ready, 1)
                act.wait_ge(cond_ready, 1)

        with nc.Fori(0, DEPTH) as l:
            with nc.Block() as block:
                @block.sync
                def _(sp):
                    sp.dma_start(par[:, :], I["par"][l]).then_inc(par_loaded, 16)

                    def load(n, words, src, i=0, du=2, ds=2):
                        if n - SLOTS in SPLIT:
                            sp.wait_ge(split_done, i * ds + SD(n - SLOTS))
                        else:
                            sp.wait_ge(unit_done, i * du + UD(n - SLOTS))
                        sp.dma_start(slot_ap(n, words), src).then_inc(loaded[slot(n)], 16)

                    with sp.Fori(0, MOD_U // 2) as i:
                        for u in range(2):
                            load(u, SLOT_W, I["w_mod"][l, i * 2 + u], i)
                    for s, j in ((0, 0), (2, 1)):
                        for grp in range(2):
                            n = U_FFN[s] + grp * GRP_U[s]
                            f0 = j * FT + grp * GF_T
                            if s == 0:
                                m0 = MOD_U * (1 + grp)
                                load(n, SLOT_W, I["w_mod"][l, m0])
                                load(n + 1, SLOT_W, I["w13"][l, f0])
                                load(n + 2, SLOT_W, I["w_mod"][l, m0 + 1])
                                with sp.Fori(0, GF_T - 1) as i:
                                    load(n + 3, SLOT_W, I["w13"][l, i + (f0 + 1)], i, ds=1)
                                    load(n + 4, SLOT_W, I["w_mod"][l, i + (m0 + 2)], i)
                                n += GF_T + MOD_U
                            else:
                                with sp.Fori(0, GF_T // 2) as i:
                                    for u in range(2):
                                        load(n + u, SLOT_W, I["w13"][l, i * 2 + (f0 + u)], i)
                                load(n + GF_T - 1, SLOT_W, I["w13"][l, f0 + GF_T - 1])
                                n += GF_T
                            d0 = (2 * j + grp) * KT
                            for u in range(2):
                                load(n + u, GF_T * P, I["w2"][l, d0 + u])
                            with sp.Fori(0, KT // 2 - 1) as i:
                                for u in range(2):
                                    load(n + 2 + u, GF_T * P, I["w2"][l, i * 2 + (d0 + 2 + u)], i)
                        if s == 0:
                            load(U_GATES, KT * 160, I["w_gates"][l])
                            for q in range(15):
                                load(U_C + q, SLOT_W, I["w_in"][l, q])
                            for q in range(4):
                                load(U_OUT + q, SLOT_W, I["w_out"][l, q])

                @block.gpsimd
                def _(pool):
                    def split(n, words, i=0, du=2):
                        pool.wait_ge(loaded[slot(n)], i * (8 * du) + use(n))
                        k = SPLIT.index(n)
                        if k >= SLOTS:
                            pool.wait_ge(unit_done, i * du + UD(SPLIT[k - SLOTS]))
                        pool.sem_inc(split_begun, 1)
                        w, src = split_ap(n, words), slot_ap(n, words)
                        nc.gpsimd.tensor_scalar(w[:, 0], src, 1.0, 1.0, ALU.mult, ALU.mult).then_inc(pool_hi, 1)
                        pool.wait_ge(pool_hi, i * 2 + (k + 1))
                        nc.gpsimd.tensor_tensor(w[:, 1], src, w[:, 0].bitcast(FP), ALU.subtract)\
                            .then_inc(split_done, 1)

                    for s in (0, 2):
                        step = 2 if s == 0 else 1
                        for grp in range(2):
                            n = U_FFN[s] + grp * GRP_U[s] + step - 1
                            for u in range(2):
                                split(n + u * step, SLOT_W)
                            with pool.Fori(0, (GF_T - 3) // 2) as i:
                                for u in range(2):
                                    split(n + (2 + u) * step, SLOT_W, i, 2 * step)
                            split(n + (GF_T - 1) * step, SLOT_W)
                            n = U_FFN[s] + (grp + 1) * GRP_U[s] - KT
                            for u in range(2):
                                split(n + u, GF_T * P)
                            with pool.Fori(0, KT // 2 - 1) as i:
                                for u in range(2):
                                    split(n + 2 + u, GF_T * P, i)
                        if s == 0:
                            split(U_GATES, KT * 160)
                            for q in range(19):
                                split(U_C + q, SLOT_W)

                @block.tensor
                def _(pe):
                    mm = pe.matmul
                    pe.sem_inc(unit_done, SLOTS)

                    def claim(n, i=0, du=2):
                        pe.wait_ge(split_done, i * 2 + SD(n))
                        pe.wait_ge(unit_evac, i * du + (n + 1))
                        return half(n)

                    def three_pass(out, w, x, first, last):
                        mm(out, w[0], x[0], start=first, stop=False)
                        mm(out, w[0], x[1], start=False, stop=False)
                        return mm(out, w[1], x[0], start=False, stop=last)

                    def mod(n, i=0, du=2):
                        pe.wait_ge(loaded[slot(n)], i * (8 * du) + use(n))
                        pe.wait_ge(unit_evac, i * du + (n + 1))
                        w = tiles(slot_ap(n, SLOT_W), KT)
                        for k in range(KT):
                            last = mm(ps[0:2, half(n):half(n) + 256], cond[:, k, :], w[:, k, :],
                                      start=k == 0, stop=k == KT - 1)
                        last.then_inc(unit_done, 1)

                    def mod_turn(n, q, i=0):
                        pe.wait_ge(mrow_ready, i + (q + 1))
                        pe.sem_inc(turn_begun, 1)
                        for m in range(2):
                            c = half(n) + BANK + 2 * m
                            last = pe.transpose(ps[:, c:c + 2], mrow[0:2, m * P:(m + 1) * P], ident[0:2, 0:2])
                        last.then_inc(mtr_done, 1)

                    def sums(v, n, fill=None):
                        pe.wait_ge(unit_evac, EV(n - 1))
                        if v % 2 == 0:
                            for k in range(KT):
                                pe.wait_ge(sq_ready, KT * v + k + 1)
                                for a in range(2):
                                    last = mm(ps[:, (2 + a) * BANK:(2 + a) * BANK + HALF], ones, yT[:, k, a * HALF:(a + 1) * HALF],
                                              start=k == 0, stop=k == KT - 1)
                        else:
                            pe.wait_ge(acc_add, KT * (v // 2 + 1))
                            for a in range(2):
                                last = mm(ps[:, (2 + a) * BANK:(2 + a) * BANK + HALF], ones, rstd[:, a * HALF:(a + 1) * HALF],
                                          start=True, stop=True)
                        last.then_inc(ss_done, 1)
                        if fill:
                            fill()
                        pe.wait_ge(rstd_ready, v + 1)

                    def feature_major(base, w, x, cols=P, between=None, need=None):
                        nk = w.shape[2]
                        for a in range(2):
                            for k in range(nk):
                                if need and a == 0:
                                    need(k)
                                last = three_pass(ps[0:cols, base + a * BANK:base + a * BANK + HALF],
                                                  (w[:, 0, k, :], w[:, 1, k, :]),
                                                  [x[:, p, k, a * HALF:(a + 1) * HALF] for p in range(2)],
                                                  k == 0, k == nk - 1)
                            if a == 0 and between:
                                between()
                        return last

                    def first_products(s, base, blocks):
                        for k in range(KT):
                            pe.wait_ge(h_ready, KT * s + k + 1)
                            for b, w in enumerate(blocks):
                                for a in range(2):
                                    c = base + (2 * b + a) * BANK
                                    last = three_pass(ps[0:w.shape[3], c:c + HALF], (w[:, 0, k, :], w[:, 1, k, :]),
                                                      [h2[:, p, k, a * HALF:(a + 1) * HALF] for p in range(2)],
                                                      k == 0, k == KT - 1)
                        last.then_inc(unit_done, 1)

                    def up_weights(n):
                        w = split_ap(n, SLOT_W).rearrange("p s (b k c) -> p s b k c", b=2, k=KT)
                        return w[:, :, 0], w[:, :, 1]

                    def up(n, i=0, du=2, between=None):
                        base = claim(n, i, du)
                        gate, value = up_weights(n)
                        feature_major(base, gate, h2)
                        if between:
                            between()
                        feature_major(base + 2 * BANK, value, h2).then_inc(unit_done, 1)

                    def down(n, i=0, between=None, need=None):
                        base = claim(n, i)
                        w = split_ap(n, GF_T * P).rearrange("p s (f c) -> p s f c", f=GF_T)
                        feature_major(base, w, a2, between=between, need=need).then_inc(unit_done, 1)

                    def ffn(s, j):
                        for grp in range(2):
                            n = U_FFN[s] + grp * GRP_U[s]
                            q = MOD_U * (1 + grp)
                            if s == 0 and grp:
                                mod(n)
                            f = n + (s == 0)
                            turn = (lambda: mod_turn(n, q)) if s == 0 else None
                            if grp:
                                up(f, between=turn)
                            else:
                                first_products(s, claim(f), up_weights(f))
                                if turn:
                                    turn()
                            if s == 0:
                                mod(n + 2)
                                with pe.Fori(0, GF_T // 2) as i:
                                    for u in range(2):
                                        m = n + 2 + 2 * u
                                        up(m + 1, i, 4, lambda: mod_turn(m, q + 1 + u, i * 2))
                                        mod(m + 2, i, 4)
                                n += GF_T + MOD_U
                                turn = lambda: mod_turn(n - 1, q + GF_T)
                            else:
                                with pe.Fori(0, GF_T // 2) as i:
                                    for u in range(2):
                                        up(n + 1 + u, i)
                                n += GF_T
                                turn = None

                            def hidden(k):
                                if k in (0, GF_T - 1):
                                    pe.wait_ge(a_lo, 1 + j * FT + grp * GF_T + (GF_T if k else GF_T - 1))

                            down(n, between=turn, need=hidden)
                            down(n + 1)
                            with pe.Fori(0, KT // 2 - 1) as i:
                                for u in range(2):
                                    down(n + 2 + u, i)

                    def features(n, x=h2):
                        base = claim(n)
                        w = split_ap(n, KT * 256).rearrange("p s (k m c) -> p s k m c", k=KT, m=2)
                        for m in range(2):
                            last = feature_major(base + 2 * m * BANK, w[:, :, :, m], x)
                        last.then_inc(unit_done, 1)

                    def tokens(n):
                        base = claim(n)
                        w = split_ap(n, KT * 256).rearrange("p s (k c) -> p s k c", k=KT)
                        for t in range(NT):
                            for k in range(KT):
                                last = three_pass(ps[:, base + t * GW:base + (t + 1) * GW],
                                                  [h2[:, p, k, t * P:(t + 1) * P] for p in range(2)],
                                                  (w[:, 0, k, :], w[:, 1, k, :]), k == 0, k == KT - 1)
                        last.then_inc(unit_done, 1)

                    def gates():
                        base = claim(U_GATES)
                        w = split_ap(U_GATES, KT * 160).rearrange("p s (k c) -> p s k c", k=KT)
                        first_products(1, base, (w[:, :, :, 0:96], w[:, :, :, 96:160]))

                    def tr(col, src, rows=P):
                        return pe.transpose(ps[:, col:col + rows], src, ident[0:rows, 0:rows])

                    def scan_group(g, z, k2, q2, qi, kt, v, vw):
                        for t in range(NT):
                            if t >= 2:
                                pe.wait_ge(t_done, R(g, z, t - 2))
                            for f in range(2):
                                c = (t % 2) * BANK + f * 2 * vw
                                last = mm(ps[:, c:c + 2 * vw], kt[:, t, f * P:(f + 1) * P],
                                          v[:, t, 2 * f * vw:2 * (f + 1) * vw], start=True, stop=True)
                            last.then_inc(u_done, 1)

                        def scores(t):
                            if t >= 2:
                                pe.wait_ge(a_done, R(g, z, t - 2))
                            b = (2 + 2 * (t % 2)) * BANK
                            if g == G_C:
                                for f, a in HEADS:
                                    row = z * 32 + 2 * f + a
                                    c = b + a * BANK + GW + f * P
                                    mm(ps[:, c:c + P], ident[:, row:row + 1].to_broadcast([P, P]),
                                       GY[:, t * P:(t + 1) * P], start=True, stop=True)
                            for f, a in HEADS:
                                rows = slice(a * HD, (a + 1) * HD)
                                c = b + a * BANK + f * P
                                last = mm(ps[:, c:c + P], k2[rows, f, t * P:(t + 1) * P],
                                          q2[rows, f, t * P:(t + 1) * P], start=True, stop=True)
                            last.then_inc(p_done, 1)

                        def output(t):
                            pe.wait_ge(a_done, R(g, z, t))
                            if t == 1:
                                pe.wait_ge(s_ready, Z(g, z))
                            if t >= 2:
                                pe.wait_ge(ot_done, R(g, z, t - 2))
                            o = (6 + t % 2) * BANK
                            own = t == 0 or g == G_C
                            for h, (f, a) in enumerate(HEADS):
                                last = mm(ps[:, o + h * vw:o + (h + 1) * vw], Asb[t % 2][:, a, f, :],
                                          v[:, t, h * vw:(h + 1) * vw], start=h == 0, stop=own,
                                          skip_group_check=True)
                            if t:
                                for f in range(2):
                                    c = o + f * P if g != G_C else (t % 2) * BANK + f * SW
                                    s = (Tst if g == G_A else Sin)[:, t, f, 0:2 * vw]
                                    last = mm(ps[:, c:c + 2 * vw], qi[:, f, t * P:(t + 1) * P], s,
                                              start=g == G_C and f == 0, stop=True, skip_group_check=True)
                            last.then_inc(o_done, 1)

                        scores(0)
                        for t in range(NT):
                            if t + 1 < NT:
                                scores(t + 1)
                            output(t)

                    def concat(c):
                        pe.wait_ge(fin_ready, c)
                        for f in range(2):
                            for t in range(NT):
                                last = tr((f * NT + t) * P, OT[:, t, f * P:(f + 1) * P])
                        last.then_inc(cat_t, 1)
                        pe.wait_ge(cat_done, c)

                    mod(0)
                    mod(1)
                    mod_turn(0, 0)
                    with pe.Fori(0, MOD_U // 2 - 1) as i:
                        for u in range(2):
                            mod(2 + u, i)
                            mod_turn(1 + u, 1 + u, i * 2)
                    mod_turn(MOD_U - 1, MOD_U - 1)
                    sums(0, U_FFN[0], lambda: mod(U_FFN[0]))
                    ffn(0, 0)
                    sums(1, U_GATES)
                    sums(2, U_GATES)
                    gates()

                    features(U_C)
                    features(U_C + 1)
                    tokens(U_C + 2)
                    tokens(U_C + 3)
                    pe.wait_ge(unit_evac, EV(U_C + 3))
                    pe.wait_ge(gate_exp, 1)
                    for t in range(NT):
                        for a, rows in enumerate((GX, GF, GM, GK)):
                            tr((t * 4 + a) * 64, rows[0:64, t * P:(t + 1) * P], 64)
                    for t in range(NT):
                        for f in range(2):
                            tr(4 * BANK + (t * 2 + f) * P, FM[:, 2 + f, t * P:(t + 1) * P])
                    for z in range(2):
                        for f in range(2):
                            c = 7 * BANK + (z * 2 + f) * NT
                            for a in range(2):
                                row = z * 32 + 2 * f + a
                                last = mm(ps[a * HD:(a + 1) * HD, c:c + NT],
                                          ident[0:64, row:row + 1].to_broadcast([64, HD]),
                                          small[0:64, 16:16 + NT], start=True, stop=True)
                    last.then_inc(gate_t, 1)
                    for z in range(2):
                        pe.wait_ge(kt_ready, z + 1)
                        if z:
                            pe.wait_ge(ot_done, R(G_C, 0, NT - 1))
                        scan_group(G_C, z, FM[:, 2:4, :], FM[:, 0:2, :], FM[:, 0:2, :], tiles(ktC, NT),
                                   Vc.rearrange("p t h w -> p t (h w)"), HD + 1)
                    pe.wait_ge(ot_done, R(G_C, 1, NT - 1))
                    concat(1)

                    features(U_A)
                    features(U_A + 1)
                    tokens(U_A + 2)
                    tokens(U_A + 3)
                    pe.wait_ge(unit_evac, EV(U_A + 3))
                    pe.wait_ge(wa2_loaded, 16)
                    for z in range(2):
                        if z:
                            pe.wait_ge(ot_done, R(G_A, 0, NT - 1))
                        for f in range(2):
                            for a in range(2):
                                c = (2 * f + a) * BANK
                                last = mm(ps[:, c:c + HALF], wa2[64:96, (2 * z + f) * P:(2 * z + f + 1) * P],
                                          GX[64:96, a * HALF:(a + 1) * HALF], start=True, stop=True)
                        last.then_inc(apre_done, 1)
                        pe.wait_ge(aqk_ready, z + 1)
                        for t in range(NT):
                            for f in range(2):
                                last = tr((t * 2 + f) * P, KM[:, f, t * P:(t + 1) * P])
                        last.then_inc(akt_done, 1)
                        pe.wait_ge(akt_ready, z + 1)
                        scan_group(G_A, z, KM, QM, QM, tiles(Bk, NT), tiles(Va, NT), HD)
                    pe.wait_ge(ot_done, R(G_A, 1, NT - 1))
                    concat(2)

                    for q in range(4):
                        tokens(U_D + q)
                    pe.wait_ge(unit_evac, EV(U_D + 3))
                    pe.wait_ge(rot_ready, 1)
                    for t in range(NT):
                        if t >= 2:
                            pe.wait_ge(rt_evac, t - 1)
                        for f in range(4):
                            last = tr((t % 2) * BANK + f * P, RQK[:, t, f * P:(f + 1) * P])
                        last.then_inc(rt_done, 1)
                    pe.wait_ge(rt_evac, NT)
                    for z in range(2):
                        pe.wait_ge(kt_ready, 2 + z + 1)
                        if z:
                            pe.wait_ge(ot_done, R(G_D, 0, NT - 1))
                        scan_group(G_D, z, FM[:, 2:4, :], FM[:, 0:2, :], QD, tiles(ktD, NT), tiles(Vd, NT), HD)
                    pe.wait_ge(ot_done, R(G_D, 1, NT - 1))
                    concat(3)

                    features(U_B)
                    features(U_B + 1)
                    tokens(U_B + 2)
                    pe.wait_ge(unit_evac, EV(U_B + 2))
                    kc = tiles(W("kc"), 2)
                    vc = W("vc")
                    vb = tiles(Va, NT)

                    def na_scores(b):
                        t, h = b // NH, b % NH
                        f, a = HEADS[h]
                        if b >= 2:
                            pe.wait_ge(na_read, b - 1)
                        rows = slice(a * HD, (a + 1) * HD)
                        c = a * 2 * BANK
                        q = FM[rows, f, t * P:(t + 1) * P]
                        if t == 0:
                            last = mm(ps[:, c:c + P], q, FM[rows, 2 + f, 0:P], start=True, stop=True)
                        else:
                            mm(ps[:, c:c + DEC], q, FM[rows, 2 + f, P:NTOK], start=True, stop=True)
                            last = mm(ps[:, c + BANK:c + BANK + P], q, kc[rows, f, :], start=True, stop=True)
                        last.then_inc(na_s, 1)

                    def na_turn(b):
                        pe.wait_ge(na_e, b + 1)
                        if b:
                            pe.wait_ge(na_ptc, b)
                        for j in range(1 if b < NH else NT):
                            last = tr(4 * BANK + j * P, SB[b % 2][:, j * P:(j + 1) * P])
                        last.then_inc(na_pt, 1)

                    def na_values(b):
                        t, h = b // NH, b % NH
                        n = 1 if t == 0 else NT
                        pe.wait_ge(na_ptc, b + 1)
                        if b >= 2:
                            pe.wait_ge(na_oc, b - 1)
                        o = (6 + b % 2) * BANK
                        for j in range(n):
                            v = vb[:, 0, :] if t == 0 else vb[:, 1 + j, :] if j < NT - 1 else vc
                            last = mm(ps[:, o:o + HD], PT[:, j * P:(j + 1) * P], v[:, h * HD:(h + 1) * HD],
                                      start=j == 0, stop=j == n - 1)
                        last.then_inc(na_o, 1)

                    na_scores(0)
                    na_scores(1)
                    for b in range(NT * NH):
                        na_turn(b)
                        if b + 2 < NT * NH:
                            na_scores(b + 2)
                        na_values(b)
                    pe.wait_ge(na_oc, NT * NH)
                    concat(4)

                    pe.wait_ge(cat_split, KT)
                    for q in range(4):
                        features(U_OUT + q)
                    sums(3, U_FFN[2])
                    sums(4, U_FFN[2])
                    ffn(2, 1)
                    sums(5, U_ALL)

                @block.scalar
                def _(act):
                    def fn(out, in_, f, **kw):
                        return act.activation(out, in_, f, **kw)

                    def ln_exp():
                        act.preload_act_table_set("natural_log_exp_and_others")

                    def norm(v, n0, per):
                        for k in range(KT):
                            if v % 2 == 0:
                                if v:
                                    act.wait_ge(x_ready, KT * (v // 2 - 1) + k + 1)
                                last = fn(yT[:, k, :], xT[:, k, :], ACT.Square)
                            else:
                                act.wait_ge(unit_evac, EV(n0 + k // per))
                                if k:
                                    act.wait_ge(acc_add, KT * (v // 2) + k)
                                last = fn(sqb, yT[:, k, :], ACT.Square)
                            last.then_inc(sq_ready, 1)
                            if v % 2:
                                act.drain()
                                if k == 0:
                                    act.wait_ge(mod_ready, v // 2 + 1)
                                for c, cols in enumerate((slice(0, SEQ), slice(SEQ, NTOK))):
                                    last = fn(yT[:, k, cols], yT[:, k, cols], ACT.Copy,
                                              scale=gg_all[:, v // 2, k, c:c + 1])
                                last.then_inc(y_scaled, 1)
                        ln_exp()
                        act.wait_ge(ss_done, v + 1)
                        fn(halves(rstd[:, :]), acc(2 * BANK), ACT.Ln, scale=1.0 / DM, bias=eps)
                        act.drain()
                        fn(rstd[:, :], rstd[:, :], ACT.Exp, scale=-0.5).then_inc(rstd_ready, 1)

                    def modulate(s):
                        for k in range(KT):
                            act.wait_ge(hmul_ready, KT * s + k + 1)
                            for c, cols in enumerate((slice(0, SEQ), slice(SEQ, NTOK))):
                                last = fn(h2[:, 0, k, cols], yT[:, k, cols], ACT.Identity,
                                          bias=modS[:, 3 * KT * s + k, c:c + 1])
                            last.then_inc(h_hi, 1)

                    def ffn(s, j):
                        def one(n, i2, f, count, per):
                            act.wait_ge(a_lo, i2 * per + (count + 1))
                            act.wait_ge(unit_done, i2 * 2 + UD(n))
                            fn(halves(rstd[:, :]), acc(half(n)), ACT.Silu).then_inc(silu_done, 1)
                            act.wait_ge(unit_evac, i2 * 2 + EV(n))
                            fn(f, rstd[:, :], ACT.Copy).then_inc(a_hi, 1)

                        act.preload_act_table_set("silu_and_others")
                        if s:
                            act.wait_ge(na_out, 32)
                            act.wait_ge(st_out, 6 * 16)
                            act.wait_ge(m_out, 16)
                        for grp in range(2):
                            n = U_FFN[s] + grp * GRP_U[s]
                            c = j * FT + grp * GF_T
                            hi = a2[:, 0].rearrange("p k n -> p (k n)")
                            if s == 0:
                                with act.Fori(0, GF_T) as i:
                                    one(n + 1, i, hi[:, bass.ds(i * NTOK, NTOK)], c, 1)
                            else:
                                with act.Fori(0, GF_T // 2) as i:
                                    for u in range(2):
                                        one(n + u, i, hi[:, bass.ds(i * (2 * NTOK) + u * NTOK, NTOK)], c + u, 2)
                                one(n + GF_T - 1, 0, a2[:, 0, GF_T - 1, :], c + GF_T - 1, 0)

                    def three(dst, base):
                        for a in (0, 512, 1024):
                            w = min(512, 1280 - a)
                            last = fn(dst[:, a:a + w], ps[:, base + a:base + a + w], ACT.Copy)
                        return last

                    def softplus(buf, n):
                        act.drain()
                        fn(buf, buf, ACT.Exp, scale=-1.0)
                        act.drain()
                        return fn(buf, buf, ACT.Ln, bias=1.0)

                    def head_rstd(c):
                        ln_exp()
                        act.wait_ge(nrm_in, c)
                        fn(small[:, 64:84], small[:, 64:84], ACT.Ln, scale=1.0 / HD, bias=eps)
                        act.drain()
                        fn(small[:, 64:84], small[:, 64:84], ACT.Exp, scale=-0.5).then_inc(nrm_out, 1)

                    def concat(c):
                        act.wait_ge(cat_t, c)
                        three(catP[c - 1].rearrange("p k n -> p (k n)"), 0).then_inc(cat_done, 1)

                    def state_in(g, z):
                        w = SW if g == G_C else P
                        if Z(g, z) > 1:
                            act.wait_ge(o_done, R(g, z, -1))
                        src = I["st_c"][l, z] if g == G_C else I["st_ad"][l, 0 if g == G_A else 1, z]
                        act.dma_start(Sin[:, order(z)[0], :, 0:w], src).then_inc(init_loaded, 16)

                    def state_out(g, z):
                        w = SW if g == G_C else P
                        act.wait_ge(t_done, R(g, z, 0))
                        act.dma_start((O["mc"], O["gla"], O["ret"])[g][l, z], Tst[:, 0, :, 0:w]).then_inc(st_out, 16)

                    eps = small[:, 255:256]

                    norm(0, 0, 1)
                    modulate(0)
                    ffn(0, 0)
                    norm(1, U_GATES - KT, 1)
                    norm(2, 0, 1)
                    modulate(1)

                    ln_exp()
                    act.wait_ge(gate_pre, 1)
                    fn(GK[0:64, :], GY[0:64, :], ACT.Abs)
                    softplus(GK[0:64, :], 64).then_inc(gate_sp, 1)
                    state_in(G_C, 0)
                    act.wait_ge(gate_log, 1)
                    act.dma_start(O["mm"][l], small[0:64, 0:1]).then_inc(m_out, 16)
                    fn(GF[0:64, :], GF[0:64, :], ACT.Exp)
                    fn(GK[0:64, :], GK[0:64, :], ACT.Exp)
                    fn(small[0:64, 16:21], small[0:64, 16:21], ACT.Exp)
                    fn(GM[0:64, :], GM[0:64, :], ACT.Exp, scale=-1.0).then_inc(gate_exp, 1)
                    act.wait_ge(gate_t, 1)
                    three(area(T0 + 6824, 1280), 0)
                    three(kTok, 4 * BANK)
                    fn(small[:, 24:44], ps[:, 7 * BANK:7 * BANK + 20], ACT.Copy).then_inc(gate_cols, 1)
                    for z in range(2):
                        for t in range(NT):
                            act.wait_ge(wl_done, z * NT + t + 1)
                            fn(WL[t % 2], WL[t % 2], ACT.Exp).then_inc(w_ready, 1)
                            if t == 0:
                                state_out(G_C, z)
                        if z == 0:
                            state_in(G_C, 1)
                    act.wait_ge(unit_evac, EV(U_C + 3))
                    fn(Oc, Oc, ACT.Sigmoid).then_inc(act_gate, 1)
                    concat(1)

                    act.dma_start(wa2[64:96, :], I["wa2"][l]).then_inc(wa2_loaded, 16)
                    ln_exp()
                    for z in range(2):
                        act.wait_ge(apre_done, z + 1)
                        for f in range(2):
                            b = W("ba")[:, 2 * z + f:2 * z + f + 1]
                            fn(halves(Wk[:, f * NTOK:(f + 1) * NTOK]), acc(2 * f * BANK), ACT.Abs, bias=b)
                            fn(halves(QM[:, f, :]), acc(2 * f * BANK), ACT.Identity, bias=b)
                        softplus(Wk, P).then_inc(asp_done, 1)
                        act.wait_ge(ad_ready, z + 1)
                        fn(QM.rearrange("p f n -> p (f n)"), Wk, ACT.Exp, scale=1.0 / TAU)
                        fn(KM.rearrange("p f n -> p (f n)"), Wk, ACT.Exp, scale=-1.0 / TAU)
                        fn(small[:, 96:126], small[:, 96:126], ACT.Exp, scale=1.0 / TAU).then_inc(ae_ready, 1)
                        act.wait_ge(akt_done, z + 1)
                        three(Bk, 0).then_inc(akt_ready, 1)
                        state_in(G_A, z)
                        state_out(G_A, z)
                    act.wait_ge(unit_evac, EV(U_A + 3))
                    head_rstd(1)
                    fn(Ga, Ga, ACT.Silu).then_inc(act_gate, 1)
                    concat(2)

                    ln_exp()
                    act.wait_ge(par_loaded, 16)
                    lg = small[:, 128:140]
                    act.wait_ge(lg_ready, 1)
                    fn(small[:, 144:156], W("rd"), ACT.Abs)
                    softplus(small[:, 144:156], P).then_inc(lg_sp, 1)
                    act.wait_ge(lg_ready, 2)
                    diff = C("diff").rearrange("p (z i) -> p z i", z=2)
                    prow = C("posrow").rearrange("p (z i) -> p z i", z=2)
                    for z in range(2):
                        for h, (f, a) in enumerate(HEADS):
                            fn(Dm[:, z, a, f, :], diff[:, z, :], ACT.Exp, scale=lg[:, 4 * z + h:4 * z + h + 1])
                        for f in range(2):
                            fn(qdec[:, z, f, :], prow[:, z, :], ACT.Exp, scale=lg[:, 8 + 2 * z + f:9 + 2 * z + f])
                    fn(small[:, 160:168], small[:, 160:168], ACT.Exp)
                    fn(small[:, 168:172], lg[:, 8:12], ACT.Exp, scale=float(P)).then_inc(dec_ready, 1)
                    for t in range(NT):
                        act.wait_ge(rt_done, t + 1)
                        b = (t % 2) * BANK
                        fn(FM[:, :, t * P:(t + 1) * P], tiles(ps[:, b:b + BANK], 4), ACT.Copy).then_inc(rt_evac, 1)
                    for z in range(2):
                        state_in(G_D, z)
                        state_out(G_D, z)
                    act.wait_ge(unit_evac, EV(U_D + 3))
                    head_rstd(2)
                    fn(Gd, Gd, ACT.Silu).then_inc(act_gate, 1)
                    concat(3)

                    act.dma_start(rpb, I["rpb"][l]).then_inc(rpb_loaded, 16)
                    act.wait_ge(unit_evac, EV(U_B + 2))
                    act.dma_start(O["nak"][l], FM[:, 2:4, 0:P]).then_inc(na_out, 16)
                    act.dma_start(O["nav"][l], Va[:, 0:GW]).then_inc(na_out, 16)
                    ln_exp()

                    def probs(b):
                        n = P if b < NH else NTOK
                        act.wait_ge(na_max, b + 1)
                        fn(SB[b % 2][:, 0:n], SB[b % 2][:, 0:n], ACT.Exp, bias=small[:, 176 + b:177 + b],
                           accum_out=small[:, 200 + b:201 + b]).then_inc(na_e, 1)

                    def turned(b):
                        n = P if b < NH else NTOK
                        act.wait_ge(na_pt, b + 1)
                        if b:
                            act.wait_ge(na_o, b)
                        for a in range(0, n, BANK):
                            w = min(BANK, n - a)
                            last = fn(PT[:, a:a + w], ps[:, 4 * BANK + a:4 * BANK + a + w], ACT.Copy)
                        last.then_inc(na_ptc, 1)

                    probs(0)
                    for b in range(NT * NH):
                        if b + 1 < NT * NH:
                            probs(b + 1)
                        turned(b)
                    concat(4)
                    act.wait_ge(cat_done, 4)
                    for c in range(4):
                        for f in range(2):
                            fn(h2[:, 0, CAT_K[c] + f, :], catP[c][:, f, :], ACT.Copy).then_inc(cat_hi, 1)

                    norm(3, U_OUT, 2)
                    norm(4, 0, 1)
                    modulate(2)
                    ffn(2, 1)
                    norm(5, U_ALL - KT, 1)

                @block.vector
                def _(dve):
                    V = nc.vector
                    dve.sem_inc(unit_evac, 2)
                    dve.sem_inc(a_lo, 1)
                    V.memset(small[:, 0:255], 0.0)
                    V.memset(small[:, 255:256], EPS)
                    dve.wait_ge(par_loaded, 16)
                    bmod = W("bmod")
                    normw = tiles(W("normw"), 6)

                    def mod_rows(n, i2):
                        dve.wait_ge(unit_done, i2 * 2 + UD(n))
                        V.tensor_copy(mrow[0:2, :], ps[0:2, half(n):half(n) + 256]).then_inc(mrow_ready, 1)

                    def mod_cols(n, q, i1=0):
                        dve.wait_ge(mtr_done, i1 + (q + 1))
                        m = i1 * 2 + 2 * q
                        V.tensor_tensor(modS[:, bass.ds(m, 2), :], tiles(ps[:, half(n) + BANK:half(n) + BANK + 4], 2),
                                        par[:, bass.ds(m + PARAMS["bmod"][0], 2)]
                                        .unsqueeze(2).to_broadcast([P, 2, 2]), ALU.add).then_inc(unit_evac, 1)

                    def mod_scales(s):
                        m0 = 3 * KT * s
                        g = lambda i: normw[:, i, :].unsqueeze(2).to_broadcast([P, KT, 2])
                        V.scalar_tensor_tensor(gg_all[:, s], modS[:, m0 + 2 * KT:m0 + 3 * KT, :],
                                               1.0 if s == 1 else 0.5, g(2 * s + 1), ALU.mult, ALU.mult)
                        V.scalar_tensor_tensor(gs_all[:, s], modS[:, m0 + KT:m0 + 2 * KT, :], 1.0, g(2 * s),
                                               ALU.add, ALU.mult).then_inc(mod_ready, 1)

                    def add_square(v, k, i=0):
                        dve.wait_ge(sq_ready, i * 2 + (KT * (2 * v + 1) + k + 1))
                        if k == 0:
                            last = V.tensor_copy(rstd[:, :], sqb)
                        else:
                            dve.wait_ge(acc_add, i * 2 + (KT * v + k))
                            last = V.tensor_tensor(rstd[:, :], rstd[:, :], sqb, ALU.add)
                        last.then_inc(acc_add, 1)

                    def norm_in(s):
                        dve.wait_ge(mod_ready, s + 1)
                        dve.wait_ge(rstd_ready, 2 * s + 1)
                        parts = tuple(enumerate((slice(0, SEQ), slice(SEQ, NTOK))))
                        for k in range(KT + 1):
                            if k < KT:
                                for c, cols in parts:
                                    last = V.scalar_tensor_tensor(yT[:, k, cols], xT[:, k, cols],
                                                                  gs_all[:, s, k, c:c + 1], rstd[:, cols],
                                                                  ALU.mult, ALU.mult)
                                last.then_inc(hmul_ready, 1)
                            if k:
                                m = k - 1
                                dve.wait_ge(h_hi, KT * s + m + 1)
                                for c, cols in parts:
                                    last = V.scalar_tensor_tensor(h2[:, 1, m, cols], yT[:, m, cols],
                                                                  modS[:, 3 * KT * s + m, c:c + 1],
                                                                  h2[:, 0, m, cols].bitcast(FP), ALU.add, ALU.subtract)
                                last.then_inc(h_ready, 1)

                    def norm_out(s):
                        dve.wait_ge(rstd_ready, 2 * s + 2)
                        for k in range(KT + 1):
                            if k < KT:
                                dve.wait_ge(y_scaled, KT * s + k + 1)
                                V.tensor_tensor(yT[:, k, :], yT[:, k, :], rstd[:, :], ALU.mult).then_inc(y_norm, 1)
                            if k:
                                dve.wait_ge(y_norm, KT * s + k)
                                V.tensor_tensor(xT[:, k - 1, :], xT[:, k - 1, :], yT[:, k - 1, :], ALU.add)\
                                    .then_inc(x_ready, 1)

                    def ffn(s, j):
                        lo, hi = (a2[:, p].rearrange("p k n -> p (k n)") for p in (1, 0))

                        def one(n, i2, at, count, per):
                            dve.wait_ge(silu_done, i2 * per + (count + 1))
                            V.tensor_tensor(halves(rstd[:, :]), halves(rstd[:, :]), acc(half(n) + 2 * BANK), ALU.mult)\
                                .then_inc(unit_evac, 1)
                            dve.wait_ge(a_hi, i2 * per + (count + 1))
                            V.tensor_tensor(lo[:, at], rstd[:, :], hi[:, at].bitcast(FP), ALU.subtract)\
                                .then_inc(a_lo, 1)

                        def down(n, i2, dst, grp):
                            dve.wait_ge(unit_done, i2 * 2 + UD(n))
                            dst = dst.rearrange("p (a n) -> p a n", a=2)
                            if grp == 0:
                                last = V.tensor_copy(dst, acc(half(n)))
                            else:
                                last = V.tensor_tensor(dst, dst, acc(half(n)), ALU.add)
                            last.then_inc(unit_evac, 1)

                        y0 = ARENA_W - KT * NTOK
                        for grp in range(2):
                            n = U_FFN[s] + grp * GRP_U[s]
                            c = j * FT + grp * GF_T
                            q = MOD_U * (1 + grp)
                            if s == 0:
                                mod_rows(n, 0)
                                with dve.Fori(0, GF_T) as i:
                                    mod_cols(n, q, i)
                                    one(n + 1, i, bass.ds(i * NTOK, NTOK), c, 1)
                                    mod_rows(n + 2, i)
                                mod_cols(n + 2 * GF_T, q + GF_T)
                                n += GF_T + MOD_U
                            else:
                                with dve.Fori(0, GF_T // 2) as i:
                                    for u in range(2):
                                        one(n + u, i, bass.ds(i * (2 * NTOK) + u * NTOK, NTOK), c + u, 2)
                                one(n + GF_T - 1, 0, slice((GF_T - 1) * NTOK, GF_T * NTOK), c + GF_T - 1, 0)
                                n += GF_T
                            for u in range(2):
                                down(n + u, 0, yT[:, u, :], grp)
                            if grp:
                                add_square(s, 0)
                            with dve.Fori(0, KT // 2 - 1) as i:
                                for u in range(2):
                                    down(n + 2 + u, i, arena[:, bass.ds(i * (2 * NTOK) + (y0 + (2 + u) * NTOK), NTOK)],
                                         grp)
                                    if grp:
                                        add_square(s, 1 + u, i)
                        add_square(s, KT - 1)

                    def evac_features(n, dst, scale=None):
                        dve.wait_ge(unit_done, UD(n))
                        src = ps[:, half(n):half(n) + 4 * BANK].rearrange("p (a n) -> p a n", a=4)[:, :, 0:HALF]
                        dst = dst.rearrange("p k n -> p (k n)").rearrange("p (a n) -> p a n", a=4)
                        if scale is None:
                            last = V.tensor_copy(dst, src)
                        else:
                            last = V.tensor_scalar(dst, src, scale, None, ALU.mult)
                        last.then_inc(unit_evac, 1)

                    def evac_tokens(n, dst, scale=1.0):
                        dve.wait_ge(unit_done, UD(n))
                        src = ps[:, half(n):half(n) + NT * GW]
                        if len(dst.shape) == 4:
                            src = src.rearrange("p (t h e) -> p t h e", t=NT, h=NH)
                        else:
                            src = tiles(src, NT)
                        V.tensor_scalar(dst, src, scale, None, ALU.mult).then_inc(unit_evac, 1)

                    def scan_group(g, z, bmask, decay):
                        w = SW if g == G_C else P
                        if Z(g, z) > 1:
                            dve.wait_ge(st_out, 16 * (Z(g, z) - 1))
                        for t in range(NT):
                            dve.wait_ge(u_done, R(g, z, t))
                            u = tiles(ps[:, (t % 2) * BANK:(t % 2) * BANK + 2 * w], 2)
                            if g == G_A:
                                for f in range(2):
                                    last = V.scalar_tensor_tensor(Tst[:, t, f, 0:w], u[:, f, :],
                                                                  small[:, 106 + f * NT + t:107 + f * NT + t],
                                                                  bmask, ALU.mult, ALU.mult)
                            else:
                                last = V.tensor_tensor(Tst[:, t, :, 0:w], u,
                                                       bmask.unsqueeze(1).to_broadcast([P, 2, w]), ALU.mult)
                            last.then_inc(t_done, 1)
                        o = order(z)
                        for a, b in zip(o[:-1], o[1:]):
                            dve.drain()
                            if a == o[0]:
                                dve.wait_ge(init_loaded, 16 * Z(g, z))
                            for f in range(2):
                                last = V.scalar_tensor_tensor(Sin[:, b, f, 0:w], Sin[:, a, f, 0:w], decay(f, a),
                                                              Tst[:, a, f, 0:w], ALU.mult, ALU.add)
                        if g == G_A:
                            dve.drain()
                            for f in range(2):
                                last = V.tensor_tensor(Tst[:, 1:NT, f, 0:w], Sin[:, 1:NT, f, 0:w],
                                                       small[:, 117 + f * NT:121 + f * NT].unsqueeze(2)
                                                       .to_broadcast([P, NT - 1, w]), ALU.mult)
                        last.then_inc(s_ready, 1)

                        def attention(t):
                            dve.wait_ge(p_done, R(g, z, t))
                            b = (2 + 2 * (t % 2)) * BANK
                            both = ps[:, b:b + 2 * BANK].rearrange("p (a q f i) -> p a q f i", a=2, q=2, f=2)
                            pr, lw = both[:, :, 0, :, :], both[:, :, 1, :, :]
                            if t >= 2:
                                dve.wait_ge(o_done, R(g, z, t - 2))
                            elif Z(g, z) > 1:
                                dve.wait_ge(o_done, R(g, z, -1))
                            if g == G_C:
                                for f, a in HEADS:
                                    last = V.scalar_tensor_tensor(
                                        WL[t % 2][:, a, f, :], lw[:, a, f, :],
                                        GT[:, t, 0, z * 32 + 2 * f + a:z * 32 + 2 * f + a + 1],
                                        anti[:, z, :], ALU.add, ALU.add)
                                last.then_inc(wl_done, 1)
                                if t:
                                    output(t - 1)
                                dve.wait_ge(w_ready, z * NT + t + 1)
                                m = WL[t % 2]
                            elif g == G_A:
                                m = causal[:, z, :].unsqueeze(1).unsqueeze(1).to_broadcast([P, 2, 2, P])
                            else:
                                m = Dm[:, z]
                            V.tensor_tensor(Asb[t % 2], pr, m, ALU.mult).then_inc(a_done, 1)

                        def output(t):
                            dve.wait_ge(o_done, R(g, z, t))
                            o = (6 + t % 2) * BANK
                            if g == G_C:
                                out = tiles(ps[:, o:o + 2 * SW], NH)
                                if t == 0:
                                    V.tensor_copy(CT[:, t], out).then_inc(ot_done, 1)
                                else:
                                    inter = tiles(ps[:, (t % 2) * BANK:(t % 2) * BANK + 2 * SW], NH)
                                    V.tensor_tensor(CT[:, t], inter,
                                                    GT[:, t, 1, z * 32:z * 32 + NH].unsqueeze(2)
                                                    .to_broadcast([P, NH, HD + 1]), ALU.mult)
                                    dve.drain()
                                    V.tensor_tensor(CT[:, t], CT[:, t], out, ALU.add).then_inc(ot_done, 1)
                            elif z == 0:
                                V.tensor_copy(OT[:, t, :], ps[:, o:o + GW]).then_inc(ot_done, 1)
                            else:
                                V.tensor_tensor(OT[:, t, :], OT[:, t, :], ps[:, o:o + GW], ALU.add)\
                                    .then_inc(ot_done, 1)

                        for t in range(NT):
                            attention(t)
                            if t and g != G_C:
                                output(t - 1)
                        output(NT - 1)

                    def head_norm(c, w, gate, centred):
                        heads = [P, NT * NH, HD]
                        sq = Tq
                        dve.drain()
                        if centred:
                            V.reduce_sum(small[:, 64:84], OTh, axis=AXX)
                            dve.drain()
                            V.tensor_scalar(small[:, 64:84], small[:, 64:84], 1.0 / HD, None, ALU.mult)
                            dve.drain()
                            V.tensor_tensor(OTh, OTh, small[:, 64:84].unsqueeze(2).to_broadcast(heads), ALU.subtract)
                            dve.drain()
                        dve.wait_ge(st_out, 16 * 2 * (c + 1))
                        V.tensor_tensor(sq, OTh, OTh, ALU.mult)
                        dve.drain()
                        V.reduce_sum(small[:, 64:84], sq, axis=AXX).then_inc(nrm_in, 1)
                        dve.wait_ge(nrm_out, c)
                        V.tensor_tensor(OTh, OTh, small[:, 64:84].unsqueeze(2).to_broadcast(heads), ALU.mult)
                        dve.drain()
                        V.tensor_tensor(OTh, OTh, w.unsqueeze(1).to_broadcast(heads), ALU.mult)
                        dve.drain()
                        dve.wait_ge(act_gate, c + 1)
                        V.tensor_tensor(OTh, OTh, gate.rearrange("p (a e) -> p a e", e=HD), ALU.mult)\
                            .then_inc(fin_ready, 1)

                    Tq = area(T0, 1280).rearrange("p (a e) -> p a e", e=HD)

                    mod_rows(0, 0)
                    with dve.Fori(0, MOD_U // 2 - 1) as i:
                        for u in range(2):
                            mod_cols(u, u, i * 2)
                            mod_rows(1 + u, i)
                    mod_cols(MOD_U - 2, MOD_U - 2)
                    mod_rows(MOD_U - 1, 0)
                    mod_cols(MOD_U - 1, MOD_U - 1)
                    dve.drain()
                    mod_scales(0)
                    norm_in(0)
                    ffn(0, 0)
                    dve.drain()
                    mod_scales(1)
                    mod_scales(2)
                    norm_out(0)
                    norm_in(1)

                    dve.wait_ge(unit_done, UD(U_GATES))
                    b0 = half(U_GATES)
                    gb = W("gb")
                    V.memset(GY[64:128, :], 0.0)
                    V.memset(GM[0:64, :], 0.0)
                    V.memset(GF[0:64, :], 0.0)
                    V.tensor_scalar(halves(GX[0:96, :]), acc(b0)[0:96], gb[0:96, 0:1], None, ALU.add)
                    V.tensor_scalar(halves(GY[0:64, :]), acc(b0 + 2 * BANK)[0:64], gb[0:64, 1:2], None, ALU.add)\
                        .then_inc(unit_evac, 1)
                    dve.drain()
                    dve.sem_inc(gate_pre, 1)
                    V.memset(area(TM0, 1300), 1.0)
                    evac_features(U_C, FM[:, 0:2, :], QSCALE)
                    evac_features(U_C + 1, FM[:, 2:4, :])
                    evac_tokens(U_C + 2, Vc[:, :, :, 0:HD])
                    evac_tokens(U_C + 3, tiles(Oc, NT))
                    dve.wait_ge(gate_sp, 1)
                    V.tensor_scalar(GY[0:64, :], GY[0:64, :], 0.0, None, ALU.min)
                    dve.drain()
                    V.tensor_tensor(GY[0:64, :], GY[0:64, :], GK[0:64, :], ALU.subtract)
                    dve.drain()
                    m0 = W("m0")
                    carry = C("carry")
                    for z, rows in enumerate((slice(0, NH), slice(32, 32 + NH))):
                        for cols, init in (((0, SEQ), 0.0), ((SEQ, NTOK), m0[rows, :])):
                            s = slice(*cols) if z == 0 else slice(cols[1] - 1, cols[0] - 1 if cols[0] else None, -1)
                            V.tensor_tensor_scan(out=GM[rows, s], data0=GY[rows, s], data1=GX[rows, s], initial=init,
                                                 op0=ALU.add, op1=ALU.max)
                        s = slice(None) if z == 0 else slice(None, None, -1)
                        V.tensor_tensor_scan(out=GF[rows, s], data0=carry[rows, :], data1=GY[rows, s], initial=0.0,
                                             op0=ALU.mult, op1=ALU.add)
                    dve.drain()
                    mlast, mprev, rlast, wprev = (small[0:64, a:a + NT] for a in (0, 5, 10, 16))
                    r0, r1 = slice(0, NH), slice(32, 32 + NH)
                    V.tensor_copy(mlast[r0], GM[r0, P - 1::P])
                    V.tensor_copy(small[32:36, 0:NT], GM[r1, 0::P])
                    V.tensor_copy(small[r0, 6:7], m0[r0])
                    V.tensor_copy(small[r1, 9:10], m0[r1])
                    V.tensor_copy(small[r0, 7:10], GM[r0, 2 * P - 1:4 * P:P])
                    V.tensor_copy(small[r1, 6:9], GM[r1, 2 * P:4 * P + 1:P])
                    V.tensor_tensor(GY[0:64, :], GF[0:64, :], GM[0:64, :], ALU.subtract)
                    V.tensor_tensor(GX[0:64, :], GX[0:64, :], GF[0:64, :], ALU.subtract)
                    dve.drain()
                    V.tensor_copy(rlast[r0], GY[r0, P - 1::P])
                    V.tensor_copy(small[32:36, 10:10 + NT], GY[r1, 0::P])
                    dve.drain()
                    V.tensor_tensor(tiles(GF[0:64, :], NT), tiles(GY[0:64, :], NT),
                                    mprev.unsqueeze(2).to_broadcast([64, NT, P]), ALU.add)
                    V.tensor_tensor(tiles(GK[0:64, :], NT), tiles(GX[0:64, :], NT),
                                    rlast.unsqueeze(2).to_broadcast([64, NT, P]), ALU.add)
                    V.tensor_tensor(wprev, rlast, mprev, ALU.add).then_inc(gate_log, 1)
                    dve.wait_ge(gate_cols, 1)
                    for z in range(2):
                        if z:
                            dve.wait_ge(u_done, R(G_C, 0, NT - 1))
                        V.tensor_tensor(ktC.rearrange("p (t h e) -> p t h e", t=NT, h=NH),
                                        kTok.rearrange("p (t h e) -> p t h e", t=NT, h=NH),
                                        GT[:, :, 3, z * 32:z * 32 + NH].unsqueeze(3).to_broadcast([P, NT, NH, HD]),
                                        ALU.mult).then_inc(kt_ready, 1)
                        scan_group(G_C, z, C("blockn"),
                                   lambda f, t: small[:, 24 + (2 * z + f) * NT + t:25 + (2 * z + f) * NT + t])
                        dve.drain()
                        den = CT[:, :, :, HD]
                        d = small[:, 44:64]
                        dt = tiles(d, NT)
                        V.scalar_tensor_tensor(dt, den, -1.0, den, ALU.mult, ALU.max)
                        dve.drain()
                        V.tensor_tensor(dt, dt, GT[:, :, 2, z * 32:z * 32 + NH], ALU.max)
                        dve.drain()
                        V.reciprocal(d, d)
                        dve.drain()
                        num, inv = CT[:, :, :, 0:HD], dt.unsqueeze(3).to_broadcast([P, NT, NH, HD])
                        o4 = OT.rearrange("p t (h e) -> p t h e", h=NH)
                        if z == 0:
                            V.tensor_tensor(o4, num, inv, ALU.mult)
                        else:
                            V.tensor_tensor(num, num, inv, ALU.mult)
                            dve.drain()
                            V.tensor_tensor(o4, o4, num, ALU.add)
                        dve.drain()
                    dve.wait_ge(act_gate, 1)
                    V.tensor_tensor(OT, OT, tiles(Oc, NT), ALU.mult).then_inc(fin_ready, 1)

                    evac_features(U_A, FM[:, 0:2, :], QSCALE)
                    evac_features(U_A + 1, FM[:, 2:4, :])
                    evac_tokens(U_A + 2, tiles(Va, NT))
                    evac_tokens(U_A + 3, tiles(Ga, NT))
                    for z in range(2):
                        dve.wait_ge(asp_done, z + 1)
                        V.scalar_tensor_tensor(Wk, QM.rearrange("p f n -> p (f n)"), 0.0, Wk, ALU.min, ALU.subtract)
                        dve.drain()
                        s = slice(None) if z == 0 else slice(None, None, -1)
                        for f in range(2):
                            V.tensor_tensor_scan(out=tiles(Bk, 2)[:, f, s], data0=carry, data1=tiles(Wk, 2)[:, f, s],
                                                 initial=0.0, op0=ALU.mult, op1=ALU.add)
                        dve.drain()
                        b3 = tiles(Bk, 2 * NT)
                        mid, end = (b3[:, :, 63], b3[:, :, P - 1]) if z == 0 else (b3[:, :, 64], b3[:, :, 0])
                        V.tensor_tensor(tiles(Wk, 2 * NT), b3, mid.unsqueeze(2).to_broadcast([P, 2 * NT, P]),
                                        ALU.subtract)
                        V.tensor_copy(small[:, 96:106], end)
                        V.tensor_tensor(small[:, 106:116], end, mid, ALU.subtract)
                        V.tensor_copy(small[:, 116:126], mid).then_inc(ad_ready, 1)
                        dve.wait_ge(ae_ready, z + 1)
                        V.tensor_tensor(QM, QM, FM[:, 0:2, :], ALU.mult)
                        V.tensor_tensor(KM, KM, FM[:, 2:4, :], ALU.mult).then_inc(aqk_ready, 1)
                        scan_group(G_A, z, C("block"),
                                   lambda f, t: small[:, 96 + f * NT + t:97 + f * NT + t])
                    head_norm(1, W("gnw"), Ga, False)

                    dve.sem_inc(lg_ready, 1)
                    evac_tokens(U_D, RQK[:, :, 0:GW], QSCALE)
                    evac_tokens(U_D + 1, RQK[:, :, GW:2 * GW])
                    evac_tokens(U_D + 2, tiles(Vd, NT))
                    evac_tokens(U_D + 3, tiles(Gd, NT))
                    dve.drain()
                    rope = C("rope").rearrange("p (t s e) -> p t s e", t=NT, s=2)
                    for t in range(NT):
                        x8 = tiles(RQK[:, t, :], 2 * NH)
                        V.tensor_tensor(tiles(rot1[:, t, :], 2 * NH), x8,
                                        rope[:, t, 0, :].unsqueeze(1).to_broadcast([P, 2 * NH, HD]), ALU.mult)
                        x5 = RQK[:, t, :].rearrange("p (h a b e) -> p h a b e", h=2 * NH, a=2, b=2)
                        r5 = rot2[:, t, :].rearrange("p (h a b e) -> p h a b e", h=2 * NH, a=2, b=2)
                        s5 = rope[:, t, 1, :].rearrange("p (a b e) -> p a b e", a=2, b=2)
                        for b in range(2):
                            V.tensor_tensor(r5[:, :, :, b, :], x5[:, :, :, 1 - b, :],
                                            s5[:, :, b, :].unsqueeze(1).to_broadcast([P, 2 * NH, 2, 16]), ALU.mult)
                    dve.drain()
                    V.tensor_tensor(RQK, rot1, rot2, ALU.add).then_inc(rot_ready, 1)
                    dve.wait_ge(lg_sp, 1)
                    lg = small[:, 128:140]
                    V.tensor_scalar(lg, W("rd"), 0.0, None, ALU.min)
                    dve.drain()
                    V.tensor_tensor(lg, lg, small[:, 144:156], ALU.subtract)
                    dve.drain()
                    pc = C("poscol")
                    for z in range(2):
                        last = V.tensor_scalar(small[:, 160 + 4 * z:164 + 4 * z], lg[:, 4 * z:4 * z + 4],
                                               pc[:, z:z + 1], None, ALU.mult)
                    last.then_inc(lg_ready, 1)
                    dve.wait_ge(dec_ready, 1)
                    dm = Dm.rearrange("p z a f i -> p z (a f) i")
                    V.tensor_tensor(dm, dm, causal.unsqueeze(2).to_broadcast([P, 2, 4, P]), ALU.mult)
                    dve.wait_ge(rt_evac, NT)
                    for z in range(2):
                        if z:
                            dve.wait_ge(o_done, R(G_D, 0, NT - 1))
                        V.tensor_tensor(ktD.rearrange("p (t h e) -> p t h e", t=NT, h=NH),
                                        RQK[:, :, GW:2 * GW].rearrange("p t (h e) -> p t h e", h=NH),
                                        small[:, 160 + 4 * z:164 + 4 * z].unsqueeze(1).unsqueeze(3)
                                        .to_broadcast([P, NT, NH, HD]), ALU.mult)
                        V.tensor_tensor(QD.rearrange("p f (t i) -> p f t i", t=NT),
                                        FM[:, 0:2, :].rearrange("p f (t i) -> p f t i", t=NT),
                                        qdec[:, z].unsqueeze(2).to_broadcast([P, 2, NT, P]), ALU.mult)\
                            .then_inc(kt_ready, 1)
                        scan_group(G_D, z, C("block"), lambda f, t: small[:, 168 + 2 * z + f:169 + 2 * z + f])
                    head_norm(2, W("rnw"), Gd, True)

                    evac_features(U_B, FM[:, 0:2, :], QSCALE)
                    evac_features(U_B + 1, FM[:, 2:4, :])
                    evac_tokens(U_B + 2, tiles(Va, NT))
                    dve.wait_ge(rpb_loaded, 16)
                    r3 = rpb.rearrange("p (m c) -> p m c", c=HD)
                    V.tensor_tensor(r3, r3, C("namask").unsqueeze(1).to_broadcast([P, 14 * NH, HD]), ALU.add)
                    dve.drain()

                    def na_in(b):
                        t, h = b // NH, b % NH
                        c = (h % 2) * 2 * BANK
                        s = SB[b % 2]
                        dve.wait_ge(na_s, b + 1)
                        if b >= 2:
                            dve.wait_ge(na_pt, b - 1)
                        if t == 0:
                            V.tensor_copy(s[:, 0:P], ps[:, c:c + P]).then_inc(na_read, 1)
                            n = P
                        else:
                            m = (h * 14 + 6 - 2 * (t - 1)) * HD
                            V.tensor_tensor(s[:, 0:DEC], ps[:, c:c + DEC], rpb[:, m:m + DEC], ALU.add)
                            V.tensor_copy(s[:, DEC:NTOK], ps[:, c + BANK:c + BANK + P]).then_inc(na_read, 1)
                            n = NTOK
                        dve.drain()
                        V.tensor_reduce(out=small[:, 176 + b:177 + b], in_=s[:, 0:n], op=ALU.max, axis=AXX,
                                        negate=True).then_inc(na_max, 1)

                    def na_outp(b):
                        t, h = b // NH, b % NH
                        dve.wait_ge(na_o, b + 1)
                        V.reciprocal(small[:, 220 + b:221 + b], small[:, 200 + b:201 + b])
                        dve.drain()
                        o = (6 + b % 2) * BANK
                        last = V.tensor_scalar(OT[:, t, h * HD:(h + 1) * HD], ps[:, o:o + HD],
                                               small[:, 220 + b:221 + b], None, ALU.mult)
                        last.then_inc(na_oc, 1)

                    na_in(0)
                    for b in range(NT * NH):
                        if b + 1 < NT * NH:
                            na_in(b + 1)
                        na_outp(b)
                    dve.drain()
                    dve.sem_inc(fin_ready, 1)

                    for c in range(4):
                        for f in range(2):
                            dve.wait_ge(cat_hi, 2 * c + f + 1)
                            k = CAT_K[c] + f
                            V.tensor_tensor(h2[:, 1, k, :], catP[c][:, f, :], h2[:, 0, k, :].bitcast(FP),
                                            ALU.subtract).then_inc(cat_split, 1)
                    for q in range(4):
                        evac_features(U_OUT + q, yT[:, 2 * q:2 * q + 2, :])
                        for k in range(max(0, 2 * q - 2), 2 * q):
                            add_square(1, k)
                    for k in (KT - 2, KT - 1):
                        add_square(1, k)
                    norm_out(1)
                    norm_in(2)
                    ffn(2, 1)
                    norm_out(2)

            nums = sorted(s.num for s in sems)
            assert nums == list(range(nums[0], nums[-1] + 1))
            nc.sync.sem_clear(range(nums[0], nums[-1] + 1))
            nc.all_engine_barrier()

        with nc.Block() as block:
            @block.sync
            def _(sp):
                sp.dma_start(O["y"], xT).then_inc(y_out, 16)
                sp.wait_ge(y_out, 16)


def constants():
    import numpy as np

    c = np.zeros((P, CONST_W), np.float32)

    def put(name, a):
        at, w = CONSTS[name]
        c[:, at:at + w] = np.asarray(a, np.float64).reshape(-1, w)

    i = np.arange(P)
    put("ident", np.eye(P))
    put("ones", np.ones((P, P)))
    tok = np.arange(DEC)
    inv = 10000.0 ** (-np.arange(16, dtype=np.float32) / 16)
    ang = np.stack([(tok // GRID_W)[:, None] * inv, (tok % GRID_W)[:, None] * inv], 1)
    cs = np.concatenate([np.ones((SEQ, 2, 16)), np.cos(ang.astype(np.float32))])
    sn = np.concatenate([np.zeros((SEQ, 2, 16)), np.sin(ang.astype(np.float32))])
    table = np.stack([np.stack([cs, cs], 2), np.stack([-sn, sn], 2)], 1)
    put("rope", table.reshape(NT, P, 2 * HD).transpose(1, 0, 2))
    q, k = np.arange(GRID_W)[:, None], np.arange(GRID_W)[None]
    lo = np.clip(q - WIN // 2, 0, GRID_W - WIN)
    put("namask", np.tile(np.where((k >= lo) & (k < lo + WIN), 0.0, NEG), (2, 1)))
    j = i[:, None]
    causal = np.stack([i[None] >= j, i[None] <= j], 1)
    put("causal", causal)
    put("anti", np.where(causal, 0.0, NEG))
    put("block", (i[:, None] // HD == i[None] // HD))
    put("blockn", (i[:, None] // HD == np.arange(SW)[None] // (HD + 1)))
    put("diff", np.stack([np.maximum(i[None] - j, 0), np.maximum(j - i[None], 0)], 1))
    put("posrow", np.broadcast_to(np.stack([i + 1, P - i]), (P, 2, P)))
    put("poscol", np.stack([P - 1 - i, i], 1))
    put("carry", np.broadcast_to(np.arange(NTOK) % P != 0, (P, NTOK)))
    return c


def lay_out(v):
    import numpy as np

    f = np.float32

    def blocks(w, cols):
        n = w.shape[-1] // cols
        return np.ascontiguousarray(w.reshape(DEPTH, KT, P, n, cols).transpose(0, 3, 2, 1, 4)).reshape(
            DEPTH, n, P, KT * cols)

    d = {"const": constants()}
    x = np.concatenate([v["x_prompt"][0], v["x_sample"][0]])
    d["x"] = np.ascontiguousarray(x.T.reshape(KT, P, NTOK).transpose(1, 0, 2))
    d["cond"] = np.ascontiguousarray(np.stack([v["c_ctx"], v["c"][0]], 1).reshape(KT, P, 2).transpose(1, 0, 2))
    d["w_mod"] = blocks(v["w_mod"], 256)
    w1, w3 = (v[n].reshape(DEPTH, 2, KT, P, FT, P).transpose(0, 1, 4, 3, 2, 5) for n in ("ffn_w1", "ffn_w3"))
    d["w13"] = np.stack([w1, w3], 4).reshape(DEPTH, 2 * FT, P, 2 * DM)
    d["w2"] = np.ascontiguousarray(v["ffn_w2"].reshape(DEPTH, 2, 2, GF_T, P, KT, P).transpose(
        0, 1, 2, 5, 4, 3, 6)).reshape(DEPTH, 4 * KT, P, GF_T * P)
    names = ["gq", "gk", "gv", "gg", "ga", "nq", "nk", "nv", "mq", "mk", "mv", "mo", "mi", "mf", "rq", "rk", "rv", "rg"]
    sizes = [GW] * 4 + [32] + [GW] * 7 + [8, 8] + [GW] * 4
    at = np.concatenate([[0], np.cumsum(sizes)])
    col = {n: v["w_in"][:, :, at[i]:at[i + 1]] for i, n in enumerate(names)}
    d["w_in"] = blocks(np.concatenate([col[n] for n in (
        "mq", "mk", "mv", "mo", "gq", "gk", "gv", "gg", "rq", "rk", "rv", "rg", "nq", "nk", "nv")], -1), 256)
    g = np.zeros((DEPTH, DM, 160), f)
    g[:, :, 64:96] = col["ga"]
    for z in range(2):
        g[:, :, z * 32:z * 32 + NH] = col["mi"][:, :, z * NH:(z + 1) * NH]
        g[:, :, 96 + z * 32:96 + z * 32 + NH] = col["mf"][:, :, z * NH:(z + 1) * NH]
    d["w_gates"] = blocks(g, 160)[:, 0]
    d["w_out"] = blocks(v["w_out"], 256)

    p = np.zeros((DEPTH, P, PARAM_W), f)

    def part(name):
        a, w = PARAMS[name]
        return p[:, :, a:a + w]

    part("bmod")[:] = v["b_mod"].reshape(DEPTH, 9 * KT, P).transpose(0, 2, 1)
    part("normw")[:] = v["norm_w"].reshape(DEPTH, 6 * KT, P).transpose(0, 2, 1)
    part("ba")[:] = v["gla_b_a"].reshape(DEPTH, 4, P).transpose(0, 2, 1)
    d["wa2"] = wa2 = np.zeros((DEPTH, 32, 4 * P), f)
    for z in range(2):
        part("gb")[:, z * 32:z * 32 + NH, 0] = v["mlstm_b_i"][:, z]
        part("gb")[:, z * 32:z * 32 + NH, 1] = v["mlstm_b_f"][:, z]
        part("m0")[:, z * 32:z * 32 + NH, 0] = v["state_mlstm_m"][0, :, z]
        wa2[:, z * 16:(z + 1) * 16, z * 2 * P:(z + 1) * 2 * P] = v["gla_w_a2"][:, z]
    part("rd")[:, :, 0:8] = v["ret_decay"].reshape(DEPTH, 1, 8)
    part("rd")[:, :, 8:12] = np.repeat(v["ret_decay"].reshape(DEPTH, 4, 2), HD, axis=2).transpose(0, 2, 1)
    part("gnw")[:] = v["gla_norm_w"][:, None]
    part("rnw")[:] = v["ret_norm_w"][:, None]
    part("kc")[:] = v["cache_na_k"][0].reshape(DEPTH, 2, 2, P, HD).transpose(0, 2, 4, 1, 3).reshape(DEPTH, P, 2 * P)
    part("vc")[:] = v["cache_na_v"][0].transpose(0, 2, 1, 3).reshape(DEPTH, P, GW)
    d["par"] = p

    st = np.zeros((DEPTH, 2, 2, P, 2, P), f)
    sc = np.zeros((DEPTH, 2, P, 2, SW), f)
    for h in range(NH):
        fa, a = h // 2, h % 2
        rows, cols = slice(a * HD, (a + 1) * HD), slice(a * HD, (a + 1) * HD)
        st[:, 0, :, rows, fa, cols] = v["state_gla"][0, :, :, h]
        st[:, 1, :, rows, fa, cols] = v["state_ret"][0, :, :, h]
        sc[:, :, rows, fa, a * (HD + 1):a * (HD + 1) + HD] = v["state_mlstm_C"][0, :, :, h]
        sc[:, :, rows, fa, a * (HD + 1) + HD] = v["state_mlstm_n"][0, :, :, h]
    d["st_ad"], d["st_c"] = st, sc
    r = np.zeros((DEPTH, NH, 15, 2 * HD - 1), f)
    r[:, :, :, HD - WIN:HD + WIN - 1] = v["na_rpb"]
    d["rpb"] = np.stack([r[:, :, 1 - row:15 - row, HD - 1 - q:2 * HD - 1 - q].reshape(DEPTH, -1)
                         for row in range(2) for q in range(GRID_W)], 1)
    return d


OUTS = {"y": (P, KT, NTOK), "nak": (DEPTH, P, 2, P), "nav": (DEPTH, P, GW), "gla": (DEPTH, 2, P, 2, P),
        "ret": (DEPTH, 2, P, 2, P), "mc": (DEPTH, 2, P, 2, SW), "mm": (DEPTH, 64, 1)}


def kernel(**inputs):
    import numpy as np
    import concourse.bacc as bacc
    from concourse.bass_utils import run_bass_kernel_spmd

    arrays = lay_out({k: np.asarray(a) for k, a in inputs.items()})
    nc = bacc.Bacc("TRN2", target_bir_lowering=False, num_devices=1)
    I = {k: nc.dram_tensor("in_" + k, a.shape, FP, kind="ExternalInput").ap() for k, a in arrays.items()}
    O = {k: nc.dram_tensor("out_" + k, s, FP, kind="ExternalOutput").ap() for k, s in OUTS.items()}
    build(nc, I, O)
    r = run_bass_kernel_spmd(nc, [{"in_" + k: a for k, a in arrays.items()}], core_ids=[0]).results[0]
    o = {k: np.asarray(r["out_" + k]) for k in OUTS}

    y = o["y"].transpose(2, 1, 0).reshape(NTOK, DM)
    nak = o["nak"].reshape(DEPTH, 2, HD, 2, P).transpose(0, 3, 1, 4, 2).reshape(1, DEPTH, NH, P, HD)
    nav = o["nav"].reshape(DEPTH, P, NH, HD).transpose(0, 2, 1, 3)[None]

    def heads(s, w, lo, hi):
        b = [s[:, :, a * HD:(a + 1) * HD, f, a * w + lo:a * w + hi] for f in range(2) for a in range(2)]
        return np.ascontiguousarray(np.stack(b, 2))[None]

    mm = np.stack([o["mm"][:, 0:NH, 0], o["mm"][:, 32:32 + NH, 0]], 1)[None]
    return (np.ascontiguousarray(y[:SEQ])[None], np.ascontiguousarray(y[SEQ:])[None],
            np.ascontiguousarray(nak), np.ascontiguousarray(nav),
            heads(o["gla"], HD, 0, HD), heads(o["mc"], HD + 1, 0, HD), heads(o["mc"], HD + 1, HD, HD + 1)[..., 0],
            np.ascontiguousarray(mm), heads(o["ret"], HD, 0, HD))
```

```python
import concourse.bass as bass
from concourse import mybir
from contextlib import ExitStack

FP = mybir.dt.float32
FR = mybir.dt.float32r
ALU = mybir.AluOpType
ACT = mybir.ActivationFunctionType
AXX = mybir.AxisListType.X

P = 128
DM = 1024
KT = DM // P
SEQ, DEC = 128, 512
NTOK = SEQ + DEC
NT = NTOK // P
HALF = NTOK // 2
DEPTH = 2
FF = 2816
FT = FF // P
HD = 64
NH = 4
GW = NH * HD
EPS = 1e-6
BANK = 512
GF_T = FT // 2
SLOTS = 2
SLOT_W = 2 * DM
QSCALE = HD ** -0.5
TAU = 16.0
NEG = -1e30
ROWS, GRID_W, WIN = DEC // 64, 64, 16
SW = 2 * (HD + 1)

MOD_U = 3 * KT // 2
U_FFN = (MOD_U, 0, 94)
GRP_U = (GF_T + MOD_U + KT, 0, GF_T + KT)
U_GATES = U_FFN[0] + 2 * GRP_U[0]
U_C = U_GATES + 1
U_A = U_C + 4
U_D = U_A + 4
U_B = U_D + 4
U_OUT = U_B + 3
U_ALL = U_FFN[2] + 2 * GRP_U[2]
assert U_OUT + 4 == U_FFN[2] and U_ALL == 132
MODS = set(range(MOD_U))
for _g in range(2):
    _n = U_FFN[0] + _g * GRP_U[0]
    MODS |= {_n + 2 * _m for _m in range(MOD_U)}
SPLIT = [n for n in range(U_ALL) if n not in MODS]

CONSTS = {}
_at = 0
for _name, _w in (("ident", P), ("ones", P), ("rope", NT * 2 * HD), ("namask", HD), ("causal", 2 * P),
                  ("anti", 2 * P), ("block", P), ("blockn", SW), ("diff", 2 * P), ("posrow", 2 * P),
                  ("poscol", 2), ("carry", NTOK)):
    CONSTS[_name] = (_at, _w)
    _at += _w
CONST_W = _at

PARAMS = {}
_at = 0
for _name, _w in (("bmod", 9 * KT), ("normw", 6 * KT), ("ba", 4), ("gb", 2), ("m0", 1), ("rd", 12),
                  ("gnw", HD), ("rnw", HD), ("kc", 2 * P), ("vc", GW)):
    PARAMS[_name] = (_at, _w)
    _at += _w
PARAM_W = _at


def build(nc, I, O):
    ctx = ExitStack()
    with ctx:
        def sb(name, words):
            return ctx.enter_context(nc.sbuf_tensor(name, [P, words], FP))

        sems = []

        def sem(name):
            s = ctx.enter_context(nc.semaphore(name))
            sems.append(s)
            return s

        xT = sb("xT", KT * NTOK)[:, :].rearrange("p (k n) -> p k n", k=KT)
        raw = sb("raw", SLOTS * SLOT_W)
        const = sb("const", CONST_W)
        par = sb("par", PARAM_W)
        modS = sb("modS", 9 * KT * 2)[:, :].rearrange("p (m c) -> p m c", c=2)
        gs_all = sb("gs", 3 * KT * 2)[:, :].rearrange("p (s m c) -> p s m c", s=3, c=2)
        gg_all = sb("gg", 3 * KT * 2)[:, :].rearrange("p (s m c) -> p s m c", s=3, c=2)
        cond = sb("cond", KT * 2)[:, :].rearrange("p (m c) -> p m c", c=2)
        rstd = sb("rstd", NTOK)
        small = sb("small", 256)

        def split_sb(name, words):
            return ctx.enter_context(nc.sbuf_tensor(name, [P, 2, words], FR))

        h2 = split_sb("h2", KT * NTOK)[:, :, :].rearrange("p s (k n) -> p s k n", k=KT)
        w_split = [split_sb("wsplit0", SLOT_W)]
        first_raw = nc.alloc_sbuf_tensor_at("first_raw", [P, SLOTS * SLOT_W], FP, offset=-(-nc.sbuf_base // 32) * 32)
        w_split.append(split_sb("wsplit1", SLOT_W))
        ARENA_W = 20736
        arena_at = -(-nc.sbuf_base // 32) * 32
        arena = sb("arena", ARENA_W)
        a2 = nc.alloc_sbuf_tensor_at("hidden", [P, 2, GF_T * NTOK], FR, offset=arena_at)[:, :, :]\
            .rearrange("p s (k n) -> p s k n", k=GF_T)
        ps = ctx.enter_context(nc.psum_tensor("ps", [P, 8 * BANK], FP))

        def C(name, parts=P):
            a, w = CONSTS[name]
            return const[0:parts, a:a + w]

        def W(name, parts=P):
            a, w = PARAMS[name]
            return par[0:parts, a:a + w]

        def area(a, w):
            return arena[:, a:a + w]

        def tiles(ap, n):
            return ap.rearrange("p (t n) -> p t n", t=n)

        sqb = area(2 * GF_T * NTOK, NTOK)
        mrow = area(2 * GF_T * NTOK + NTOK, 256)
        yT = tiles(area(ARENA_W - KT * NTOK, KT * NTOK), KT)
        OT = tiles(area(0, 1280), NT)
        FM = tiles(area(1280, 2560), 4)
        TM0 = 3840
        T0 = TM0 + 5140
        catP = [tiles(area(ARENA_W - 1280 * (i + 1), 1280), 2) for i in range(4)]
        CAT_K = [0, 2, 4, 6]
        OTh = area(0, 1280).rearrange("p (a e) -> p a e", e=HD)
        Tst = area(T0, 1300).rearrange("p (t f w) -> p t f w", t=NT, f=2)
        Sin = area(T0 + 1300, 1300).rearrange("p (t f w) -> p t f w", t=NT, f=2)
        Asb = [area(T0 + 2600 + 512 * i, 512).rearrange("p (a f i) -> p a f i", a=2, f=2) for i in (0, 1)]
        GX = rstd[:, :]
        GY = area(T0 + 4264, NTOK)
        GM = area(T0 + 4904, NTOK)
        GF = area(T0 + 5544, NTOK)
        GK = area(T0 + 6184, NTOK)
        CT = area(T0 + 4904, 1300).rearrange("p (t h w) -> p t h w", t=NT, h=NH)
        GT = area(T0 + 6824, 1280).rearrange("p (t a r) -> p t a r", t=NT, a=4)
        WL = [area(T0 + 8104 + 512 * i, 512).rearrange("p (a f i) -> p a f i", a=2, f=2) for i in (0, 1)]
        Vc = area(TM0, 1300).rearrange("p (t h w) -> p t h w", t=NT, h=NH)
        Oc = area(TM0 + 1300, 1280)
        ktC = [area(TM0 + 2580 + 1280 * z, 1280) for z in range(2)]
        Wk = area(T0 + 3624, 1280)
        Bk = area(TM0 + 2560, 1280)
        QM = tiles(area(TM0, 1280), 2)
        KM = tiles(area(T0 + 4904, 1280), 2)
        wa2 = area(TM0 + 3840, 4 * P)
        Va = area(ARENA_W - 2560, 1280)
        Ga = area(TM0 + 1280, 1280)
        RQK = tiles(area(ARENA_W - 5120, 2560), NT)
        rot1 = tiles(area(TM0, 2560), NT)
        rot2 = tiles(area(T0, 2560), NT)
        Vd = area(TM0 + 2560, 1280)
        Gd = area(TM0 + 3840, 1280)
        ktD = area(T0 + 5160, 1280)
        QD = tiles(area(TM0, 1280), 2)
        Dm = area(T0 + 3624, 1024).rearrange("p (z a f i) -> p z a f i", z=2, a=2, f=2)
        qdec = area(T0 + 4648, 512).rearrange("p (z f i) -> p z f i", z=2, f=2)
        qk2 = nc.alloc_sbuf_tensor_at("na_qk", [P, 2, 4 * NTOK], FR, offset=arena_at + 4 * 1280)[:, :, :]\
            .rearrange("p s (f n) -> p s f n", f=4)
        kc2 = nc.alloc_sbuf_tensor_at("na_kc", [P, 2, 2 * P], FR, offset=arena_at + 4 * 6400)[:, :, :]\
            .rearrange("p s (f n) -> p s f n", f=2)
        knew = tiles(area(6912, 2 * P), 2)
        Vn = area(0, 1280)
        SB = [area(T0 + NTOK * i, NTOK) for i in (0, 1)]
        PT = area(T0 + 1280, NTOK)
        rpb = area(T0 + 1920, NH * 14 * HD)

        ident, ones = C("ident"), C("ones")
        causal = C("causal").rearrange("p (z i) -> p z i", z=2)
        anti = C("anti").rearrange("p (z i) -> p z i", z=2)

        once = lambda name: ctx.enter_context(nc.semaphore(name))
        cond_loaded, const_loaded, x_loaded = once("cond_loaded"), once("const_loaded"), once("x_loaded")

        rpb_loaded = sem("rpb_loaded")
        wa2_loaded = sem("wa2_loaded")

        first_loaded = [sem(f"first{i}_loaded") for i in range(SLOTS)]
        loaded = [sem(f"slot{i}_loaded") for i in range(SLOTS)]
        pool_hi = sem("pool_hi")
        split_done = sem("split_done")
        mrow_ready = sem("mrow_ready")
        mtr_done = sem("mtr_done")
        turn_begun = sem("turn_begun")
        split_begun = sem("split_begun")
        a_hi = sem("a_hi")
        a_lo = sem("a_lo")
        acc_add = sem("acc_add")
        y_scaled = sem("y_scaled")
        y_norm = sem("y_norm")
        out_part = sem("out_part")
        out_evac = sem("out_evac")
        h_hi = sem("h_hi")
        cat_hi = sem("cat_hi")
        cat_split = sem("cat_split")
        init_loaded = sem("init_loaded")
        st_out = sem("st_out")
        na_out = sem("na_out")
        m_out = sem("m_out")
        unit_done = sem("unit_done")
        unit_evac = sem("unit_evac")
        par_loaded = sem("par_loaded")
        mod_ready = sem("mod_ready")
        gate_ready = sem("gate_ready")
        sq_ready = sem("sq_ready")
        ss_done = sem("ss_done")
        rstd_ready = sem("rstd_ready")
        hmul_ready = sem("hmul_ready")
        h_ready = sem("h_ready")
        silu_done = sem("silu_done")
        x_ready = sem("x_ready")
        gate_pre = sem("gate_pre")
        gate_sp = sem("gate_sp")
        gate_log = sem("gate_log")
        gate_exp = sem("gate_exp")
        gate_t = sem("gate_t")
        gate_cols = sem("gate_cols")
        apre_done = sem("apre_done")
        asp_done = sem("asp_done")
        ad_ready = sem("ad_ready")
        ae_ready = sem("ae_ready")
        aqk_ready = sem("aqk_ready")
        akt_done = sem("akt_done")
        akt_ready = sem("akt_ready")
        lg_ready = sem("lg_ready")
        lg_sp = sem("lg_sp")
        dec_ready = sem("dec_ready")
        rot_ready = sem("rot_ready")
        rt_done = sem("rt_done")
        rt_evac = sem("rt_evac")
        qd_ready = sem("qd_ready")
        kt_ready = sem("kt_ready")
        u_done = sem("u_done")
        t_done = sem("t_done")
        s_ready = sem("s_ready")
        p_done = sem("p_done")
        wl_done = sem("wl_done")
        w_ready = sem("w_ready")
        a_done = sem("a_done")
        o_done = sem("o_done")
        ot_done = sem("ot_done")
        act_gate = sem("act_gate")
        nrm_in = sem("nrm_in")
        nrm_out = sem("nrm_out")
        fin_ready = sem("fin_ready")
        cat_t = sem("cat_t")
        cat_done = sem("cat_done")
        na_s = sem("na_s")
        na_read = sem("na_read")
        na_max = sem("na_max")
        na_e = sem("na_e")
        na_n = sem("na_n")
        na_pt = sem("na_pt")
        na_ptc = sem("na_ptc")
        na_o = sem("na_o")
        na_oc = sem("na_oc")
        cond_ready = sem("cond_ready")
        y_out = sem("y_out")

        UD = lambda n: n + 1 + SLOTS
        EV = lambda n: n + 1 + 2
        slot = lambda n: n % SLOTS
        use = lambda n: 16 * ((n if n < MOD_U else n - MOD_U) // SLOTS + 1)
        SD = lambda n: SPLIT.index(n) + 1
        half = lambda n: (n % 2) * 4 * BANK
        G_C, G_A, G_D = 0, 1, 2
        CAT_TURNS = range(5, 11)
        R = lambda g, z, t: (g * 2 + z) * NT + t + 1
        Z = lambda g, z: g * 2 + z + 1
        HEADS = [(h // 2, h % 2) for h in range(NH)]
        order = lambda z: (1, 2, 3, 4) if z == 0 else (4, 3, 2, 1)

        def acc(base):
            return ps[:, base:base + 2 * BANK].rearrange("p (a n) -> p a n", a=2)[:, :, 0:HALF]

        def halves(ap):
            return ap.rearrange("p (a n) -> p a n", a=2)

        def slot_ap(n, words):
            ring = first_raw if n < MOD_U else raw
            return ring[:, slot(n) * SLOT_W:slot(n) * SLOT_W + words]

        def arrival(n):
            return (first_loaded if n < MOD_U else loaded)[slot(n)]

        def split_ap(n, words):
            return w_split[SPLIT.index(n) % SLOTS][:, :, 0:words]

        with nc.Block() as block:
            @block.sync
            def _(sp):
                sp.dma_start(cond, I["cond"]).then_inc(cond_loaded, 16)
                sp.dma_start(const[:, :], I["const"]).then_inc(const_loaded, 16)

            @block.scalar
            def _(act):
                act.dma_start(xT, I["x"]).then_inc(x_loaded, 16)
                act.wait_ge(cond_loaded, 16)
                act.activation(cond, cond, ACT.Silu).then_inc(cond_ready, 1)
                act.wait_ge(cond_ready, 1)

        with nc.Fori(0, DEPTH) as l:
            with nc.Block() as block:
                @block.sync
                def _(sp):
                    sp.dma_start(par[:, :], I["par"][l]).then_inc(par_loaded, 16)

                    def load(n, words, src, i=0, du=2, ds=2):
                        if MOD_U <= n < MOD_U + SLOTS:
                            pass
                        elif n - SLOTS in SPLIT:
                            sp.wait_ge(split_done, i * ds + SD(n - SLOTS))
                        else:
                            sp.wait_ge(unit_done, i * du + UD(n - SLOTS))
                        sp.dma_start(slot_ap(n, words), src).then_inc(arrival(n), 16)

                    for u in range(2):
                        load(u, SLOT_W, I["w_mod"][l, u])
                    load(MOD_U + 1, SLOT_W, I["w13"][l, 0])
                    with sp.Fori(0, MOD_U // 2 - 1) as i:
                        for u in range(2):
                            load(2 + u, SLOT_W, I["w_mod"][l, i * 2 + (2 + u)], i)
                    load(MOD_U, SLOT_W, I["w_mod"][l, MOD_U])
                    for s, j in ((0, 0), (2, 1)):
                        for grp in range(2):
                            n = U_FFN[s] + grp * GRP_U[s]
                            f0 = j * FT + grp * GF_T
                            if s == 0:
                                m0 = MOD_U * (1 + grp)
                                if grp:
                                    load(n, SLOT_W, I["w_mod"][l, m0])
                                    load(n + 1, SLOT_W, I["w13"][l, f0])
                                load(n + 2, SLOT_W, I["w_mod"][l, m0 + 1])
                                with sp.Fori(0, GF_T - 1) as i:
                                    load(n + 3, SLOT_W, I["w13"][l, i + (f0 + 1)], i, ds=1)
                                    load(n + 4, SLOT_W, I["w_mod"][l, i + (m0 + 2)], i)
                                n += GF_T + MOD_U
                            else:
                                with sp.Fori(0, GF_T // 2) as i:
                                    for u in range(2):
                                        load(n + u, SLOT_W, I["w13"][l, i * 2 + (f0 + u)], i)
                                load(n + GF_T - 1, SLOT_W, I["w13"][l, f0 + GF_T - 1])
                                n += GF_T
                            d0 = (2 * j + grp) * KT
                            for u in range(2):
                                load(n + u, GF_T * P, I["w2"][l, d0 + u])
                            with sp.Fori(0, KT // 2 - 1) as i:
                                for u in range(2):
                                    load(n + 2 + u, GF_T * P, I["w2"][l, i * 2 + (d0 + 2 + u)], i)
                        if s == 0:
                            load(U_GATES, KT * 160, I["w_gates"][l])
                            for q in range(15):
                                load(U_C + q, SLOT_W, I["w_in"][l, q])
                            for q in range(4):
                                load(U_OUT + q, SLOT_W, I["w_out"][l, q])

                @block.gpsimd
                def _(pool):
                    def split(n, words, i=0, du=2):
                        pool.wait_ge(arrival(n), i * (8 * du) + use(n))
                        k = SPLIT.index(n)
                        if k == 1:
                            pool.wait_ge(unit_done, UD(MOD_U - 1))
                        if k >= SLOTS:
                            pool.wait_ge(unit_done, i * du + UD(SPLIT[k - SLOTS]))
                        pool.sem_inc(split_begun, 1)
                        w, src = split_ap(n, words), slot_ap(n, words)
                        nc.gpsimd.tensor_scalar(w[:, 0], src, 1.0, 1.0, ALU.mult, ALU.mult).then_inc(pool_hi, 1)
                        pool.wait_ge(pool_hi, i * 2 + (k + 1))
                        nc.gpsimd.tensor_tensor(w[:, 1], src, w[:, 0].bitcast(FP), ALU.subtract)\
                            .then_inc(split_done, 1)

                    for s in (0, 2):
                        step = 2 if s == 0 else 1
                        for grp in range(2):
                            n = U_FFN[s] + grp * GRP_U[s] + step - 1
                            for u in range(2):
                                split(n + u * step, SLOT_W)
                            with pool.Fori(0, (GF_T - 3) // 2) as i:
                                for u in range(2):
                                    split(n + (2 + u) * step, SLOT_W, i, 2 * step)
                            split(n + (GF_T - 1) * step, SLOT_W)
                            n = U_FFN[s] + (grp + 1) * GRP_U[s] - KT
                            for u in range(2):
                                split(n + u, GF_T * P)
                            with pool.Fori(0, KT // 2 - 1) as i:
                                for u in range(2):
                                    split(n + 2 + u, GF_T * P, i)
                        if s == 0:
                            split(U_GATES, KT * 160)
                            for q in range(19):
                                split(U_C + q, SLOT_W)

                @block.tensor
                def _(pe):
                    mm = pe.matmul
                    pe.sem_inc(unit_done, SLOTS)

                    def claim(n, i=0, du=2):
                        pe.wait_ge(split_done, i * 2 + SD(n))
                        pe.wait_ge(unit_evac, i * du + (n + 1))
                        return half(n)

                    def three_pass(out, w, x, first, last):
                        mm(out, w[0], x[0], start=first, stop=False)
                        mm(out, w[0], x[1], start=False, stop=False)
                        return mm(out, w[1], x[0], start=False, stop=last)

                    def mod(n, i=0, du=2):
                        pe.wait_ge(arrival(n), i * (8 * du) + use(n))
                        pe.wait_ge(unit_evac, i * du + (n + 1))
                        w = tiles(slot_ap(n, SLOT_W), KT)
                        for k in range(KT):
                            last = mm(ps[0:2, half(n):half(n) + 256], cond[:, k, :], w[:, k, :],
                                      start=k == 0, stop=k == KT - 1)
                        last.then_inc(unit_done, 1)

                    def mod_turn(n, q, i=0):
                        pe.wait_ge(mrow_ready, i + (q + 1))
                        pe.sem_inc(turn_begun, 1)
                        for m in range(2):
                            c = half(n) + BANK + 2 * m
                            last = pe.transpose(ps[:, c:c + 2], mrow[0:2, m * P:(m + 1) * P], ident[0:2, 0:2])
                        last.then_inc(mtr_done, 1)

                    def sums(v, n=None):
                        if n:
                            pe.wait_ge(unit_evac, EV(n - 1))
                        if v and v % 2 == 0:
                            for k in range(KT):
                                pe.wait_ge(sq_ready, KT * v + k + 1)
                                for a in range(2):
                                    last = mm(ps[:, (2 + a) * BANK:(2 + a) * BANK + HALF], ones, yT[:, k, a * HALF:(a + 1) * HALF],
                                              start=k == 0, stop=k == KT - 1)
                        else:
                            pe.wait_ge(acc_add, KT * ((v + 1) // 2 + 1))
                            for a in range(2):
                                last = mm(ps[:, (2 + a) * BANK:(2 + a) * BANK + HALF], ones, rstd[:, a * HALF:(a + 1) * HALF],
                                          start=True, stop=True)
                        last.then_inc(ss_done, 1)
                        if v:
                            pe.wait_ge(rstd_ready, v + 1)

                    def feature_major(base, w, x, cols=P, between=None, need=None):
                        nk = w.shape[2]
                        for a in range(2):
                            for k in range(nk):
                                if need and a == 0:
                                    need(k)
                                last = three_pass(ps[0:cols, base + a * BANK:base + a * BANK + HALF],
                                                  (w[:, 0, k, :], w[:, 1, k, :]),
                                                  [x[:, p, k, a * HALF:(a + 1) * HALF] for p in range(2)],
                                                  k == 0, k == nk - 1)
                            if a == 0 and between:
                                between()
                        return last

                    def first_products(s, base, blocks):
                        for k in range(KT):
                            pe.wait_ge(h_ready, KT * s + k + 1)
                            for b, w in enumerate(blocks):
                                for a in range(2):
                                    c = base + (2 * b + a) * BANK
                                    last = three_pass(ps[0:w.shape[3], c:c + HALF], (w[:, 0, k, :], w[:, 1, k, :]),
                                                      [h2[:, p, k, a * HALF:(a + 1) * HALF] for p in range(2)],
                                                      k == 0, k == KT - 1)
                        last.then_inc(unit_done, 1)

                    def up_weights(n):
                        w = split_ap(n, SLOT_W).rearrange("p s (b k c) -> p s b k c", b=2, k=KT)
                        return w[:, :, 0], w[:, :, 1]

                    def up(n, i=0, du=2, between=None):
                        base = claim(n, i, du)
                        gate, value = up_weights(n)
                        feature_major(base, gate, h2)
                        if between:
                            between()
                        feature_major(base + 2 * BANK, value, h2).then_inc(unit_done, 1)

                    def down(n, i=0, between=None, need=None):
                        base = claim(n, i)
                        w = split_ap(n, GF_T * P).rearrange("p s (f c) -> p s f c", f=GF_T)
                        feature_major(base, w, a2, between=between, need=need).then_inc(unit_done, 1)

                    def ffn(s, j):
                        for grp in range(2):
                            n = U_FFN[s] + grp * GRP_U[s]
                            q = MOD_U * (1 + grp)
                            if s == 0 and grp:
                                mod(n)
                            f = n + (s == 0)
                            turn = (lambda: mod_turn(n, q)) if s == 0 else None
                            if grp:
                                up(f, between=turn)
                            else:
                                first_products(s, claim(f), up_weights(f))
                                if turn:
                                    turn()
                            if s == 0:
                                mod(n + 2)
                                with pe.Fori(0, GF_T // 2) as i:
                                    for u in range(2):
                                        m = n + 2 + 2 * u
                                        up(m + 1, i, 4, lambda: mod_turn(m, q + 1 + u, i * 2))
                                        mod(m + 2, i, 4)
                                n += GF_T + MOD_U
                                turn = lambda: mod_turn(n - 1, q + GF_T)
                            else:
                                with pe.Fori(0, GF_T // 2) as i:
                                    for u in range(2):
                                        up(n + 1 + u, i)
                                n += GF_T
                                turn = None

                            def hidden(k):
                                if k in (0, GF_T - 1):
                                    pe.wait_ge(a_lo, 1 + j * FT + grp * GF_T + (GF_T if k else GF_T - 1))

                            down(n, between=turn, need=hidden)
                            down(n + 1)
                            with pe.Fori(0, KT // 2 - 1) as i:
                                for u in range(2):
                                    down(n + 2 + u, i)

                    def features(n, need=None, part=None):
                        base = claim(n)
                        w = split_ap(n, KT * 256).rearrange("p s (k m c) -> p s k m c", k=KT, m=2)
                        for m in range(2):
                            last = feature_major(base + 2 * m * BANK, w[:, :, :, m], h2, need=None if m else need)
                            if part and m == 0:
                                last.then_inc(part, 1)
                        last.then_inc(unit_done, 1)

                    def tokens(n):
                        base = claim(n)
                        w = split_ap(n, KT * 256).rearrange("p s (k c) -> p s k c", k=KT)
                        for t in range(NT):
                            for k in range(KT):
                                last = three_pass(ps[:, base + t * GW:base + (t + 1) * GW],
                                                  [h2[:, p, k, t * P:(t + 1) * P] for p in range(2)],
                                                  (w[:, 0, k, :], w[:, 1, k, :]), k == 0, k == KT - 1)
                        last.then_inc(unit_done, 1)

                    def gates():
                        base = claim(U_GATES)
                        w = split_ap(U_GATES, KT * 160).rearrange("p s (k c) -> p s k c", k=KT)
                        first_products(1, base, (w[:, :, :, 0:96], w[:, :, :, 96:160]))

                    def tr(col, src, rows=P):
                        return pe.transpose(ps[:, col:col + rows], src, ident[0:rows, 0:rows])

                    def scan_group(g, z, k2, q2, qi, kt, v, vw):
                        for t in range(NT):
                            if t >= 2:
                                pe.wait_ge(t_done, R(g, z, t - 2))
                            for f in range(2):
                                c = (t % 2) * BANK + f * 2 * vw
                                last = mm(ps[:, c:c + 2 * vw], kt[:, t, f * P:(f + 1) * P],
                                          v[:, t, 2 * f * vw:2 * (f + 1) * vw], start=True, stop=True)
                            last.then_inc(u_done, 1)

                        def scores(t):
                            if t >= 2:
                                pe.wait_ge(a_done, R(g, z, t - 2))
                            b = (2 + 2 * (t % 2)) * BANK
                            if g == G_C:
                                for f, a in HEADS:
                                    row = z * 32 + 2 * f + a
                                    c = b + a * BANK + GW + f * P
                                    mm(ps[:, c:c + P], ident[:, row:row + 1].to_broadcast([P, P]),
                                       GY[:, t * P:(t + 1) * P], start=True, stop=True)
                            for f, a in HEADS:
                                rows = slice(a * HD, (a + 1) * HD)
                                c = b + a * BANK + f * P
                                last = mm(ps[:, c:c + P], k2[rows, f, t * P:(t + 1) * P],
                                          q2[rows, f, t * P:(t + 1) * P], start=True, stop=True)
                            last.then_inc(p_done, 1)

                        def output(t):
                            pe.wait_ge(a_done, R(g, z, t))
                            if t == 1:
                                pe.wait_ge(s_ready, Z(g, z))
                                if g == G_D:
                                    pe.wait_ge(qd_ready, z + 1)
                            if t >= 2:
                                pe.wait_ge(ot_done, R(g, z, t - 2))
                            o = (6 + t % 2) * BANK
                            own = t == 0 or g == G_C
                            for h, (f, a) in enumerate(HEADS):
                                last = mm(ps[:, o + h * vw:o + (h + 1) * vw], Asb[t % 2][:, a, f, :],
                                          v[:, t, h * vw:(h + 1) * vw], start=h == 0, stop=own,
                                          skip_group_check=True)
                            if t:
                                for f in range(2):
                                    c = o + f * P if g != G_C else (t % 2) * BANK + f * SW
                                    s = (Tst if g == G_A else Sin)[:, t, f, 0:2 * vw]
                                    last = mm(ps[:, c:c + 2 * vw], qi[:, f, t * P:(t + 1) * P], s,
                                              start=g == G_C and f == 0, stop=True, skip_group_check=True)
                            last.then_inc(o_done, 1)

                        scores(0)
                        if (g, z) == (G_C, 0):
                            pe.wait_ge(kt_ready, 2)
                        for t in range(NT):
                            if t + 1 < NT:
                                scores(t + 1)
                            output(t)

                    def concat(c, base=0):
                        pe.wait_ge(fin_ready, c)
                        for f in range(2):
                            for t in range(NT):
                                last = tr(base + (f * NT + t) * P, OT[:, t, f * P:(f + 1) * P])
                        last.then_inc(cat_t, 1)
                        pe.wait_ge(cat_done, c)

                    mod(0)
                    mod(1)
                    pe.wait_ge(const_loaded, 16)
                    mod_turn(0, 0)
                    for a, b in ((0, 3), (3, MOD_U // 2 - 1)):
                        with pe.Fori(0, b - a) as i:
                            for u in range(2):
                                mod(2 * a + 2 + u, i)
                                mod_turn(2 * a + 1 + u, 2 * a + 1 + u, i * 2)
                        if a == 0:
                            sums(0)
                    mod(U_FFN[0])
                    mod_turn(MOD_U - 1, MOD_U - 1)
                    ffn(0, 0)
                    sums(1, U_GATES)
                    sums(2, U_GATES)
                    gates()

                    features(U_C)
                    features(U_C + 1)
                    tokens(U_C + 2)
                    tokens(U_C + 3)
                    tokens(U_A)
                    pe.wait_ge(unit_evac, EV(U_C + 3))
                    pe.wait_ge(gate_exp, 1)
                    for t in range(NT):
                        for a, rows in enumerate((GX, GF, GM, GK)):
                            tr((t * 4 + a) * 64, rows[0:64, t * P:(t + 1) * P], 64)
                    pe.wait_ge(unit_evac, EV(U_A))
                    for t in range(NT):
                        for f in range(2):
                            tr(4 * BANK + (t * 2 + f) * P, FM[:, 2 + f, t * P:(t + 1) * P])
                    for z in range(2):
                        for f in range(2):
                            c = 7 * BANK + (z * 2 + f) * NT
                            for a in range(2):
                                row = z * 32 + 2 * f + a
                                last = mm(ps[a * HD:(a + 1) * HD, c:c + NT],
                                          ident[0:64, row:row + 1].to_broadcast([64, HD]),
                                          small[0:64, 16:16 + NT], start=True, stop=True)
                    last.then_inc(gate_t, 1)
                    for z in range(2):
                        pe.wait_ge(kt_ready, z + 1)
                        if z:
                            pe.wait_ge(ot_done, R(G_C, 0, NT - 1))
                        scan_group(G_C, z, FM[:, 2:4, :], FM[:, 0:2, :], FM[:, 0:2, :], tiles(ktC[z], NT),
                                   Vc.rearrange("p t h w -> p t (h w)"), HD + 1)
                    pe.wait_ge(ot_done, R(G_C, 1, NT - 1))
                    features(U_A + 1)
                    concat(1, 4 * BANK)

                    features(U_A + 2)
                    tokens(U_A + 3)
                    pe.wait_ge(unit_evac, EV(U_A + 3))
                    pe.wait_ge(wa2_loaded, 16)
                    for z in range(2):
                        if z:
                            pe.wait_ge(ot_done, R(G_A, 0, NT - 1))
                        for f in range(2):
                            for a in range(2):
                                c = (4 * z + 2 * f + a) * BANK
                                last = mm(ps[:, c:c + HALF], wa2[64:96, (2 * z + f) * P:(2 * z + f + 1) * P],
                                          GX[64:96, a * HALF:(a + 1) * HALF], start=True, stop=True)
                        last.then_inc(apre_done, 1)
                        tokens(U_D + z)
                        pe.wait_ge(unit_evac, EV(U_D + z))
                        pe.wait_ge(aqk_ready, z + 1)
                        for t in range(NT):
                            for f in range(2):
                                last = tr((t * 2 + f) * P, KM[:, f, t * P:(t + 1) * P])
                        last.then_inc(akt_done, 1)
                        pe.wait_ge(akt_ready, z + 1)
                        scan_group(G_A, z, KM, QM, QM, tiles(Bk, NT), tiles(Va, NT), HD)
                    pe.wait_ge(ot_done, R(G_A, 1, NT - 1))
                    tokens(U_D + 2)
                    concat(2)

                    tokens(U_D + 3)
                    pe.wait_ge(unit_evac, EV(U_D + 3))
                    pe.wait_ge(rot_ready, 1)
                    for t in range(NT):
                        if t >= 2:
                            pe.wait_ge(rt_evac, t - 1)
                        for f in range(4):
                            last = tr((t % 2) * BANK + f * P, RQK[:, t, f * P:(f + 1) * P])
                        last.then_inc(rt_done, 1)
                    pe.wait_ge(rt_evac, NT)
                    for z in range(2):
                        pe.wait_ge(kt_ready, 2 + z + 1)
                        if z:
                            pe.wait_ge(ot_done, R(G_D, 0, NT - 1))
                        scan_group(G_D, z, FM[:, 2:4, :], FM[:, 0:2, :], QD, tiles(ktD, NT), tiles(Vd, NT), HD)
                    pe.wait_ge(ot_done, R(G_D, 1, NT - 1))
                    features(U_B)
                    concat(3)

                    features(U_B + 1)
                    tokens(U_B + 2)
                    vc = W("vc")
                    vb = tiles(Vn, NT)

                    def na_scores(b):
                        t, h = b // NH, b % NH
                        f, a = HEADS[h]
                        if b >= 2:
                            pe.wait_ge(na_read, b - 1)
                        rows = slice(a * HD, (a + 1) * HD)
                        c = a * 2 * BANK
                        q = [qk2[rows, p, f, t * P:(t + 1) * P] for p in range(2)]

                        def keys(c, k):
                            return three_pass(ps[:, c:c + k[0].shape[-1]], q, k, True, True)

                        if t == 0:
                            last = keys(c, [qk2[rows, p, 2 + f, 0:P] for p in range(2)])
                        else:
                            keys(c, [qk2[rows, p, 2 + f, P:NTOK] for p in range(2)])
                            last = keys(c + BANK, [kc2[rows, p, f, :] for p in range(2)])
                        last.then_inc(na_s, 1)

                    def na_turn(b):
                        pe.wait_ge(na_n, b + 1)
                        if b:
                            pe.wait_ge(na_ptc, b)
                        for j in range(1 if b < NH else NT):
                            last = tr(4 * BANK + j * P, SB[b % 2][:, j * P:(j + 1) * P])
                        last.then_inc(na_pt, 1)

                    def na_values(b):
                        t, h = b // NH, b % NH
                        n = 1 if t == 0 else NT
                        pe.wait_ge(na_ptc, b + 1)
                        if b >= 2:
                            pe.wait_ge(na_oc, b - 1)
                        o = (6 + b % 2) * BANK
                        rows = slice(h % 2 * HD, (h % 2 + 1) * HD)
                        for j in range(n):
                            v = vb[:, 0, :] if t == 0 else vb[:, 1 + j, :] if j < NT - 1 else vc
                            last = mm(ps[rows, o:o + P], v[:, h * HD:(h + 1) * HD], PT[:, j * P:(j + 1) * P],
                                      start=j == 0, stop=j == n - 1)
                        last.then_inc(na_o, 1)

                    pe.wait_ge(unit_evac, EV(U_B + 1))
                    na_scores(0)
                    na_scores(1)
                    pe.wait_ge(unit_evac, EV(U_B + 2))
                    for b in range(NT * NH):
                        na_turn(b)
                        if b + 2 < NT * NH:
                            na_scores(b + 2)
                        na_values(b)

                    def cat_ready(k):
                        if k in (0, CAT_K[3]):
                            pe.wait_ge(cat_split, KT if k else CAT_K[3])

                    for q in range(4):
                        features(U_OUT + q, cat_ready if q == 0 else None, out_part if q == 3 else None)
                    sums(3, U_FFN[2])
                    sums(4, U_FFN[2])
                    ffn(2, 1)
                    sums(5, U_ALL)

                @block.scalar
                def _(act):
                    def fn(out, in_, f, **kw):
                        return act.activation(out, in_, f, **kw)

                    def ln_exp():
                        act.preload_act_table_set("natural_log_exp_and_others")

                    def norm(v, n0, per):
                        for k in range(KT):
                            if v % 2 == 0:
                                if v:
                                    act.wait_ge(x_ready, KT * (v // 2 - 1) + k + 1)
                                last = fn(yT[:, k, :], xT[:, k, :], ACT.Square)
                            else:
                                if v == 3 and k == KT - 2:
                                    act.wait_ge(out_evac, 1)
                                else:
                                    act.wait_ge(unit_evac, EV(n0 + k // per))
                                if k:
                                    act.wait_ge(acc_add, KT * (v // 2 + 1) + k)
                                last = fn(sqb, yT[:, k, :], ACT.Square)
                            last.then_inc(sq_ready, 1)
                            if v % 2:
                                act.drain()
                                if k == 0:
                                    act.wait_ge(gate_ready, v // 2 + 1)
                                for c, cols in enumerate((slice(0, SEQ), slice(SEQ, NTOK))):
                                    last = fn(yT[:, k, cols], yT[:, k, cols], ACT.Copy,
                                              scale=gg_all[:, v // 2, k, c:c + 1])
                                last.then_inc(y_scaled, 1)
                        ln_exp()
                        act.wait_ge(ss_done, v + 1)
                        fn(halves(rstd[:, :]), acc(2 * BANK), ACT.Ln, scale=1.0 / DM, bias=eps)
                        act.drain()
                        fn(rstd[:, :], rstd[:, :], ACT.Exp, scale=-0.5).then_inc(rstd_ready, 1)

                    def modulate(s):
                        for k in range(KT):
                            act.wait_ge(hmul_ready, KT * s + k + 1)
                            for c, cols in enumerate((slice(0, SEQ), slice(SEQ, NTOK))):
                                last = fn(h2[:, 0, k, cols], yT[:, k, cols], ACT.Identity,
                                          bias=modS[:, 3 * KT * s + k, c:c + 1])
                            last.then_inc(h_hi, 1)

                    def ffn(s, j):
                        def one(n, i2, f, count, per):
                            act.wait_ge(a_lo, i2 * per + (count + 1))
                            act.wait_ge(unit_done, i2 * 2 + UD(n))
                            fn(halves(rstd[:, :]), acc(half(n)), ACT.Silu).then_inc(silu_done, 1)
                            act.wait_ge(unit_evac, i2 * 2 + EV(n))
                            fn(f, rstd[:, :], ACT.Copy).then_inc(a_hi, 1)

                        act.preload_act_table_set("silu_and_others")
                        if s:
                            act.wait_ge(st_out, 6 * 16)
                            act.wait_ge(m_out, 16)
                        for grp in range(2):
                            n = U_FFN[s] + grp * GRP_U[s]
                            c = j * FT + grp * GF_T
                            hi = a2[:, 0].rearrange("p k n -> p (k n)")
                            if s == 0:
                                with act.Fori(0, GF_T) as i:
                                    one(n + 1, i, hi[:, bass.ds(i * NTOK, NTOK)], c, 1)
                            else:
                                with act.Fori(0, GF_T // 2) as i:
                                    for u in range(2):
                                        one(n + u, i, hi[:, bass.ds(i * (2 * NTOK) + u * NTOK, NTOK)], c + u, 2)
                                one(n + GF_T - 1, 0, a2[:, 0, GF_T - 1, :], c + GF_T - 1, 0)

                    def three(dst, base):
                        for a in (0, 512, 1024):
                            w = min(512, 1280 - a)
                            last = fn(dst[:, a:a + w], ps[:, base + a:base + a + w], ACT.Copy)
                        return last

                    def softplus(buf, n):
                        act.drain()
                        fn(buf, buf, ACT.Exp, scale=-1.0)
                        act.drain()
                        return fn(buf, buf, ACT.Ln, bias=1.0)

                    def head_rstd(c):
                        ln_exp()
                        act.wait_ge(nrm_in, c)
                        fn(small[:, 64:84], small[:, 64:84], ACT.Ln, scale=1.0 / HD, bias=eps)
                        act.drain()
                        fn(small[:, 64:84], small[:, 64:84], ACT.Exp, scale=-0.5).then_inc(nrm_out, 1)

                    def concat(c, base=0):
                        act.wait_ge(cat_t, c)
                        three(catP[c - 1].rearrange("p k n -> p (k n)"), base).then_inc(cat_done, 1)

                    def cat_upper(k):
                        if k % 2 == 0:
                            if k < CAT_K[3]:
                                act.wait_ge(cat_done, k // 2 + 1)
                            else:
                                act.wait_ge(na_oc, NT * NH)
                        fn(h2[:, 0, k, :], catP[k // 2][:, k % 2, :], ACT.Copy).then_inc(cat_hi, 1)

                    def evac(n, dst, scale=1.0):
                        act.wait_ge(unit_done, UD(n))
                        act.wait_ge(unit_evac, EV(n - 1))
                        fn(dst, tiles(ps[:, half(n):half(n) + NT * GW], NT), ACT.Copy, scale=scale)\
                            .then_inc(unit_evac, 1)

                    def state_in(g, z):
                        w = SW if g == G_C else P
                        if Z(g, z) > 1:
                            act.wait_ge(o_done, R(g, z, -1))
                        src = I["st_c"][l, z] if g == G_C else I["st_ad"][l, 0 if g == G_A else 1, z]
                        act.dma_start(Sin[:, order(z)[0], :, 0:w], src).then_inc(init_loaded, 16)

                    def state_out(g, z):
                        w = SW if g == G_C else P
                        act.wait_ge(t_done, R(g, z, 0))
                        act.dma_start((O["mc"], O["gla"], O["ret"])[g][l, z], Tst[:, 0, :, 0:w]).then_inc(st_out, 16)

                    eps = small[:, 255:256]

                    act.wait_ge(x_loaded, 16)
                    act.wait_ge(const_loaded, 16)
                    norm(0, 0, 1)
                    modulate(0)
                    ffn(0, 0)
                    norm(1, U_GATES - KT, 1)
                    norm(2, 0, 1)
                    modulate(1)

                    ln_exp()
                    act.wait_ge(gate_pre, 1)
                    fn(GK[0:64, :], GY[0:64, :], ACT.Abs)
                    softplus(GK[0:64, :], 64).then_inc(gate_sp, 1)
                    state_in(G_C, 0)
                    act.wait_ge(gate_log, 1)
                    act.dma_start(O["mm"][l], small[0:64, 0:1]).then_inc(m_out, 16)
                    fn(GF[0:64, :], GF[0:64, :], ACT.Exp)
                    fn(GK[0:64, :], GK[0:64, :], ACT.Exp)
                    fn(small[0:64, 16:21], small[0:64, 16:21], ACT.Exp)
                    fn(GM[0:64, :], GM[0:64, :], ACT.Exp, scale=-1.0).then_inc(gate_exp, 1)
                    evac(U_A, tiles(Va, NT))
                    act.wait_ge(gate_t, 1)
                    three(area(T0 + 6824, 1280), 0)
                    fn(small[:, 24:44], ps[:, 7 * BANK:7 * BANK + 20], ACT.Copy).then_inc(gate_cols, 1)
                    for z in range(2):
                        for t in range(NT):
                            act.wait_ge(wl_done, z * NT + t + 1)
                            fn(WL[t % 2], WL[t % 2], ACT.Exp).then_inc(w_ready, 1)
                            if t == 0:
                                state_out(G_C, z)
                        if z == 0:
                            state_in(G_C, 1)
                    act.wait_ge(unit_evac, EV(U_C + 3))
                    fn(Oc, Oc, ACT.Sigmoid).then_inc(act_gate, 1)
                    concat(1, 4 * BANK)

                    act.dma_start(wa2[64:96, :], I["wa2"][l]).then_inc(wa2_loaded, 16)
                    ln_exp()
                    for z in range(2):
                        act.wait_ge(apre_done, z + 1)
                        for f in range(2):
                            b = W("ba")[:, 2 * z + f:2 * z + f + 1]
                            fn(halves(Wk[:, f * NTOK:(f + 1) * NTOK]), acc((4 * z + 2 * f) * BANK), ACT.Abs, bias=b)
                            fn(halves(QM[:, f, :]), acc((4 * z + 2 * f) * BANK), ACT.Identity, bias=b)
                        softplus(Wk, P).then_inc(asp_done, 1)
                        act.wait_ge(ad_ready, z + 1)
                        fn(QM.rearrange("p f n -> p (f n)"), Wk, ACT.Exp, scale=1.0 / TAU)
                        fn(KM.rearrange("p f n -> p (f n)"), Wk, ACT.Exp, scale=-1.0 / TAU)
                        fn(small[:, 96:126], small[:, 96:126], ACT.Exp, scale=1.0 / TAU).then_inc(ae_ready, 1)
                        evac(U_D + z, RQK[:, :, z * GW:(z + 1) * GW], 1.0 if z else QSCALE)
                        act.wait_ge(akt_done, z + 1)
                        three(Bk, 0).then_inc(akt_ready, 1)
                        state_in(G_A, z)
                        state_out(G_A, z)
                    act.wait_ge(unit_evac, EV(U_A + 3))
                    head_rstd(1)
                    fn(Ga, Ga, ACT.Silu).then_inc(act_gate, 1)
                    concat(2)

                    ln_exp()
                    act.wait_ge(par_loaded, 16)
                    lg = small[:, 128:140]
                    act.wait_ge(lg_ready, 1)
                    fn(small[:, 144:156], W("rd"), ACT.Abs)
                    softplus(small[:, 144:156], P).then_inc(lg_sp, 1)
                    act.wait_ge(lg_ready, 2)
                    diff = C("diff").rearrange("p (z i) -> p z i", z=2)
                    prow = C("posrow").rearrange("p (z i) -> p z i", z=2)
                    for z in range(2):
                        for h, (f, a) in enumerate(HEADS):
                            fn(Dm[:, z, a, f, :], diff[:, z, :], ACT.Exp, scale=lg[:, 4 * z + h:4 * z + h + 1])
                        for f in range(2):
                            fn(qdec[:, z, f, :], prow[:, z, :], ACT.Exp, scale=lg[:, 8 + 2 * z + f:9 + 2 * z + f])
                    fn(small[:, 160:168], small[:, 160:168], ACT.Exp)
                    fn(small[:, 168:172], lg[:, 8:12], ACT.Exp, scale=float(P)).then_inc(dec_ready, 1)
                    for t in range(NT):
                        act.wait_ge(rt_done, t + 1)
                        b = (t % 2) * BANK
                        fn(FM[:, :, t * P:(t + 1) * P], tiles(ps[:, b:b + BANK], 4), ACT.Copy).then_inc(rt_evac, 1)
                    for z in range(2):
                        state_in(G_D, z)
                        state_out(G_D, z)
                    act.wait_ge(unit_evac, EV(U_D + 3))
                    head_rstd(2)
                    fn(Gd, Gd, ACT.Silu).then_inc(act_gate, 1)
                    concat(3)

                    act.dma_start(rpb, I["rpb"][l]).then_inc(rpb_loaded, 16)
                    act.wait_ge(unit_evac, EV(U_B + 2))
                    act.dma_start(O["nak"][l], knew).then_inc(na_out, 16)
                    act.dma_start(O["nav"][l], Vn[:, 0:GW]).then_inc(na_out, 16)
                    ln_exp()

                    def probs(b):
                        n = P if b < NH else NTOK
                        act.wait_ge(na_max, b + 1)
                        fn(SB[b % 2][:, 0:n], SB[b % 2][:, 0:n], ACT.Exp, bias=small[:, 176 + b:177 + b],
                           accum_out=small[:, 200 + b:201 + b]).then_inc(na_e, 1)

                    def turned(b):
                        n = P if b < NH else NTOK
                        act.wait_ge(na_pt, b + 1)
                        if b:
                            act.wait_ge(na_o, b)
                        for a in range(0, n, BANK):
                            w = min(BANK, n - a)
                            last = fn(PT[:, a:a + w], ps[:, 4 * BANK + a:4 * BANK + a + w], ACT.Copy)
                        last.then_inc(na_ptc, 1)

                    probs(0)
                    probs(1)
                    for b in range(NT * NH):
                        turned(b)
                        if b + 2 < NT * NH:
                            probs(b + 2)
                        if b in CAT_TURNS:
                            cat_upper(b - CAT_TURNS[0])
                    cat_upper(6)
                    cat_upper(7)

                    act.wait_ge(na_out, 32)
                    norm(3, U_OUT, 2)
                    norm(4, 0, 1)
                    modulate(2)
                    ffn(2, 1)
                    norm(5, U_ALL - KT, 1)

                @block.vector
                def _(dve):
                    V = nc.vector
                    dve.sem_inc(unit_evac, 2)
                    dve.sem_inc(a_lo, 1)
                    V.memset(small[:, 0:255], 0.0)
                    V.memset(small[:, 255:256], EPS)
                    dve.wait_ge(par_loaded, 16)
                    dve.wait_ge(const_loaded, 16)
                    bmod = W("bmod")
                    normw = tiles(W("normw"), 6)

                    def mod_rows(n, i2):
                        dve.wait_ge(unit_done, i2 * 2 + UD(n))
                        V.tensor_copy(mrow[0:2, :], ps[0:2, half(n):half(n) + 256]).then_inc(mrow_ready, 1)

                    def mod_cols(n, q, i1=0):
                        dve.wait_ge(mtr_done, i1 + (q + 1))
                        m = i1 * 2 + 2 * q
                        V.tensor_tensor(modS[:, bass.ds(m, 2), :], tiles(ps[:, half(n) + BANK:half(n) + BANK + 4], 2),
                                        par[:, bass.ds(m + PARAMS["bmod"][0], 2)]
                                        .unsqueeze(2).to_broadcast([P, 2, 2]), ALU.add).then_inc(unit_evac, 1)

                    def mod_gates(s):
                        m0 = 3 * KT * s
                        g = normw[:, 2 * s + 1, :].unsqueeze(2).to_broadcast([P, KT, 2])
                        V.scalar_tensor_tensor(gg_all[:, s], modS[:, m0 + 2 * KT:m0 + 3 * KT, :],
                                               1.0 if s == 1 else 0.5, g, ALU.mult, ALU.mult).then_inc(gate_ready, 1)

                    def mod_scales(s):
                        m0 = 3 * KT * s
                        g = normw[:, 2 * s, :].unsqueeze(2).to_broadcast([P, KT, 2])
                        V.scalar_tensor_tensor(gs_all[:, s], modS[:, m0 + KT:m0 + 2 * KT, :], 1.0, g,
                                               ALU.add, ALU.mult).then_inc(mod_ready, 1)

                    def add_square(v, k, i=0):
                        dve.wait_ge(sq_ready, i * 2 + (KT * v + k + 1))
                        sq = sqb if v else yT[:, k, :]
                        if k == 0:
                            last = V.tensor_copy(rstd[:, :], sq)
                        else:
                            dve.wait_ge(acc_add, i * 2 + (KT * ((v + 1) // 2) + k))
                            last = V.tensor_tensor(rstd[:, :], rstd[:, :], sq, ALU.add)
                        last.then_inc(acc_add, 1)

                    def norm_step(s, k):
                        parts = tuple(enumerate((slice(0, SEQ), slice(SEQ, NTOK))))
                        if k < KT:
                            for c, cols in parts:
                                last = V.scalar_tensor_tensor(yT[:, k, cols], xT[:, k, cols], gs_all[:, s, k, c:c + 1],
                                                              rstd[:, cols], ALU.mult, ALU.mult)
                            last.then_inc(hmul_ready, 1)
                        if k:
                            m = k - 1
                            dve.wait_ge(h_hi, KT * s + m + 1)
                            for c, cols in parts:
                                last = V.scalar_tensor_tensor(h2[:, 1, m, cols], yT[:, m, cols],
                                                              modS[:, 3 * KT * s + m, c:c + 1],
                                                              h2[:, 0, m, cols].bitcast(FP), ALU.add, ALU.subtract)
                            last.then_inc(h_ready, 1)

                    def norm_in(s):
                        dve.wait_ge(mod_ready, s + 1)
                        dve.wait_ge(rstd_ready, 2 * s + 1)
                        for k in range(KT + 1):
                            norm_step(s, k)

                    def norm_out(s):
                        dve.wait_ge(rstd_ready, 2 * s + 2)
                        for k in range(KT + 1):
                            if k < KT:
                                dve.wait_ge(y_scaled, KT * s + k + 1)
                                V.tensor_tensor(yT[:, k, :], yT[:, k, :], rstd[:, :], ALU.mult).then_inc(y_norm, 1)
                            if k:
                                dve.wait_ge(y_norm, KT * s + k)
                                V.tensor_tensor(xT[:, k - 1, :], xT[:, k - 1, :], yT[:, k - 1, :], ALU.add)\
                                    .then_inc(x_ready, 1)

                    def ffn(s, j):
                        lo, hi = (a2[:, p].rearrange("p k n -> p (k n)") for p in (1, 0))

                        def one(n, i2, at, count, per):
                            dve.wait_ge(silu_done, i2 * per + (count + 1))
                            V.tensor_tensor(halves(rstd[:, :]), halves(rstd[:, :]), acc(half(n) + 2 * BANK), ALU.mult)\
                                .then_inc(unit_evac, 1)
                            dve.wait_ge(a_hi, i2 * per + (count + 1))
                            V.tensor_tensor(lo[:, at], rstd[:, :], hi[:, at].bitcast(FP), ALU.subtract)\
                                .then_inc(a_lo, 1)

                        def down(n, i2, dst, grp):
                            dve.wait_ge(unit_done, i2 * 2 + UD(n))
                            dst = dst.rearrange("p (a n) -> p a n", a=2)
                            if grp == 0:
                                last = V.tensor_copy(dst, acc(half(n)))
                            else:
                                last = V.tensor_tensor(dst, dst, acc(half(n)), ALU.add)
                            last.then_inc(unit_evac, 1)

                        y0 = ARENA_W - KT * NTOK
                        for grp in range(2):
                            n = U_FFN[s] + grp * GRP_U[s]
                            c = j * FT + grp * GF_T
                            q = MOD_U * (1 + grp)
                            if s == 0:
                                mod_rows(n, 0)
                                with dve.Fori(0, GF_T) as i:
                                    mod_cols(n, q, i)
                                    one(n + 1, i, bass.ds(i * NTOK, NTOK), c, 1)
                                    mod_rows(n + 2, i)
                                mod_cols(n + 2 * GF_T, q + GF_T)
                                n += GF_T + MOD_U
                            else:
                                with dve.Fori(0, GF_T // 2) as i:
                                    for u in range(2):
                                        one(n + u, i, bass.ds(i * (2 * NTOK) + u * NTOK, NTOK), c + u, 2)
                                one(n + GF_T - 1, 0, slice((GF_T - 1) * NTOK, GF_T * NTOK), c + GF_T - 1, 0)
                                n += GF_T
                            for u in range(2):
                                down(n + u, 0, yT[:, u, :], grp)
                            if grp:
                                add_square(2 * s + 1, 0)
                            with dve.Fori(0, KT // 2 - 1) as i:
                                for u in range(2):
                                    down(n + 2 + u, i, arena[:, bass.ds(i * (2 * NTOK) + (y0 + (2 + u) * NTOK), NTOK)],
                                         grp)
                                    if grp:
                                        add_square(2 * s + 1, 1 + u, i)
                        add_square(2 * s + 1, KT - 1)

                    def evac_features(n, dst, scale=None):
                        dve.wait_ge(unit_done, UD(n))
                        src = ps[:, half(n):half(n) + 4 * BANK].rearrange("p (a n) -> p a n", a=4)[:, :, 0:HALF]
                        dst = dst.rearrange("p k n -> p (k n)").rearrange("p (a n) -> p a n", a=4)
                        if scale is None:
                            last = V.tensor_copy(dst, src)
                        else:
                            last = V.tensor_scalar(dst, src, scale, None, ALU.mult)
                        last.then_inc(unit_evac, 1)

                    def evac_tokens(n, dst, scale=1.0):
                        dve.wait_ge(unit_done, UD(n))
                        src = ps[:, half(n):half(n) + NT * GW]
                        if len(dst.shape) == 4:
                            src = src.rearrange("p (t h e) -> p t h e", t=NT, h=NH)
                        else:
                            src = tiles(src, NT)
                        V.tensor_scalar(dst, src, scale, None, ALU.mult).then_inc(unit_evac, 1)

                    def scan_group(g, z, bmask, decay):
                        def attention(t):
                            dve.wait_ge(p_done, R(g, z, t))
                            b = (2 + 2 * (t % 2)) * BANK
                            both = ps[:, b:b + 2 * BANK].rearrange("p (a q f i) -> p a q f i", a=2, q=2, f=2)
                            pr, lw = both[:, :, 0, :, :], both[:, :, 1, :, :]
                            if t >= 2:
                                dve.wait_ge(o_done, R(g, z, t - 2))
                            elif Z(g, z) > 1:
                                dve.wait_ge(o_done, R(g, z, -1))
                            if g == G_C:
                                for f, a in HEADS:
                                    last = V.scalar_tensor_tensor(
                                        WL[t % 2][:, a, f, :], lw[:, a, f, :],
                                        GT[:, t, 0, z * 32 + 2 * f + a:z * 32 + 2 * f + a + 1],
                                        anti[:, z, :], ALU.add, ALU.add)
                                last.then_inc(wl_done, 1)
                                if t:
                                    output(t - 1)
                                dve.wait_ge(w_ready, z * NT + t + 1)
                                m = WL[t % 2]
                            elif g == G_A:
                                m = causal[:, z, :].unsqueeze(1).unsqueeze(1).to_broadcast([P, 2, 2, P])
                            else:
                                m = Dm[:, z]
                            V.tensor_tensor(Asb[t % 2], pr, m, ALU.mult).then_inc(a_done, 1)

                        def output(t):
                            dve.wait_ge(o_done, R(g, z, t))
                            o = (6 + t % 2) * BANK
                            if g == G_C:
                                out = tiles(ps[:, o:o + 2 * SW], NH)
                                if t == 0:
                                    V.tensor_copy(CT[:, t], out).then_inc(ot_done, 1)
                                else:
                                    inter = tiles(ps[:, (t % 2) * BANK:(t % 2) * BANK + 2 * SW], NH)
                                    V.tensor_tensor(CT[:, t], inter,
                                                    GT[:, t, 1, z * 32:z * 32 + NH].unsqueeze(2)
                                                    .to_broadcast([P, NH, HD + 1]), ALU.mult)
                                    dve.drain()
                                    V.tensor_tensor(CT[:, t], CT[:, t], out, ALU.add).then_inc(ot_done, 1)
                            elif z == 0:
                                V.tensor_copy(OT[:, t, :], ps[:, o:o + GW]).then_inc(ot_done, 1)
                            else:
                                V.tensor_tensor(OT[:, t, :], OT[:, t, :], ps[:, o:o + GW], ALU.add)\
                                    .then_inc(ot_done, 1)

                        w = SW if g == G_C else P
                        if Z(g, z) > 1:
                            dve.wait_ge(st_out, 16 * (Z(g, z) - 1))
                        for t in range(NT):
                            dve.wait_ge(u_done, R(g, z, t))
                            u = tiles(ps[:, (t % 2) * BANK:(t % 2) * BANK + 2 * w], 2)
                            if g == G_A:
                                for f in range(2):
                                    last = V.scalar_tensor_tensor(Tst[:, t, f, 0:w], u[:, f, :],
                                                                  small[:, 106 + f * NT + t:107 + f * NT + t],
                                                                  bmask, ALU.mult, ALU.mult)
                            else:
                                last = V.tensor_tensor(Tst[:, t, :, 0:w], u,
                                                       bmask.unsqueeze(1).to_broadcast([P, 2, w]), ALU.mult)
                            last.then_inc(t_done, 1)
                        if g != G_C:
                            attention(0)
                        o = order(z)
                        for a, b in zip(o[:-1], o[1:]):
                            dve.drain()
                            if a == o[0]:
                                dve.wait_ge(init_loaded, 16 * Z(g, z))
                            for f in range(2):
                                last = V.scalar_tensor_tensor(Sin[:, b, f, 0:w], Sin[:, a, f, 0:w], decay(f, a),
                                                              Tst[:, a, f, 0:w], ALU.mult, ALU.add)
                        if g == G_A:
                            dve.drain()
                            for f in range(2):
                                last = V.tensor_tensor(Tst[:, 1:NT, f, 0:w], Sin[:, 1:NT, f, 0:w],
                                                       small[:, 117 + f * NT:121 + f * NT].unsqueeze(2)
                                                       .to_broadcast([P, NT - 1, w]), ALU.mult)
                        last.then_inc(s_ready, 1)

                        for t in range(NT):
                            if t or g == G_C:
                                attention(t)
                            if t and g != G_C:
                                output(t - 1)
                        output(NT - 1)

                    def cat_lower(k):
                        dve.wait_ge(cat_hi, k + 1)
                        V.tensor_tensor(h2[:, 1, k, :], catP[k // 2][:, k % 2, :], h2[:, 0, k, :].bitcast(FP),
                                        ALU.subtract).then_inc(cat_split, 1)

                    def head_norm(c, w, gate, centred):
                        heads = [P, NT * NH, HD]
                        sq = Tq
                        dve.drain()
                        if centred:
                            V.reduce_sum(small[:, 64:84], OTh, axis=AXX)
                            dve.drain()
                            V.tensor_scalar(small[:, 64:84], small[:, 64:84], 1.0 / HD, None, ALU.mult)
                            dve.drain()
                            V.tensor_tensor(OTh, OTh, small[:, 64:84].unsqueeze(2).to_broadcast(heads), ALU.subtract)
                            dve.drain()
                        dve.wait_ge(st_out, 16 * 2 * (c + 1))
                        V.tensor_tensor(sq, OTh, OTh, ALU.mult)
                        dve.drain()
                        V.reduce_sum(small[:, 64:84], sq, axis=AXX).then_inc(nrm_in, 1)
                        dve.wait_ge(nrm_out, c)
                        V.tensor_tensor(OTh, OTh, small[:, 64:84].unsqueeze(2).to_broadcast(heads), ALU.mult)
                        dve.drain()
                        V.tensor_tensor(OTh, OTh, w.unsqueeze(1).to_broadcast(heads), ALU.mult)
                        dve.drain()
                        dve.wait_ge(act_gate, c + 1)
                        V.tensor_tensor(OTh, OTh, gate.rearrange("p (a e) -> p a e", e=HD), ALU.mult)\
                            .then_inc(fin_ready, 1)

                    Tq = area(T0, 1280).rearrange("p (a e) -> p a e", e=HD)

                    mod_rows(0, 0)
                    for a, b in ((0, 1), (1, 2), (2, 3)):
                        with dve.Fori(0, b - a) as i:
                            for u in range(2):
                                mod_cols(2 * a + u, 2 * a + u, i * 2)
                                mod_rows(2 * a + 1 + u, i)
                        if a < 2:
                            for k in range(a * KT // 2, (a + 1) * KT // 2):
                                add_square(0, k)
                    for n in range(6, 8):
                        mod_cols(n, n)
                        mod_rows(n + 1, 0)
                    dve.drain()
                    mod_scales(0)
                    dve.wait_ge(mod_ready, 1)
                    dve.wait_ge(rstd_ready, 1)
                    for n in range(8, MOD_U):
                        for k in (2 * n - 16, 2 * n - 15):
                            norm_step(0, k)
                        mod_cols(n, n)
                        if n + 1 < MOD_U:
                            mod_rows(n + 1, 0)
                    norm_step(0, KT)
                    dve.drain()
                    mod_gates(0)
                    ffn(0, 0)
                    dve.drain()
                    mod_scales(1)
                    mod_scales(2)
                    mod_gates(1)
                    mod_gates(2)
                    norm_out(0)
                    norm_in(1)

                    dve.wait_ge(unit_done, UD(U_GATES))
                    b0 = half(U_GATES)
                    gb = W("gb")
                    V.memset(GY[64:128, :], 0.0)
                    V.memset(GM[0:64, :], 0.0)
                    V.memset(GF[0:64, :], 0.0)
                    V.tensor_scalar(halves(GX[0:96, :]), acc(b0)[0:96], gb[0:96, 0:1], None, ALU.add)
                    V.tensor_scalar(halves(GY[0:64, :]), acc(b0 + 2 * BANK)[0:64], gb[0:64, 1:2], None, ALU.add)\
                        .then_inc(unit_evac, 1)
                    dve.drain()
                    dve.sem_inc(gate_pre, 1)
                    V.memset(area(TM0, 1300), 1.0)
                    evac_features(U_C, FM[:, 0:2, :], QSCALE)
                    evac_features(U_C + 1, FM[:, 2:4, :])
                    evac_tokens(U_C + 2, Vc[:, :, :, 0:HD])
                    evac_tokens(U_C + 3, tiles(Oc, NT))
                    dve.wait_ge(gate_sp, 1)
                    V.tensor_scalar(GY[0:64, :], GY[0:64, :], 0.0, None, ALU.min)
                    dve.drain()
                    V.tensor_tensor(GY[0:64, :], GY[0:64, :], GK[0:64, :], ALU.subtract)
                    dve.drain()
                    m0 = W("m0")
                    carry = C("carry")
                    for z, rows in enumerate((slice(0, NH), slice(32, 32 + NH))):
                        for cols, init in (((0, SEQ), 0.0), ((SEQ, NTOK), m0[rows, :])):
                            s = slice(*cols) if z == 0 else slice(cols[1] - 1, cols[0] - 1 if cols[0] else None, -1)
                            V.tensor_tensor_scan(out=GM[rows, s], data0=GY[rows, s], data1=GX[rows, s], initial=init,
                                                 op0=ALU.add, op1=ALU.max)
                        s = slice(None) if z == 0 else slice(None, None, -1)
                        V.tensor_tensor_scan(out=GF[rows, s], data0=carry[rows, :], data1=GY[rows, s], initial=0.0,
                                             op0=ALU.mult, op1=ALU.add)
                    dve.drain()
                    mlast, mprev, rlast, wprev = (small[0:64, a:a + NT] for a in (0, 5, 10, 16))
                    r0, r1 = slice(0, NH), slice(32, 32 + NH)
                    V.tensor_copy(mlast[r0], GM[r0, P - 1::P])
                    V.tensor_copy(small[32:36, 0:NT], GM[r1, 0::P])
                    V.tensor_copy(small[r0, 6:7], m0[r0])
                    V.tensor_copy(small[r1, 9:10], m0[r1])
                    V.tensor_copy(small[r0, 7:10], GM[r0, 2 * P - 1:4 * P:P])
                    V.tensor_copy(small[r1, 6:9], GM[r1, 2 * P:4 * P + 1:P])
                    V.tensor_tensor(GY[0:64, :], GF[0:64, :], GM[0:64, :], ALU.subtract)
                    V.tensor_tensor(GX[0:64, :], GX[0:64, :], GF[0:64, :], ALU.subtract)
                    dve.drain()
                    V.tensor_copy(rlast[r0], GY[r0, P - 1::P])
                    V.tensor_copy(small[32:36, 10:10 + NT], GY[r1, 0::P])
                    dve.drain()
                    V.tensor_tensor(tiles(GF[0:64, :], NT), tiles(GY[0:64, :], NT),
                                    mprev.unsqueeze(2).to_broadcast([64, NT, P]), ALU.add)
                    V.tensor_tensor(tiles(GK[0:64, :], NT), tiles(GX[0:64, :], NT),
                                    rlast.unsqueeze(2).to_broadcast([64, NT, P]), ALU.add)
                    V.tensor_tensor(wprev, rlast, mprev, ALU.add).then_inc(gate_log, 1)
                    dve.wait_ge(gate_cols, 1)
                    keys = ps[:, 4 * BANK:4 * BANK + 1280].rearrange("p (t h e) -> p t h e", t=NT, h=NH)
                    for z in range(2):
                        V.tensor_tensor(ktC[z].rearrange("p (t h e) -> p t h e", t=NT, h=NH), keys,
                                        GT[:, :, 3, z * 32:z * 32 + NH].unsqueeze(3).to_broadcast([P, NT, NH, HD]),
                                        ALU.mult).then_inc(kt_ready, 1)
                    for z in range(2):
                        scan_group(G_C, z, C("blockn"),
                                   lambda f, t: small[:, 24 + (2 * z + f) * NT + t:25 + (2 * z + f) * NT + t])
                        dve.drain()
                        den = CT[:, :, :, HD]
                        d = small[:, 44:64]
                        dt = tiles(d, NT)
                        V.scalar_tensor_tensor(dt, den, -1.0, den, ALU.mult, ALU.max)
                        dve.drain()
                        V.tensor_tensor(dt, dt, GT[:, :, 2, z * 32:z * 32 + NH], ALU.max)
                        dve.drain()
                        V.reciprocal(d, d)
                        dve.drain()
                        num, inv = CT[:, :, :, 0:HD], dt.unsqueeze(3).to_broadcast([P, NT, NH, HD])
                        o4 = OT.rearrange("p t (h e) -> p t h e", h=NH)
                        if z == 0:
                            V.tensor_tensor(o4, num, inv, ALU.mult)
                        else:
                            V.tensor_tensor(num, num, inv, ALU.mult)
                            dve.drain()
                            V.tensor_tensor(o4, o4, num, ALU.add)
                        dve.drain()
                    dve.wait_ge(act_gate, 1)
                    V.tensor_tensor(OT, OT, tiles(Oc, NT), ALU.mult).then_inc(fin_ready, 1)

                    evac_features(U_A + 1, FM[:, 0:2, :], QSCALE)
                    evac_features(U_A + 2, FM[:, 2:4, :])
                    evac_tokens(U_A + 3, tiles(Ga, NT))
                    for z in range(2):
                        dve.wait_ge(asp_done, z + 1)
                        V.scalar_tensor_tensor(Wk, QM.rearrange("p f n -> p (f n)"), 0.0, Wk, ALU.min, ALU.subtract)
                        dve.drain()
                        s = slice(None) if z == 0 else slice(None, None, -1)
                        for f in range(2):
                            V.tensor_tensor_scan(out=tiles(Bk, 2)[:, f, s], data0=carry, data1=tiles(Wk, 2)[:, f, s],
                                                 initial=0.0, op0=ALU.mult, op1=ALU.add)
                        dve.drain()
                        b3 = tiles(Bk, 2 * NT)
                        mid, end = (b3[:, :, 63], b3[:, :, P - 1]) if z == 0 else (b3[:, :, 64], b3[:, :, 0])
                        V.tensor_tensor(tiles(Wk, 2 * NT), b3, mid.unsqueeze(2).to_broadcast([P, 2 * NT, P]),
                                        ALU.subtract)
                        V.tensor_copy(small[:, 96:106], end)
                        V.tensor_tensor(small[:, 106:116], end, mid, ALU.subtract)
                        V.tensor_copy(small[:, 116:126], mid).then_inc(ad_ready, 1)
                        dve.wait_ge(ae_ready, z + 1)
                        V.tensor_tensor(QM, QM, FM[:, 0:2, :], ALU.mult)
                        V.tensor_tensor(KM, KM, FM[:, 2:4, :], ALU.mult).then_inc(aqk_ready, 1)
                        scan_group(G_A, z, C("block"),
                                   lambda f, t: small[:, 96 + f * NT + t:97 + f * NT + t])
                    head_norm(1, W("gnw"), Ga, False)

                    dve.sem_inc(lg_ready, 1)
                    dve.drain()
                    rope = C("rope").rearrange("p (t s e) -> p t s e", t=NT, s=2)
                    for t in range(NT):
                        x8 = tiles(RQK[:, t, :], 2 * NH)
                        V.tensor_tensor(tiles(rot1[:, t, :], 2 * NH), x8,
                                        rope[:, t, 0, :].unsqueeze(1).to_broadcast([P, 2 * NH, HD]), ALU.mult)
                        x5 = RQK[:, t, :].rearrange("p (h a b e) -> p h a b e", h=2 * NH, a=2, b=2)
                        r5 = rot2[:, t, :].rearrange("p (h a b e) -> p h a b e", h=2 * NH, a=2, b=2)
                        s5 = rope[:, t, 1, :].rearrange("p (a b e) -> p a b e", a=2, b=2)
                        for b in range(2):
                            V.tensor_tensor(r5[:, :, :, b, :], x5[:, :, :, 1 - b, :],
                                            s5[:, :, b, :].unsqueeze(1).to_broadcast([P, 2 * NH, 2, 16]), ALU.mult)
                    dve.drain()
                    V.tensor_tensor(RQK, rot1, rot2, ALU.add).then_inc(rot_ready, 1)
                    dve.wait_ge(lg_sp, 1)
                    lg = small[:, 128:140]
                    V.tensor_scalar(lg, W("rd"), 0.0, None, ALU.min)
                    dve.drain()
                    V.tensor_tensor(lg, lg, small[:, 144:156], ALU.subtract)
                    dve.drain()
                    pc = C("poscol")
                    for z in range(2):
                        last = V.tensor_scalar(small[:, 160 + 4 * z:164 + 4 * z], lg[:, 4 * z:4 * z + 4],
                                               pc[:, z:z + 1], None, ALU.mult)
                    last.then_inc(lg_ready, 1)
                    evac_tokens(U_D + 2, tiles(Vd, NT))
                    evac_tokens(U_D + 3, tiles(Gd, NT))
                    dve.wait_ge(dec_ready, 1)
                    for z in range(2):
                        if z:
                            dve.wait_ge(o_done, R(G_D, 0, NT - 1))
                        V.tensor_tensor(ktD.rearrange("p (t h e) -> p t h e", t=NT, h=NH),
                                        RQK[:, :, GW:2 * GW].rearrange("p t (h e) -> p t h e", h=NH),
                                        small[:, 160 + 4 * z:164 + 4 * z].unsqueeze(1).unsqueeze(3)
                                        .to_broadcast([P, NT, NH, HD]), ALU.mult).then_inc(kt_ready, 1)
                        if z == 0:
                            dm = Dm.rearrange("p z a f i -> p z (a f) i")
                            V.tensor_tensor(dm, dm, causal.unsqueeze(2).to_broadcast([P, 2, 4, P]), ALU.mult)
                            dve.wait_ge(rt_evac, NT)
                        V.tensor_tensor(QD.rearrange("p f (t i) -> p f t i", t=NT),
                                        FM[:, 0:2, :].rearrange("p f (t i) -> p f t i", t=NT),
                                        qdec[:, z].unsqueeze(2).to_broadcast([P, 2, NT, P]), ALU.mult)\
                            .then_inc(qd_ready, 1)
                        scan_group(G_D, z, C("block"), lambda f, t: small[:, 168 + 2 * z + f:169 + 2 * z + f])
                    head_norm(2, W("rnw"), Gd, True)

                    kc = tiles(W("kc"), 2)
                    V.tensor_copy(kc2[:, 0], kc)

                    def evac_split(n, f, scale):
                        dve.wait_ge(unit_done, UD(n))
                        src = ps[:, half(n):half(n) + 4 * BANK].rearrange("p (a n) -> p a n", a=4)[:, :, 0:HALF]
                        hi, lo = (qk2[:, p, f:f + 2, :].rearrange("p k n -> p (k n)")
                                  .rearrange("p (a n) -> p a n", a=4) for p in range(2))
                        V.tensor_scalar(hi, src, scale, None, ALU.mult)
                        if f:
                            V.tensor_copy(knew, src[:, 0::2, 0:P])
                        dve.drain()
                        V.scalar_tensor_tensor(lo, src, scale, hi.bitcast(FP), ALU.mult, ALU.subtract)\
                            .then_inc(unit_evac, 1)

                    evac_split(U_B, 0, QSCALE)
                    V.tensor_tensor(kc2[:, 1], kc, kc2[:, 0].bitcast(FP), ALU.subtract)
                    dve.wait_ge(rpb_loaded, 16)
                    r3 = rpb.rearrange("p (m c) -> p m c", c=HD)
                    V.tensor_tensor(r3, r3, C("namask").unsqueeze(1).to_broadcast([P, 14 * NH, HD]), ALU.add)
                    evac_split(U_B + 1, 2, 1.0)
                    evac_tokens(U_B + 2, tiles(Vn, NT))
                    dve.drain()

                    def na_in(b):
                        t, h = b // NH, b % NH
                        c = (h % 2) * 2 * BANK
                        s = SB[b % 2]
                        dve.wait_ge(na_s, b + 1)
                        if b >= 2:
                            dve.wait_ge(na_pt, b - 1)
                        if t == 0:
                            V.tensor_copy(s[:, 0:P], ps[:, c:c + P]).then_inc(na_read, 1)
                            n = P
                        else:
                            m = (h * 14 + 6 - 2 * (t - 1)) * HD
                            V.tensor_tensor(s[:, 0:DEC], ps[:, c:c + DEC], rpb[:, m:m + DEC], ALU.add)
                            V.tensor_copy(s[:, DEC:NTOK], ps[:, c + BANK:c + BANK + P]).then_inc(na_read, 1)
                            n = NTOK
                        dve.drain()
                        V.tensor_reduce(out=small[:, 176 + b:177 + b], in_=s[:, 0:n], op=ALU.max, axis=AXX,
                                        negate=True).then_inc(na_max, 1)

                    def na_norm(b):
                        sb, n = SB[b % 2], P if b < NH else NTOK
                        dve.wait_ge(na_e, b + 1)
                        V.reciprocal(small[:, 220 + b:221 + b], small[:, 200 + b:201 + b])
                        dve.drain()
                        V.tensor_scalar(sb[:, 0:n], sb[:, 0:n], small[:, 220 + b:221 + b], None, ALU.mult)\
                            .then_inc(na_n, 1)

                    def na_outp(b):
                        t, h = b // NH, b % NH
                        rows = slice(h % 2 * HD, (h % 2 + 1) * HD)
                        dve.wait_ge(na_o, b + 1)
                        o = (6 + b % 2) * BANK
                        V.tensor_copy(catP[3][rows, h // 2, t * P:(t + 1) * P], ps[rows, o:o + P]).then_inc(na_oc, 1)

                    na_in(0)
                    na_in(1)
                    na_norm(0)
                    for b in range(NT * NH):
                        if b + 1 < NT * NH:
                            na_norm(b + 1)
                        if b + 2 < NT * NH:
                            na_in(b + 2)
                        na_outp(b)
                        if b in CAT_TURNS:
                            cat_lower(b - CAT_TURNS[0])
                    cat_lower(6)
                    cat_lower(7)
                    for q in range(4):
                        if q < 3:
                            evac_features(U_OUT + q, yT[:, 2 * q:2 * q + 2, :])
                        else:
                            b = half(U_OUT + q)
                            dve.wait_ge(out_part, 1)
                            V.tensor_copy(halves(yT[:, 2 * q, :]), acc(b)).then_inc(out_evac, 1)
                        for k in range(max(0, 2 * q - 2), 2 * q):
                            add_square(3, k)
                    dve.wait_ge(unit_done, UD(U_OUT + 3))
                    V.tensor_copy(halves(yT[:, KT - 1, :]), acc(b + 2 * BANK)).then_inc(unit_evac, 1)
                    for k in (KT - 2, KT - 1):
                        add_square(3, k)
                    norm_out(1)
                    norm_in(2)
                    ffn(2, 1)
                    norm_out(2)

            nums = sorted(s.num for s in sems)
            assert nums == list(range(nums[0], nums[-1] + 1))
            nc.sync.sem_clear(range(nums[0], nums[-1] + 1))
            nc.all_engine_barrier()

        with nc.Block() as block:
            @block.sync
            def _(sp):
                sp.dma_start(O["y"], xT).then_inc(y_out, 16)
                sp.wait_ge(y_out, 16)


def constants():
    import numpy as np

    c = np.zeros((P, CONST_W), np.float32)

    def put(name, a):
        at, w = CONSTS[name]
        c[:, at:at + w] = np.asarray(a, np.float64).reshape(-1, w)

    i = np.arange(P)
    put("ident", np.eye(P))
    put("ones", np.ones((P, P)))
    tok = np.arange(DEC)
    inv = 10000.0 ** (-np.arange(16, dtype=np.float32) / 16)
    ang = np.stack([(tok // GRID_W)[:, None] * inv, (tok % GRID_W)[:, None] * inv], 1)
    cs = np.concatenate([np.ones((SEQ, 2, 16)), np.cos(ang.astype(np.float32))])
    sn = np.concatenate([np.zeros((SEQ, 2, 16)), np.sin(ang.astype(np.float32))])
    table = np.stack([np.stack([cs, cs], 2), np.stack([-sn, sn], 2)], 1)
    put("rope", table.reshape(NT, P, 2 * HD).transpose(1, 0, 2))
    q, k = np.arange(GRID_W)[:, None], np.arange(GRID_W)[None]
    lo = np.clip(q - WIN // 2, 0, GRID_W - WIN)
    put("namask", np.tile(np.where((k >= lo) & (k < lo + WIN), 0.0, NEG), (2, 1)))
    j = i[:, None]
    causal = np.stack([i[None] >= j, i[None] <= j], 1)
    put("causal", causal)
    put("anti", np.where(causal, 0.0, NEG))
    put("block", (i[:, None] // HD == i[None] // HD))
    put("blockn", (i[:, None] // HD == np.arange(SW)[None] // (HD + 1)))
    put("diff", np.stack([np.maximum(i[None] - j, 0), np.maximum(j - i[None], 0)], 1))
    put("posrow", np.broadcast_to(np.stack([i + 1, P - i]), (P, 2, P)))
    put("poscol", np.stack([P - 1 - i, i], 1))
    put("carry", np.broadcast_to(np.arange(NTOK) % P != 0, (P, NTOK)))
    return c


def lay_out(v):
    import numpy as np

    f = np.float32

    def blocks(w, cols):
        n = w.shape[-1] // cols
        return np.ascontiguousarray(w.reshape(DEPTH, KT, P, n, cols).transpose(0, 3, 2, 1, 4)).reshape(
            DEPTH, n, P, KT * cols)

    d = {"const": constants()}
    x = np.concatenate([v["x_prompt"][0], v["x_sample"][0]])
    d["x"] = np.ascontiguousarray(x.T.reshape(KT, P, NTOK).transpose(1, 0, 2))
    d["cond"] = np.ascontiguousarray(np.stack([v["c_ctx"], v["c"][0]], 1).reshape(KT, P, 2).transpose(1, 0, 2))
    d["w_mod"] = blocks(v["w_mod"], 256)
    w1, w3 = (v[n].reshape(DEPTH, 2, KT, P, FT, P).transpose(0, 1, 4, 3, 2, 5) for n in ("ffn_w1", "ffn_w3"))
    d["w13"] = np.stack([w1, w3], 4).reshape(DEPTH, 2 * FT, P, 2 * DM)
    d["w2"] = np.ascontiguousarray(v["ffn_w2"].reshape(DEPTH, 2, 2, GF_T, P, KT, P).transpose(
        0, 1, 2, 5, 4, 3, 6)).reshape(DEPTH, 4 * KT, P, GF_T * P)
    names = ["gq", "gk", "gv", "gg", "ga", "nq", "nk", "nv", "mq", "mk", "mv", "mo", "mi", "mf", "rq", "rk", "rv", "rg"]
    sizes = [GW] * 4 + [32] + [GW] * 7 + [8, 8] + [GW] * 4
    at = np.concatenate([[0], np.cumsum(sizes)])
    col = {n: v["w_in"][:, :, at[i]:at[i + 1]] for i, n in enumerate(names)}
    d["w_in"] = blocks(np.concatenate([col[n] for n in (
        "mq", "mk", "mv", "mo", "gv", "gq", "gk", "gg", "rq", "rk", "rv", "rg", "nq", "nk", "nv")], -1), 256)
    g = np.zeros((DEPTH, DM, 160), f)
    g[:, :, 64:96] = col["ga"]
    for z in range(2):
        g[:, :, z * 32:z * 32 + NH] = col["mi"][:, :, z * NH:(z + 1) * NH]
        g[:, :, 96 + z * 32:96 + z * 32 + NH] = col["mf"][:, :, z * NH:(z + 1) * NH]
    d["w_gates"] = blocks(g, 160)[:, 0]
    d["w_out"] = blocks(v["w_out"].reshape(DEPTH, 4, GW, DM)[:, [2, 0, 3, 1]].reshape(DEPTH, DM, DM), 256)

    p = np.zeros((DEPTH, P, PARAM_W), f)

    def part(name):
        a, w = PARAMS[name]
        return p[:, :, a:a + w]

    part("bmod")[:] = v["b_mod"].reshape(DEPTH, 9 * KT, P).transpose(0, 2, 1)
    part("normw")[:] = v["norm_w"].reshape(DEPTH, 6 * KT, P).transpose(0, 2, 1)
    part("ba")[:] = v["gla_b_a"].reshape(DEPTH, 4, P).transpose(0, 2, 1)
    d["wa2"] = wa2 = np.zeros((DEPTH, 32, 4 * P), f)
    for z in range(2):
        part("gb")[:, z * 32:z * 32 + NH, 0] = v["mlstm_b_i"][:, z]
        part("gb")[:, z * 32:z * 32 + NH, 1] = v["mlstm_b_f"][:, z]
        part("m0")[:, z * 32:z * 32 + NH, 0] = v["state_mlstm_m"][0, :, z]
        wa2[:, z * 16:(z + 1) * 16, z * 2 * P:(z + 1) * 2 * P] = v["gla_w_a2"][:, z]
    part("rd")[:, :, 0:8] = v["ret_decay"].reshape(DEPTH, 1, 8)
    part("rd")[:, :, 8:12] = np.repeat(v["ret_decay"].reshape(DEPTH, 4, 2), HD, axis=2).transpose(0, 2, 1)
    part("gnw")[:] = v["gla_norm_w"][:, None]
    part("rnw")[:] = v["ret_norm_w"][:, None]
    part("kc")[:] = v["cache_na_k"][0].reshape(DEPTH, 2, 2, P, HD).transpose(0, 2, 4, 1, 3).reshape(DEPTH, P, 2 * P)
    part("vc")[:] = v["cache_na_v"][0].transpose(0, 2, 1, 3).reshape(DEPTH, P, GW)
    d["par"] = p

    st = np.zeros((DEPTH, 2, 2, P, 2, P), f)
    sc = np.zeros((DEPTH, 2, P, 2, SW), f)
    for h in range(NH):
        fa, a = h // 2, h % 2
        rows, cols = slice(a * HD, (a + 1) * HD), slice(a * HD, (a + 1) * HD)
        st[:, 0, :, rows, fa, cols] = v["state_gla"][0, :, :, h]
        st[:, 1, :, rows, fa, cols] = v["state_ret"][0, :, :, h]
        sc[:, :, rows, fa, a * (HD + 1):a * (HD + 1) + HD] = v["state_mlstm_C"][0, :, :, h]
        sc[:, :, rows, fa, a * (HD + 1) + HD] = v["state_mlstm_n"][0, :, :, h]
    d["st_ad"], d["st_c"] = st, sc
    r = np.zeros((DEPTH, NH, 15, 2 * HD - 1), f)
    r[:, :, :, HD - WIN:HD + WIN - 1] = v["na_rpb"]
    d["rpb"] = np.stack([r[:, :, 1 - row:15 - row, HD - 1 - q:2 * HD - 1 - q].reshape(DEPTH, -1)
                         for row in range(2) for q in range(GRID_W)], 1)
    return d


OUTS = {"y": (P, KT, NTOK), "nak": (DEPTH, P, 2, P), "nav": (DEPTH, P, GW), "gla": (DEPTH, 2, P, 2, P),
        "ret": (DEPTH, 2, P, 2, P), "mc": (DEPTH, 2, P, 2, SW), "mm": (DEPTH, 64, 1)}


def kernel(**inputs):
    import numpy as np
    import concourse.bacc as bacc
    from concourse.bass_utils import run_bass_kernel_spmd

    arrays = lay_out({k: np.asarray(a) for k, a in inputs.items()})
    nc = bacc.Bacc("TRN2", target_bir_lowering=False, num_devices=1)
    I = {k: nc.dram_tensor("in_" + k, a.shape, FP, kind="ExternalInput").ap() for k, a in arrays.items()}
    O = {k: nc.dram_tensor("out_" + k, s, FP, kind="ExternalOutput").ap() for k, s in OUTS.items()}
    build(nc, I, O)
    r = run_bass_kernel_spmd(nc, [{"in_" + k: a for k, a in arrays.items()}], core_ids=[0]).results[0]
    o = {k: np.asarray(r["out_" + k]) for k in OUTS}

    y = o["y"].transpose(2, 1, 0).reshape(NTOK, DM)
    nak = o["nak"].reshape(DEPTH, 2, HD, 2, P).transpose(0, 3, 1, 4, 2).reshape(1, DEPTH, NH, P, HD)
    nav = o["nav"].reshape(DEPTH, P, NH, HD).transpose(0, 2, 1, 3)[None]

    def heads(s, w, lo, hi):
        b = [s[:, :, a * HD:(a + 1) * HD, f, a * w + lo:a * w + hi] for f in range(2) for a in range(2)]
        return np.ascontiguousarray(np.stack(b, 2))[None]

    mm = np.stack([o["mm"][:, 0:NH, 0], o["mm"][:, 32:32 + NH, 0]], 1)[None]
    return (np.ascontiguousarray(y[:SEQ])[None], np.ascontiguousarray(y[SEQ:])[None],
            np.ascontiguousarray(nak), np.ascontiguousarray(nav),
            heads(o["gla"], HD, 0, HD), heads(o["mc"], HD + 1, 0, HD), heads(o["mc"], HD + 1, HD, HD + 1)[..., 0],
            np.ascontiguousarray(mm), heads(o["ret"], HD, 0, HD))
```
